# Optimizing a Trainium2 kernel written in Bass

```python
import math
import jax, jax.numpy as jnp
from jax import lax
import numpy as np

D_MODEL = 1024
BATCH = 1
SEQ = 512
DEPTH = 2

CHUNK = 64
Q_BLOCK = 128
ROPE_THETA = 10000.0
EPS = 1e-6
NEG_INF = -1e30

A_HEADS = 8
A_KV_HEADS = 2
A_HEAD_DIM = 64
A_WINDOW = 128
A_WIN_CHUNKS = A_WINDOW // CHUNK
MLA_HEADS = 8
MLA_Q_RANK = 256
MLA_KV_RANK = 128
MLA_NOPE = 64
MLA_ROPE = 32
MLA_V = 64
FOX_HEADS = 8
FOX_HEAD_DIM = 64
N_BRANCH = 3
BRANCH_WIDTH = 512
P_HEADS = 8
P_NKEYS = 128
P_EXPERTS = P_NKEYS * P_NKEYS
P_DKEY = 128
P_HALF = P_DKEY // 2
P_TOPK = 16
P_TOKEN_BLOCK = 128

IN_SIZES = (A_HEADS * A_HEAD_DIM, A_KV_HEADS * A_HEAD_DIM, A_KV_HEADS * A_HEAD_DIM,
            MLA_Q_RANK, MLA_KV_RANK, MLA_ROPE,
            FOX_HEADS * FOX_HEAD_DIM, FOX_HEADS * FOX_HEAD_DIM, FOX_HEADS * FOX_HEAD_DIM, FOX_HEADS,
            N_BRANCH * D_MODEL)
IN_COLS = sum(IN_SIZES)

kernel_name = "hybrid_chunk_causal_swa_mla_fox_peer"

def rmsnorm(x, g):
    x32 = x.astype(jnp.float32)
    y = x32 * lax.rsqrt(jnp.mean(x32 * x32, axis=-1, keepdims=True) + EPS)
    return (y * g.astype(jnp.float32)).astype(x.dtype)

def rope_tables(pos, dim):
    inv = ROPE_THETA ** (-jnp.arange(0, dim, 2, dtype=jnp.float32) / dim)
    ang = pos[:, None] * inv[None, :]
    return jnp.cos(ang), jnp.sin(ang)

def apply_rope(x, cos, sin):
    half = x.shape[-1] // 2
    x32 = x.astype(jnp.float32)
    x1, x2 = x32[..., :half], x32[..., half:]
    cs, sn = cos[:, None, :], sin[:, None, :]
    return jnp.concatenate([x1 * cs - x2 * sn, x2 * cs + x1 * sn], axis=-1).astype(x.dtype)

def swa_attention(q, k, v, sink):
    bsz, seq = q.shape[0], q.shape[1]
    n_chunks = seq // CHUNK
    group = A_HEADS // A_KV_HEADS
    qc = q.reshape(bsz, n_chunks, CHUNK, A_KV_HEADS, group, A_HEAD_DIM)
    kc = k.reshape(bsz, n_chunks, CHUNK, A_KV_HEADS, A_HEAD_DIM)
    vc = v.reshape(bsz, n_chunks, CHUNK, A_KV_HEADS, A_HEAD_DIM)
    shifts = list(range(A_WIN_CHUNKS - 1, -1, -1))

    def band(t):
        return jnp.concatenate(
            [jnp.pad(t, ((0, 0), (j, 0), (0, 0), (0, 0), (0, 0)))[:, :n_chunks] for j in shifts], axis=2)

    kb, vb = band(kc), band(vc)
    s = jnp.einsum('bnqgrd,bnkgd->bngrqk', qc, kb).astype(jnp.float32) * (A_HEAD_DIM ** -0.5)
    chunk_ids = jnp.arange(n_chunks)
    valid = jnp.concatenate(
        [jnp.broadcast_to((chunk_ids >= j)[:, None], (n_chunks, CHUNK)) for j in shifts], axis=1)
    s = jnp.where(valid[None, :, None, None, None, :], s, NEG_INF)
    sink_logit = jnp.broadcast_to(sink.astype(jnp.float32).reshape(1, 1, A_KV_HEADS, group, 1, 1),
                                  s.shape[:-1] + (1,))
    p = jax.nn.softmax(jnp.concatenate([s, sink_logit], axis=-1), axis=-1)[..., :-1]
    o = jnp.einsum('bngrqk,bnkgd->bnqgrd', p.astype(v.dtype), vb)
    return o.reshape(bsz, seq, A_HEADS * A_HEAD_DIM)

def swept_attention(q, k, v, scale, frame_causal, log_f_cum=None):
    bsz, seq, heads, _ = q.shape
    dv = v.shape[-1]
    n_blocks = seq // Q_BLOCK
    kpos = jnp.arange(seq)
    f_all = None if log_f_cum is None else jnp.transpose(log_f_cum, (0, 2, 1))

    def one_block(i):
        start = i * Q_BLOCK
        qb = lax.dynamic_slice_in_dim(q, start, Q_BLOCK, axis=1)
        s = jnp.einsum('bqhd,bkhd->bhqk', qb, k).astype(jnp.float32) * scale
        qpos = start + jnp.arange(Q_BLOCK)
        if frame_causal:
            allowed = kpos[None, :] <= qpos[:, None]
        else:
            allowed = (kpos[None, :] // CHUNK) <= (qpos[:, None] // CHUNK)
        if f_all is not None:
            fq = lax.dynamic_slice_in_dim(f_all, start, Q_BLOCK, axis=2)
            s = s + fq[..., :, None] - f_all[..., None, :]
        s = jnp.where(allowed[None, None], s, NEG_INF)
        p = jax.nn.softmax(s, axis=-1)
        return jnp.einsum('bhqk,bkhd->bqhd', p.astype(v.dtype), v)

    out = lax.map(one_block, jnp.arange(n_blocks))
    return jnp.transpose(out, (1, 0, 2, 3, 4)).reshape(bsz, seq, heads, dv)

def hybrid_mixer(h, w_in, b_gate, b_forget, swa_sink, swa_qnorm, swa_knorm,
                 mla_q_norm, mla_w_q_up, mla_kv_norm, mla_w_kv_up, mla_qnorm, mla_knorm,
                 fox_qnorm, fox_knorm, w_branch, w_out, cos_a, sin_a, cos_b, sin_b):
    bsz, seq, _ = h.shape
    proj = h @ w_in
    cuts = []
    acc = 0
    for size in IN_SIZES[:-1]:
        acc += size
        cuts.append(acc)
    (a_q, a_k, a_v, m_cq, m_ckv, m_kr, f_q, f_k, f_v, f_f, gate_cols) = jnp.split(proj, cuts, axis=-1)

    qa = a_q.reshape(bsz, seq, A_HEADS, A_HEAD_DIM)
    ka = a_k.reshape(bsz, seq, A_KV_HEADS, A_HEAD_DIM)
    va = a_v.reshape(bsz, seq, A_KV_HEADS, A_HEAD_DIM)
    qa = apply_rope(rmsnorm(qa, swa_qnorm), cos_a, sin_a)
    ka = apply_rope(rmsnorm(ka, swa_knorm), cos_a, sin_a)
    o_a = swa_attention(qa, ka, va, swa_sink)

    cq = rmsnorm(m_cq, mla_q_norm)
    qb = (cq @ mla_w_q_up).reshape(bsz, seq, MLA_HEADS, MLA_NOPE + MLA_ROPE)
    ckv = rmsnorm(m_ckv, mla_kv_norm)
    kv = (ckv @ mla_w_kv_up).reshape(bsz, seq, MLA_HEADS, MLA_NOPE + MLA_V)
    k_nope, vb = kv[..., :MLA_NOPE], kv[..., MLA_NOPE:]
    k_rope = jnp.broadcast_to(m_kr[:, :, None, :], (bsz, seq, MLA_HEADS, MLA_ROPE))
    kb = jnp.concatenate([k_nope, k_rope], axis=-1)
    qb = rmsnorm(qb, mla_qnorm)
    kb = rmsnorm(kb, mla_knorm)
    qb = jnp.concatenate([qb[..., :MLA_NOPE], apply_rope(qb[..., MLA_NOPE:], cos_b, sin_b)], axis=-1)
    kb = jnp.concatenate([kb[..., :MLA_NOPE], apply_rope(kb[..., MLA_NOPE:], cos_b, sin_b)], axis=-1)
    o_b = swept_attention(qb, kb, vb, (MLA_NOPE + MLA_ROPE) ** -0.5, frame_causal=False)
    o_b = o_b.reshape(bsz, seq, MLA_HEADS * MLA_V)

    qf = rmsnorm(f_q.reshape(bsz, seq, FOX_HEADS, FOX_HEAD_DIM), fox_qnorm)
    kf = rmsnorm(f_k.reshape(bsz, seq, FOX_HEADS, FOX_HEAD_DIM), fox_knorm)
    vf = f_v.reshape(bsz, seq, FOX_HEADS, FOX_HEAD_DIM)
    log_f = jax.nn.log_sigmoid(f_f.astype(jnp.float32) + b_forget.astype(jnp.float32))
    log_f_cum = jnp.cumsum(log_f, axis=1)
    o_c = swept_attention(qf, kf, vf, FOX_HEAD_DIM ** -0.5, frame_causal=True, log_f_cum=log_f_cum)
    o_c = o_c.reshape(bsz, seq, FOX_HEADS * FOX_HEAD_DIM)

    gates = jax.nn.sigmoid(gate_cols + b_gate).reshape(bsz, seq, N_BRANCH, D_MODEL)
    branches = (o_a, o_b, o_c)
    y = gates[:, :, 0] * (branches[0] @ w_branch[0])
    for i in range(1, N_BRANCH):
        y = y + gates[:, :, i] * (branches[i] @ w_branch[i])
    return y @ w_out

def peer_ffn(h, w_q, sub_keys, u_tab, v_tab):
    bsz, seq, d = h.shape
    tokens = h.reshape(-1, P_TOKEN_BLOCK, d)

    def one_block(xb):
        q = (xb @ w_q).reshape(P_TOKEN_BLOCK, P_HEADS, 2, P_HALF)
        s = jnp.einsum('thcd,ckd->thck', q, sub_keys).astype(jnp.float32)
        sv, si = lax.top_k(s, P_TOPK)
        cand = (sv[:, :, 0, :, None] + sv[:, :, 1, None, :]).reshape(P_TOKEN_BLOCK, P_HEADS, P_TOPK * P_TOPK)
        cidx = (si[:, :, 0, :, None] * P_NKEYS + si[:, :, 1, None, :]).reshape(P_TOKEN_BLOCK, P_HEADS, P_TOPK * P_TOPK)
        top_s, top_pos = lax.top_k(cand, P_TOPK)
        experts = jnp.take_along_axis(cidx, top_pos, axis=-1).reshape(P_TOKEN_BLOCK, P_HEADS * P_TOPK)
        g = jax.nn.softmax(top_s, axis=-1).reshape(P_TOKEN_BLOCK, P_HEADS * P_TOPK)
        u = u_tab[experts]
        vv = v_tab[experts]
        a = jax.nn.gelu(jnp.einsum('td,ted->te', xb, u).astype(jnp.float32), approximate=False) * g
        return jnp.einsum('te,ted->td', a.astype(vv.dtype), vv)

    return lax.map(one_block, tokens).reshape(bsz, seq, d)

def setup_inputs(seed: int = 0) -> dict:
    key = jax.random.key(seed)
    ks = jax.random.split(key, 32)
    f32 = jnp.float32

    def nrm(k, shape, scale):
        return jax.random.normal(k, shape, f32) * scale

    def gain(k, shape):
        return 1.0 + 0.02 * jax.random.normal(k, shape, f32)

    L, D = DEPTH, D_MODEL
    return {
        "x": nrm(ks[0], (BATCH, SEQ, D), 1.0),
        "c": nrm(ks[1], (BATCH, D), 1.0),
        "w_ada": nrm(ks[2], (L, D, 6 * D), D ** -0.5),
        "b_ada": nrm(ks[3], (L, 6 * D), 0.02),
        "norm1_g": gain(ks[4], (L, D)),
        "norm2_g": gain(ks[5], (L, D)),
        "w_in": nrm(ks[6], (L, D, IN_COLS), D ** -0.5),
        "b_gate": nrm(ks[7], (L, N_BRANCH * D), 0.02),
        "b_forget": 3.0 + 0.5 * jax.random.normal(ks[8], (L, FOX_HEADS), f32),
        "swa_sink": nrm(ks[9], (L, A_HEADS), 1.0),
        "swa_qnorm": gain(ks[10], (L, A_HEAD_DIM)),
        "swa_knorm": gain(ks[11], (L, A_HEAD_DIM)),
        "mla_q_norm": gain(ks[12], (L, MLA_Q_RANK)),
        "mla_w_q_up": nrm(ks[13], (L, MLA_Q_RANK, MLA_HEADS * (MLA_NOPE + MLA_ROPE)), MLA_Q_RANK ** -0.5),
        "mla_kv_norm": gain(ks[14], (L, MLA_KV_RANK)),
        "mla_w_kv_up": nrm(ks[15], (L, MLA_KV_RANK, MLA_HEADS * (MLA_NOPE + MLA_V)), MLA_KV_RANK ** -0.5),
        "mla_qnorm": gain(ks[16], (L, MLA_NOPE + MLA_ROPE)),
        "mla_knorm": gain(ks[17], (L, MLA_NOPE + MLA_ROPE)),
        "fox_qnorm": gain(ks[18], (L, FOX_HEAD_DIM)),
        "fox_knorm": gain(ks[19], (L, FOX_HEAD_DIM)),
        "w_branch": nrm(ks[20], (L, N_BRANCH, BRANCH_WIDTH, D), BRANCH_WIDTH ** -0.5),
        "w_out": nrm(ks[21], (L, D, D), D ** -0.5),
        "peer_w_q": nrm(ks[22], (L, D, P_HEADS * P_DKEY), D ** -0.5),
        "peer_sub_keys": nrm(ks[23], (L, 2, P_NKEYS, P_HALF), P_HALF ** -0.5),
        "peer_u": nrm(ks[24], (L, P_EXPERTS, D), D ** -0.5),
        "peer_v": nrm(ks[25], (L, P_EXPERTS, D), P_HEADS ** -0.5),
    }

def reference(x, c, w_ada, b_ada, norm1_g, norm2_g, w_in, b_gate, b_forget,
              swa_sink, swa_qnorm, swa_knorm, mla_q_norm, mla_w_q_up, mla_kv_norm, mla_w_kv_up,
              mla_qnorm, mla_knorm, fox_qnorm, fox_knorm, w_branch, w_out,
              peer_w_q, peer_sub_keys, peer_u, peer_v):
    seq = x.shape[1]
    pos = jnp.arange(seq, dtype=jnp.float32)
    cos_a, sin_a = rope_tables(pos, A_HEAD_DIM)
    cos_b, sin_b = rope_tables(pos, MLA_ROPE)
    cond = jax.nn.silu(c)
    for l in range(DEPTH):
        mod = (cond @ w_ada[l] + b_ada[l])[:, None, :]
        sh1, sc1, g1, sh2, sc2, g2 = jnp.split(mod, 6, axis=-1)
        h = rmsnorm(x, norm1_g[l]) * (1.0 + sc1) + sh1
        mix = hybrid_mixer(h, w_in[l], b_gate[l], b_forget[l], swa_sink[l], swa_qnorm[l], swa_knorm[l],
                           mla_q_norm[l], mla_w_q_up[l], mla_kv_norm[l], mla_w_kv_up[l],
                           mla_qnorm[l], mla_knorm[l], fox_qnorm[l], fox_knorm[l],
                           w_branch[l], w_out[l], cos_a, sin_a, cos_b, sin_b)
        x = x + g1 * mix
        h = rmsnorm(x, norm2_g[l]) * (1.0 + sc2) + sh2
        x = x + g2 * peer_ffn(h, peer_w_q[l], peer_sub_keys[l], peer_u[l], peer_v[l])
    return x


_drawn_inputs = setup_inputs


def setup_inputs(seed=0):
    import zlib

    import numpy as np

    out = dict(_drawn_inputs(seed))
    spreads = {}
    factors = {'norm1_g': 3.176,
     'b_gate': 5.005,
     'swa_sink': 4.241,
     'swa_qnorm': 6.633,
     'swa_knorm': 7.31,
     'mla_q_norm': 8.0,
     'mla_kv_norm': 4.051,
     'mla_qnorm': 8.0,
     'mla_knorm': 8.0,
     'fox_qnorm': 5.698,
     'fox_knorm': 5.607}
    for name, (base, spread) in spreads.items():
        noise = np.random.default_rng([zlib.crc32(name.encode()), seed]).standard_normal(out[name].shape)
        drawn = base * np.exp(spread * noise) if base else spread * noise
        out[name] = __import__('jax').numpy.asarray(drawn.astype(out[name].dtype))
    for name, factor in factors.items():
        out[name] = (out[name] * factor).astype(out[name].dtype)
    return out
```

```python
from contextlib import ExitStack

import numpy as np

import concourse.bass as bass
from concourse import mybir

F32 = mybir.dt.float32
BF16 = mybir.dt.bfloat16
U32 = mybir.dt.uint32
ALU = mybir.AluOpType
ACT = mybir.ActivationFunctionType
AX = mybir.AxisListType
ds = bass.ds

LAYERS = 2
D = 1024
T = 512
KT = D // 128
TT = T // 128
HEADS = 8
PAIRS = HEADS // 2
EPS = 1e-6
NEG = -1e30
LOWEST = -3.0e38
PICKS = 16
KEYS = 128
GROUP = 4
TOKENS = 32

TILES = {
    "ada": (6, [0, 1, 2, 3, 4, 5, 6, 7]),
    "swa_kv": (1, [8, 9]),
    "swa": (PAIRS, [0]),
    "mla_c": (1, [1, 2, 3, 4]),
    "mla": (PAIRS, [5]),
    "fox": (PAIRS, [6, 7, 8]),
    "gates": (4, [9, 0, 1, 2, 3, 4, 5, 6, 7]),
    "w_out": (2, [8, 0, 1, 2]),
    "query": (4, [3, 4]),
    "dense": (KEYS // GROUP, [5, 6, 7, 8, 9, 0, 1, 2]),
}
SLOTS = 10
STAGES = ["ada", "norm1", "swa_kv", "swa", "mla_c", "mla", "fox", "gates", "w_out",
          "norm2", "query", "select", "route", "dense", "final"]
STEPS = {"ada": 6, "norm1": 1, "swa_kv": 1, "swa": PAIRS, "mla_c": 1, "mla": PAIRS, "fox": PAIRS,
         "gates": 4, "w_out": 2, "norm2": 1, "query": 4, "select": TT, "route": T // (2 * TOKENS),
         "dense": KEYS // GROUP, "final": 1}
STREAM_TILES = sum(s * len(k) for n, (s, k) in TILES.items() if n != "dense")

CONST = {}
_n = 0
for _name, _w in (("ident", 128), ("block64", 128), ("ones", 128), ("rot_a", 128), ("rot_b", 128),
                  ("cos_a", T), ("sin_a", T), ("cos_b", T), ("sin_b", T),
                  ("mask_own_chunks", 128), ("mask_window", 256), ("mask_frames", 128),
                  ("iota", 128), ("head_pick", 8), ("eps", 1), ("one", 1), ("zero", 1), ("fq", T), ("fk", T)):
    CONST[_name] = (_n, _w)
    _n += _w
CONST_COLS = _n
VEC = {}
_n = 0
for _name, _w in (("b_ada", 48), ("norm1", 8), ("norm2", 8), ("b_gate", 24), ("sink", 8), ("swa_q", 1), ("swa_k", 1),
                  ("cq", 2), ("ckv", 1), ("mla_q", 1), ("mla_k", 1), ("fox_q", 1), ("fox_k", 1),
                  ("b_forget", 1), ("c", 8), ("keys", 128)):
    VEC[_name] = (_n, _w)
    _n += _w
VEC_COLS = _n


class Signal:

    def __init__(self, sem, per_step, credit=1):
        self.sem = sem
        self.per_step = per_step
        self.credit = credit
        self.base, n = {}, credit
        for stage in STAGES:
            self.base[stage] = n
            n += STEPS[stage] * per_step.get(stage, 0)
        self.per_layer = n - credit

    def at(self, stage, layer, step, n):
        return layer * self.per_layer + step * self.per_step.get(stage, 0) + (self.base[stage] + n)


class Chain:

    def __init__(self, eng, own):
        self.eng, self.own = eng, own

    def begin(self, stage, layer, step):
        self.where, self.n = (stage, layer, step), 0

    def mark(self, ins):
        ins.then_inc(self.own.sem, 1)
        self.n += 1

    def settle(self):
        self.eng.wait_ge(self.own.sem, self.own.at(*self.where, self.n))

    def link(self, ins):
        self.mark(ins)
        self.settle()

    def settle_for_search(self):
        self.settle()
        self.eng.sem_inc(self.held, 1)

    def end(self):
        want = self.own.per_step.get(self.where[0], 0)
        if want != self.n:
            MISCOUNTED.append((self.own.sem.name, self.where[0], want, self.n))


MISCOUNTED = []

VECTOR_LINKS = {"norm1": 1, "swa_kv": 4, "swa": 26, "mla_c": 6, "mla": 12, "fox": 8, "gates": 4, "norm2": 1,
                "query": 82, "select": 51}
SCALAR_LINKS = {"norm1": 1, "swa_kv": 1, "swa": 1, "mla_c": 4, "mla": 4, "fox": 2, "norm2": 1}


def build_trunk(nc, x_t, stream, vecs, consts, tab_u, tab_v, out_t, route_dram, stages=None, layers=LAYERS):
    stages = stages or STAGES
    ctx = ExitStack()
    with ctx:
        def sb(name, shape, dt=F32):
            return ctx.enter_context(nc.sbuf_tensor(name, shape, dt))

        def sem(name):
            return ctx.enter_context(nc.semaphore(name))

        signals = []

        def signal(name, per_step, credit=1):
            signals.append(Signal(sem(name), per_step, credit))
            return signals[-1]

        C = sb("C", [128, CONST_COLS])
        V = sb("V", [128, VEC_COLS])
        ident16 = sb("ident16", [128, 128], BF16)
        masks16 = sb("masks16", [128, 512], BF16)
        xT = sb("xT", [128, KT, T])
        hT = sb("hT", [128, KT, T])
        mixT = sb("mixT", [128, KT, T])
        W = sb("W", [128, SLOTS, 1024])
        cond = sb("cond", [128, 2, KT])
        row = sb("row", [1, 1024])
        modT = sb("modT", [128, 6 * KT])
        gain = sb("gain", [128, 2 * KT])
        gq = sb("gq", [128, 3])

        arena = sb("arena", [128, 22 * 1024])
        at = [0]

        def carve(cols, shape, dt=F32):
            a = arena[:, at[0]:at[0] + cols]
            at[0] += cols
            if dt != F32:
                a = a.bitcast(dt)
            if len(shape) == 1:
                return a
            names = "abcdef"[:len(shape)]
            return a.rearrange(f"p ({' '.join(names)}) -> p {' '.join(names)}",
                               **{k: v for k, v in zip(names[1:], shape[1:])})

        oT = [carve(4 * T, [4, T]) for _ in range(3)]
        sq = carve(2 * T, [2, T])
        rstd = carve(2 * T, [2, T])
        lnv = carve(T, [T])
        qn = carve(2 * T, [2, T])
        rope = carve(2 * T, [2, T])
        q_cur = carve(2 * T, [2, T])
        k_cur = carve(2 * T, [2, T])
        v_cur = carve(T, [TT, 128])
        c_lat = carve(3 * T, [3, T])
        k_rot = carve(T, [T])
        probs = carve(2 * T, [2, T])
        pnorm = carve(2 * T, [2, T])
        probsT = carve(2 * T, [2, T])
        stat = carve(64, [64])
        fgt = carve(4 * T, [4, T])
        fq_head = carve(2 * T, [2, T])
        sig, gated = probs, pnorm
        gate_b = carve(8, [8])
        sinks = carve(2, [2])
        assert at[0] <= 22 * 1024, at[0]

        at[0] = 0
        q_peer = carve(2 * T, [2, T])
        sval_cur = carve(2 * TT * 2 * 16, [2, TT, 2, 16])
        sidx_cur = carve(2 * TT * 2 * 16, [2, TT, 2, 16], U32)
        rest = carve(8 * 128, [8, 128])
        sval = carve(TT * HEADS * 32, [TT, HEADS, 2, 16])
        sidx = carve(TT * HEADS * 32, [TT, HEADS, 2, 16])
        cand = carve(HEADS * 256, [HEADS, 256])
        onehot16 = carve(HEADS * 256, [HEADS * 16, 16])
        top = carve(128, [HEADS, 16])
        pos = carve(128, [HEADS, 16], U32)
        pos_part = carve(2 * 128, [2, 128], U32)
        pos_f = carve(2 * 128, [2, 128])
        pick = carve(3 * 128, [3, 128])
        esum = carve(16, [2, 8])
        pickT = carve(3 * T, [3, T])
        keep = at[0]
        route = [carve(128 * TOKENS, [128, TOKENS]) for _ in range(2)]
        oh_i = carve(2 * 4 * 128, [2, 4, 128])
        oh_j = carve(2 * 4 * 128, [2, 4, 128])
        at[0] = keep
        g_cur = carve(GROUP * T, [T // TOKENS, GROUP * TOKENS])
        a_cur = carve(GROUP * T, [GROUP, T])
        assert at[0] <= 22 * 1024

        PS = [ctx.enter_context(nc.psum_tensor(f"bank{i}", [128, 512], F32)) for i in range(8)]
        P0, S0, T0, O0, NS = PS[0:2], PS[2:4], PS[4:6], PS[6], PS[7]

        def cst(name):
            a, w = CONST[name]
            return C[:, a:a + w]

        def vec(name):
            a, w = VEC[name]
            return V[:, a:a + w]

        consts_loaded = sem("consts_loaded")
        x_loaded = sem("x_loaded")
        out_stored = sem("out_stored")
        setup_done = sem("setup_done")
        vecs_loaded = sem("vecs_loaded")
        cond_sigmoid = sem("cond_sigmoid")
        cond_ready = sem("cond_ready")
        sum_cleared = sem("sum_cleared")
        tile_loaded = [signal(f"tile_loaded{s}", {n: 16 for n, (_, k) in TILES.items() if s in k})
                       for s in range(SLOTS)]
        tile_used = signal("tile_used", {n: len(k) for n, (_, k) in TILES.items()}, credit=8)
        boundary = sem("boundary")
        held = sem("held")
        row_copied = signal("row_copied", {"ada": 2})
        mod_columns = signal("mod_columns", {"ada": 1})
        mod_drained = signal("mod_drained", {"ada": 1})
        squares = signal("squares", {"norm1": KT, "norm2": KT})
        square_sums = signal("square_sums", {"norm1": KT, "norm2": KT})
        stream_rstd = signal("stream_rstd", {"norm1": 1, "norm2": 1})
        stream_scaled = signal("stream_scaled", {"norm1": KT, "norm2": KT})
        tiles_n = {"swa_kv": 2, "swa": 1, "mla_c": 5, "mla": 5, "fox": 3}
        norms_n = {"swa_kv": 1, "swa": 1, "mla_c": 2, "mla": 4, "fox": 2}
        proj_ready = signal("proj_ready", {"mla_c": 1, "mla": 4})
        proj_squared = signal("proj_squared", {"swa_kv": 1, "swa": 1, "mla_c": 3, "mla": 4, "fox": 2})
        proj_sums = signal("proj_sums", norms_n)
        proj_rstd = signal("proj_rstd", norms_n)
        proj_drained = signal("proj_drained", tiles_n)
        rotated = signal("rotated", {"swa_kv": 1, "swa": 1, "mla": 4})
        rotation_read = signal("rotation_read", {"swa_kv": 1, "swa": 1, "mla": 4})
        qk_ready = signal("qk_ready", {"swa": 1, "mla": 4, "swa_kv": 1})
        forget_bias = signal("forget_bias", {"fox": 2})
        U8 = {"swa": 8, "mla": 8, "fox": 8}
        scores_ready = signal("scores_ready", U8)
        max_ready = signal("max_ready", U8)
        probs_ready = signal("probs_ready", U8)
        probs_scaled = signal("probs_scaled", U8)
        probs_turned = signal("probs_turned", U8)
        turned_copied = signal("turned_copied", U8)
        unit_out = signal("unit_out", U8)
        pair_stored = signal("pair_stored", {"swa": 1, "mla": 1, "fox": 1})
        branch_ready = signal("branch_ready", {"gates": 3})
        bias_copied = signal("bias_copied", {"gates": 1})
        gate_open = signal("gate_open", {"gates": 6})
        branch_gated = signal("branch_gated", {"gates": 6})
        mixed = signal("mixed", {"w_out": 4})
        query_copied = signal("query_copied", {"query": 2})
        key_scores = signal("key_scores", {"query": 2})
        key_scores_read = signal("key_scores_read", {"query": 2})
        pick_shifted = signal("pick_shifted", {"select": 1})
        pick_exp = signal("pick_exp", {"select": 1})
        picks_ready = signal("picks_ready", {"select": 3})
        picks_turned = signal("picks_turned", {"select": 1})
        picks_copied = signal("picks_copied", {"select": 1})
        Q = 2 * TOKENS // 4
        onehots = signal("onehots", {"route": Q})
        route_product = signal("route_product", {"route": Q})
        route_copied = signal("route_copied", {"route": Q})
        route_stored = [signal(f"route_stored{b}", {"route": 16}, credit=0) for b in range(2)]
        route_free = [signal(f"route_free{b}", {"route": 1}) for b in range(2)]
        route_loaded = signal("route_loaded", {"dense": 16}, credit=0)
        gelu_done = signal("gelu_done", {"dense": GROUP})
        weighted = signal("weighted", {"dense": GROUP})
        y_ready = signal("y_ready", {"dense": KT - 1})
        y_added = signal("y_added", {"dense": KT})
        vector_chain = signal("vector_chain", VECTOR_LINKS)
        scalar_chain = signal("scalar_chain", SCALAR_LINKS)

        def used(stages_):
            return [s for s in STAGES if s in stages_]

        nstage = len(stages)

        def enter(eng, stage, layer):
            eng.wait_ge(boundary, (layer * nstage + stages.index(stage)) * 4 + 1)
            eng.sem_inc(held, 1)

        def leave(eng):
            eng.drain().then_inc(boundary, 1)

        def tile(stage, layer, step, n):
            slot = TILES[stage][1][n]
            return W[:, slot, :], tile_loaded[slot], slot

        def earlier(signal, stage, layer, step, n, depth):
            return signal.at(stage, layer, step, max(n - depth + 1, 0))

        def proj_wait(eng, stage, layer, step, n):
            if stage == "mla" and n < 4:
                eng.wait_ge(proj_ready.sem, proj_ready.at(stage, layer, step, n + 1))
            elif stage == "mla_c" and n == 3:
                eng.wait_ge(proj_ready.sem, proj_ready.at(stage, layer, step, 1))
            else:
                t = {"mla": 0, "mla_c": min(n, 3)}.get(stage, n)
                eng.wait_ge(tile_used.sem, tile_used.at(stage, layer, step, t + 1))

        def norms(stage):
            if stage == "swa_kv":
                return [([0], 128, 64, [vec("swa_k")], [k_cur[:, 0, :]], cst("block64"), "a")]
            if stage == "swa":
                return [([0], 128, 64, [gq[:, 0:1]], [q_cur[:, 0, :]], cst("block64"), "a")]
            if stage == "mla_c":
                return [([0, 1], 128, 256, [vec("cq")[:, 0:1], vec("cq")[:, 1:2]],
                         [c_lat[:, 0, :], c_lat[:, 1, :]], cst("ones"), None),
                        ([2], 128, 128, [vec("ckv")], [c_lat[:, 2, :]], cst("ones"), None)]
            if stage == "mla":
                return [([2 * e + k], 96, 96, [(gq[:, 1:2], vec("mla_k"))[k]],
                         [(q_cur, k_cur)[k][:, e, :]], cst("ones"), "b")
                        for e in range(2) for k in range(2)]
            return [([k], 128, 64, [(gq[:, 2:3], vec("fox_k"))[k]], [(q_cur, k_cur)[k][:, 0, :]],
                     cst("block64"), None) for k in range(2)]

        def head(stage, e):
            if stage == "mla":
                return slice(0, 96), q_cur[:, e, :], k_cur[:, e, :]
            return slice(64 * e, 64 * e + 64), q_cur[:, 0, :], k_cur[:, 0, :]

        def key_tiles(stage, i):
            return range(max(i - 1, 0), i + 1) if stage == "swa" else range(i + 1)

        block = ctx.enter_context(nc.Block())

        @block.sync
        def _(sp):
            sp.dma_start(C[:], consts).then_inc(consts_loaded, 16)
            sp.dma_start(xT[:], x_t).then_inc(x_loaded, 16)
            with sp.Fori(0, layers) as layer:
                sp.dma_start(V[:], vecs[layer]).then_inc(vecs_loaded, 16)
                tenant = {}
                count = 0
                for stage in [s for s in stages if s in TILES]:
                    steps, slots = TILES[stage]
                    before = [tenant[s] for s in slots if s in tenant]
                    if before:
                        sp.wait_ge(tile_used.sem, layer * tile_used.per_layer + (max(before) + 1))
                        sp.sem_inc(held, 1)
                    with sp.Fori(0, steps) as step:
                        for n, slot in enumerate(slots):
                            if steps > 1:
                                sp.wait_ge(tile_used.sem, tile_used.at(stage, layer, step, n + 1 - len(slots)))
                            if stage == "dense":
                                tab = tab_u if n < GROUP else tab_v
                                src = tab[layer * KEYS + step * GROUP + n % GROUP]
                            else:
                                src = stream[layer * STREAM_TILES + step * len(slots) + (count + n)]
                            sp.dma_start(W[:, slot, :], src).then_inc(tile_loaded[slot].sem, 16)
                            tenant[slot] = tile_used.base[stage] + (steps - 1) * len(slots) + n
                    count += steps * len(slots)
                sp.wait_ge(boundary, (layer + 1) * (nstage * 4) + 1)
                sp.sem_inc(held, 1)
            sp.dma_start(out_t, xT[:]).then_inc(out_stored, 16)
            sp.wait_ge(out_stored, 16)

        @block.tensor
        def _(pe):
            mm = nc.tensor.matmul

            def load_wait(stage, layer, step, n):
                w, loaded, _ = tile(stage, layer, step, n)
                pe.wait_ge(loaded.sem, loaded.at(stage, layer, step, 16))
                return w

            def project(out, w, act, width=128, off=0, pitch=128, kts=KT):
                for k in range(kts):
                    last = mm(out, w[:, k * pitch + off:k * pitch + off + width], act[:, k, :],
                              start=(k == 0), stop=(k == kts - 1))
                return last

            def stream_norm(stage, layer):
                enter(pe, stage, layer)
                for k in range(KT):
                    pe.wait_ge(squares.sem, squares.at(stage, layer, 0, k + 1))
                    mm(NS[:], cst("ones"), sq[:, k % 2, :], start=(k == 0), stop=(k == KT - 1)
                       ).then_inc(square_sums.sem, 1)
                leave(pe)

            def proj_bank(stage, layer, step, n):
                pe.wait_ge(proj_drained.sem, earlier(proj_drained, stage, layer, step, n, 2))
                return P0[n % 2]

            def norm_sums(stage, layer, step, u):
                tiles_, parts, _, _, _, ones, rot = norms(stage)[u]
                first = sum(len(x[0]) for x in norms(stage)[:u])
                for i, n in enumerate(tiles_):
                    pe.wait_ge(proj_squared.sem, proj_squared.at(stage, layer, step, first + i + 1))
                    if i == 0 and rot:
                        pe.wait_ge(rotation_read.sem, rotation_read.at(stage, layer, step, u))
                    elif i == 0:
                        pe.wait_ge(proj_rstd.sem, proj_rstd.at(stage, layer, step, u))
                    last = mm(NS[0:parts, :], ones[0:parts, 0:parts], sq[0:parts, (first + i) % 2, :],
                              start=(i == 0), stop=(i == len(tiles_) - 1))
                last.then_inc(proj_sums.sem, 1)

            def norm_rotate(stage, layer, step, u):
                tiles_, parts, _, _, _, _, rot = norms(stage)[u]
                pe.wait_ge(proj_drained.sem, proj_drained.at(stage, layer, step, tiles_[0] + 1))
                mm(NS[0:parts, :], cst("rot_" + rot)[0:parts, 0:parts], qn[0:parts, u % 2, :],
                   start=True, stop=True).then_inc(rotated.sem, 1)

            def values(stage, layer, step, n, w, act, off, pitch, kts, src=0):
                bank = proj_bank(stage, layer, step, n)
                for t in range(TT):
                    for k in range(kts):
                        last = mm(bank[:, t * 128:(t + 1) * 128], act[:, src + k, t * 128:(t + 1) * 128],
                                  w[:, k * pitch + off:k * pitch + off + 128], start=(k == 0), stop=(k == kts - 1))
                last.then_inc(tile_used.sem, 1)

            def attention(stage, layer, step):
                units = [(e, i) for e in range(2) for i in range(TT)]
                mask = {"swa": "mask_window", "mla": "mask_own_chunks", "fox": "mask_frames"}[stage]
                m0 = {"mask_own_chunks": 0, "mask_window": 128, "mask_frames": 384}[mask]

                def scores(u):
                    e, i = units[u]
                    rows, q, k = head(stage, e)
                    tiles_ = key_tiles(stage, i)
                    width = len(tiles_) * 128
                    pe.wait_ge(probs_ready.sem, earlier(probs_ready, stage, layer, step, u, 2))
                    if stage == "fox" and i == 0:
                        pe.wait_ge(forget_bias.sem, forget_bias.at(stage, layer, step, e + 1))
                    masked = width if stage == "swa" else 128
                    for lo, hi in ((0, width - masked), (width - masked, width)):
                        if lo == hi:
                            continue
                        out = S0[u % 2][:, lo:hi]
                        plain = hi < width
                        last = mm(out, q[rows, i * 128:(i + 1) * 128],
                                  k[rows, tiles_[0] * 128 + lo:tiles_[0] * 128 + hi],
                                  start=True, stop=plain and stage != "fox")
                        if stage == "fox":
                            bias_rows = slice(64 * e, 64 * e + 40)
                            last = mm(out, fq_head[bias_rows, e, i * 128:(i + 1) * 128], cst("fk")[bias_rows, lo:hi],
                                      start=False, stop=plain)
                    mlo = m0 + (256 - width if stage == "swa" else 0)
                    mm(out, ident16[:], masks16[:, mlo:mlo + masked], start=False, stop=True
                       ).then_inc(scores_ready.sem, 1)

                def turn(u):
                    e, i = units[u]
                    n = len(key_tiles(stage, i))
                    pe.wait_ge(probs_scaled.sem, probs_scaled.at(stage, layer, step, u + 1))
                    pe.wait_ge(turned_copied.sem, earlier(turned_copied, stage, layer, step, u, 2))
                    for b in range(n):
                        last = nc.tensor.transpose(T0[u % 2][:, b * 128:(b + 1) * 128],
                                                   pnorm[:, u % 2, b * 128:(b + 1) * 128], cst("ident"))
                    last.then_inc(probs_turned.sem, 1)

                def output(u):
                    e, i = units[u]
                    pe.wait_ge(turned_copied.sem, turned_copied.at(stage, layer, step, u + 1))
                    if u == 0:
                        pe.wait_ge(pair_stored.sem, pair_stored.at(stage, layer, step, 0))
                    tiles_ = list(key_tiles(stage, i))
                    for b, kt in enumerate(tiles_):
                        last = mm(O0[64 * e:64 * e + 64, i * 128:(i + 1) * 128], v_cur[:, kt, 64 * e:64 * e + 64],
                                  probsT[:, u % 2, b * 128:(b + 1) * 128], start=(b == 0), stop=(b == len(tiles_) - 1))
                    last.then_inc(unit_out.sem, 1)

                for u in range(len(units) + 2):
                    if u < len(units):
                        scores(u)
                    if 1 <= u <= len(units):
                        turn(u - 1)
                    if u >= 2:
                        output(u - 2)

            pe.wait_ge(consts_loaded, 16)
            pe.wait_ge(setup_done, 2)
            with pe.Fori(0, layers) as layer:
                if "ada" in stages:
                    enter(pe, "ada", layer)
                    pe.wait_ge(cond_ready, layer + 1)
                    pe.sem_inc(held, 1)
                    with pe.Fori(0, STEPS["ada"]) as step:
                        for k in range(KT):
                            w = load_wait("ada", layer, step, k)
                            if k == 0:
                                pe.wait_ge(row_copied.sem, row_copied.at("ada", layer, step, 0))
                            for h in range(2):
                                last = mm(PS[h][0:1, :], cond[:, 1, k:k + 1], w[:, h * 512:(h + 1) * 512],
                                          start=(k == 0), stop=(k == KT - 1))
                            last.then_inc(tile_used.sem, 1)
                        pe.wait_ge(row_copied.sem, row_copied.at("ada", layer, step, 2))
                        pe.wait_ge(mod_drained.sem, mod_drained.at("ada", layer, step, 0))
                        for k in range(KT):
                            last = mm(PS[2][:, k:k + 1], row[0:1, k * 128:(k + 1) * 128], cst("one")[0:1, :],
                                      start=True, stop=True)
                        last.then_inc(mod_columns.sem, 1)
                    leave(pe)
                if "norm1" in stages:
                    stream_norm("norm1", layer)
                if "swa_kv" in stages:
                    enter(pe, "swa_kv", layer)
                    w = load_wait("swa_kv", layer, 0, 0)
                    project(proj_bank("swa_kv", layer, 0, 0)[:], w, hT).then_inc(tile_used.sem, 1)
                    w = load_wait("swa_kv", layer, 0, 1)
                    values("swa_kv", layer, 0, 1, w, hT, 0, 128, KT)
                    norm_sums("swa_kv", layer, 0, 0)
                    norm_rotate("swa_kv", layer, 0, 0)
                    leave(pe)
                if "swa" in stages:
                    enter(pe, "swa", layer)
                    with pe.Fori(0, PAIRS) as step:
                        w = load_wait("swa", layer, step, 0)
                        project(proj_bank("swa", layer, step, 0)[:], w, hT).then_inc(tile_used.sem, 1)
                        norm_sums("swa", layer, step, 0)
                        norm_rotate("swa", layer, step, 0)
                        pe.wait_ge(qk_ready.sem, qk_ready.at("swa", layer, step, 1))
                        attention("swa", layer, step)
                    leave(pe)
                if "mla_c" in stages:
                    enter(pe, "mla_c", layer)
                    for n in range(3):
                        w = load_wait("mla_c", layer, 0, n)
                        if n == 2:
                            norm_sums("mla_c", layer, 0, 0)
                        project(proj_bank("mla_c", layer, 0, n)[:], w, hT).then_inc(tile_used.sem, 1)
                    w = load_wait("mla_c", layer, 0, 3)
                    project(proj_bank("mla_c", layer, 0, 3)[64:96, :], w, hT, width=32, pitch=40).then_inc(proj_ready.sem, 1)
                    project(T0[0][0:8, :], w, hT, width=8, off=32, pitch=40).then_inc(tile_used.sem, 1)
                    norm_sums("mla_c", layer, 0, 1)
                    leave(pe)
                if "mla" in stages:
                    enter(pe, "mla", layer)
                    with pe.Fori(0, PAIRS) as step:
                        w = load_wait("mla", layer, step, 0)

                        def up(n):
                            e, k = n // 2, n % 2
                            bank = proj_bank("mla", layer, step, n)
                            if k == 0:
                                project(bank[0:96, :], w, c_lat, width=96, off=96 * e, pitch=192, kts=2
                                        ).then_inc(proj_ready.sem, 1)
                            else:
                                mm(bank[0:64, :], w[:, 384 + 64 * e:448 + 64 * e], c_lat[:, 2, :], start=True, stop=True)
                                mm(bank[64:96, :], cst("ident")[64:96, 64:96], k_rot[64:96, :],
                                   start=True, stop=True, skip_group_check=True).then_inc(proj_ready.sem, 1)

                        up(0)
                        up(1)
                        for u in range(4):
                            norm_sums("mla", layer, step, u)
                            norm_rotate("mla", layer, step, u)
                            if u + 2 < 4:
                                up(u + 2)
                            elif u == 2:
                                values("mla", layer, step, 4, w, c_lat, 512, 0, 1, src=2)
                        pe.wait_ge(qk_ready.sem, qk_ready.at("mla", layer, step, 4))
                        pe.wait_ge(proj_drained.sem, proj_drained.at("mla", layer, step, 5))
                        attention("mla", layer, step)
                    leave(pe)
                if "fox" in stages:
                    enter(pe, "fox", layer)
                    with pe.Fori(0, PAIRS) as step:
                        for n in range(2):
                            w = load_wait("fox", layer, step, n)
                            project(proj_bank("fox", layer, step, n)[:], w, hT).then_inc(tile_used.sem, 1)
                        norm_sums("fox", layer, step, 0)
                        norm_sums("fox", layer, step, 1)
                        w = load_wait("fox", layer, step, 2)
                        values("fox", layer, step, 2, w, hT, 0, 128, KT)
                        pe.wait_ge(proj_drained.sem, proj_drained.at("fox", layer, step, 3))
                        attention("fox", layer, step)
                    leave(pe)
                if "gates" in stages:
                    enter(pe, "gates", layer)
                    with pe.Fori(0, 4) as step:
                        tile_of = [0, 1, 3, 4, 6, 7]
                        wb = {}
                        for g in range(6):
                            i = g % 3
                            w = load_wait("gates", layer, step, tile_of[g])
                            pe.wait_ge(branch_gated.sem, earlier(branch_gated, "gates", layer, step, g, 2))
                            project(PS[g % 2][:], w, hT).then_inc(tile_used.sem, 1)
                            if g % 2 == 0:
                                wb[g // 2] = load_wait("gates", layer, step, 3 * (g // 2) + 2)
                            last = project(PS[2 + g % 2][:], wb[g // 2][:, (g % 2) * 512:(g % 2) * 512 + 512], oT[i], kts=4)
                            last.then_inc((branch_ready if g % 2 == 0 else tile_used).sem, 1)
                    leave(pe)
                if "w_out" in stages:
                    enter(pe, "w_out", layer)
                    with pe.Fori(0, 2) as step:
                        for n in range(4):
                            w = load_wait("w_out", layer, step, n)
                            pe.wait_ge(mixed.sem, earlier(mixed, "w_out", layer, step, n, 4))
                            project(PS[n][:], w, mixT).then_inc(tile_used.sem, 1)
                    leave(pe)
                if "norm2" in stages:
                    stream_norm("norm2", layer)
                if "query" in stages:
                    enter(pe, "query", layer)
                    with pe.Fori(0, 4) as step:
                        for e in range(2):
                            w = load_wait("query", layer, step, e)
                            pe.wait_ge(query_copied.sem, earlier(query_copied, "query", layer, step, e, 2))
                            project(PS[e][:], w, hT).then_inc(tile_used.sem, 1)
                        for e in range(2):
                            pe.wait_ge(query_copied.sem, query_copied.at("query", layer, step, e + 1))
                            pe.wait_ge(key_scores_read.sem, earlier(key_scores_read, "query", layer, step, e, 2))
                            for c in range(2):
                                for t in range(TT):
                                    last = mm(PS[2 + 2 * e + c][:, t * 128:(t + 1) * 128],
                                              q_peer[64 * c:64 * c + 64, e, t * 128:(t + 1) * 128],
                                              vec("keys")[64 * c:64 * c + 64, :], start=True, stop=True)
                            last.then_inc(key_scores.sem, 1)
                    leave(pe)
                if "select" in stages:
                    enter(pe, "select", layer)
                    with pe.Fori(0, TT) as step:
                        pe.wait_ge(picks_copied.sem, picks_copied.at("select", layer, step, 0))
                        pe.wait_ge(picks_ready.sem, picks_ready.at("select", layer, step, 3))
                        for n in range(3):
                            last = nc.tensor.transpose(PS[0][:, n * 128:(n + 1) * 128], pick[:, n, :], cst("ident"))
                        last.then_inc(picks_turned.sem, 1)
                    leave(pe)
                if "route" in stages:
                    enter(pe, "route", layer)
                    with pe.Fori(0, STEPS["route"]) as step:
                        for q in range(Q):
                            pe.wait_ge(onehots.sem, onehots.at("route", layer, step, q + 1))
                            pe.wait_ge(route_copied.sem, earlier(route_copied, "route", layer, step, q, 4))
                            for t in range(4):
                                last = mm(PS[q % 4][:, t * 128:(t + 1) * 128], oh_i[:, q % 2, t, :], oh_j[:, q % 2, t, :],
                                          start=True, stop=True)
                            last.then_inc(route_product.sem, 1)
                    leave(pe)
                if "dense" in stages:
                    enter(pe, "dense", layer)
                    with pe.Fori(0, STEPS["dense"]) as step:
                        for j in range(GROUP):
                            w = load_wait("dense", layer, step, j)
                            pe.wait_ge(gelu_done.sem, earlier(gelu_done, "dense", layer, step, j, 4))
                            project(PS[j][:], w, hT).then_inc(tile_used.sem, 1)
                        wv = []

                        def apply(m, j):
                            if m == 0:
                                wv.append(load_wait("dense", layer, step, GROUP + j))
                                pe.wait_ge(weighted.sem, weighted.at("dense", layer, step, j + 1))
                            if j == 0:
                                pe.wait_ge(y_added.sem, earlier(y_added, "dense", layer, step, m, 4))
                            last = mm(PS[4 + m % 4][:], wv[j][:, m * 128:(m + 1) * 128], a_cur[:, j, :],
                                      start=(j == 0), stop=(j == GROUP - 1), skip_group_check=True)
                            if m == KT - 1:
                                last.then_inc(tile_used.sem, 1)
                            elif j == GROUP - 1:
                                last.then_inc(y_ready.sem, 1)

                        for j in range(GROUP - 1):
                            apply(0, j)
                        for j in range(GROUP - 1):
                            apply(1, j)
                        apply(0, GROUP - 1)
                        apply(1, GROUP - 1)
                        for m in range(2, KT):
                            for j in range(GROUP):
                                apply(m, j)
                    leave(pe)
                if "final" in stages:
                    enter(pe, "final", layer)
                    leave(pe)

        @block.scalar
        def _(act):
            chain = Chain(act, scalar_chain)
            fn = nc.scalar.activation

            def stream_norm(stage, layer):
                enter(act, stage, layer)
                chain.begin(stage, layer, 0)
                for k in range(KT):
                    if k >= 2:
                        act.wait_ge(square_sums.sem, square_sums.at(stage, layer, 0, k - 1))
                    fn(sq[:, k % 2, :], xT[:, k, :], ACT.Square).then_inc(squares.sem, 1)
                act.wait_ge(square_sums.sem, square_sums.at(stage, layer, 0, KT))
                chain.link(fn(lnv, NS[:], ACT.Ln, bias=cst("eps"), scale=1.0 / D))
                fn(rstd[:, 0, :], lnv, ACT.Exp, scale=-0.5).then_inc(stream_rstd.sem, 1)
                b = 0 if stage == "norm1" else 3 * KT
                for k in range(KT):
                    act.wait_ge(stream_scaled.sem, stream_scaled.at(stage, layer, 0, k + 1))
                    fn(hT[:, k, :], hT[:, k, :], ACT.Identity, bias=modT[:, b + k:b + k + 1])
                chain.end()
                leave(act)

            def square(stage, layer, step, n, parts, slot):
                proj_wait(act, stage, layer, step, n)
                fn(sq[0:parts, slot % 2, :], P0[n % 2][0:parts, :], ACT.Square).then_inc(proj_squared.sem, 1)

            def norm(stage, layer, step, u):
                tiles_, parts, width, _, _, _, rot = norms(stage)[u]
                first = sum(len(x[0]) for x in norms(stage)[:u])
                for i, n in enumerate(tiles_):
                    square(stage, layer, step, n, parts, first + i)
                act.wait_ge(proj_sums.sem, proj_sums.at(stage, layer, step, u + 1))
                chain.link(fn(lnv[0:parts, :], NS[0:parts, :], ACT.Ln, bias=cst("eps")[0:parts, :], scale=1.0 / width))
                first_of = norms(stage)[u - 2][0][-1] + 1 if u >= 2 else 0
                act.wait_ge(proj_drained.sem, proj_drained.at(stage, layer, step, first_of))
                fn(rstd[0:parts, u % 2, :], lnv[0:parts, :], ACT.Exp, scale=-0.5).then_inc(proj_rstd.sem, 1)

            def attention(stage, layer, step):
                units = [(e, i) for e in range(2) for i in range(TT)]

                def expo(u):
                    e, i = units[u]
                    width = len(key_tiles(stage, i)) * 128
                    act.wait_ge(max_ready.sem, max_ready.at(stage, layer, step, u + 1))
                    nm = stat[:, u:u + 1]
                    if stage == "swa":
                        fn(stat[:, 16 + u:17 + u], sinks[:, e:e + 1], ACT.Exp, bias=nm)
                    fn(probs[:, u % 2, 0:width], S0[u % 2][:, 0:width], ACT.Exp, bias=nm,
                       accum_out=stat[:, 8 + u:9 + u]).then_inc(probs_ready.sem, 1)

                def copy(u):
                    e, i = units[u]
                    width = len(key_tiles(stage, i)) * 128
                    act.wait_ge(probs_turned.sem, probs_turned.at(stage, layer, step, u + 1))
                    act.wait_ge(unit_out.sem, earlier(unit_out, stage, layer, step, u, 2))
                    fn(probsT[:, u % 2, 0:width], T0[u % 2][:, 0:width], ACT.Copy).then_inc(turned_copied.sem, 1)

                for u in range(len(units) + 1):
                    if u < len(units):
                        expo(u)
                    if u >= 1:
                        copy(u - 1)

            act.wait_ge(consts_loaded, 16)
            fn(ident16[:], cst("ident"), ACT.Copy).then_inc(setup_done, 1)
            fn(masks16[:], C[:, CONST["mask_own_chunks"][0]:CONST["mask_own_chunks"][0] + 512], ACT.Copy
               ).then_inc(setup_done, 1)
            act.wait_ge(x_loaded, 16)
            with act.Fori(0, layers) as layer:
                if "ada" in stages:
                    enter(act, "ada", layer)
                    act.wait_ge(vecs_loaded, layer * 16 + 16)
                    fn(cond[:, 0, :], vec("c"), ACT.Sigmoid).then_inc(cond_sigmoid, 1)
                    with act.Fori(0, STEPS["ada"]) as step:
                        chain.begin("ada", layer, step)
                        for h in range(2):
                            act.wait_ge(tile_used.sem, tile_used.at("ada", layer, step, 8))
                            if h == 0:
                                act.wait_ge(mod_columns.sem, mod_columns.at("ada", layer, step, 0))
                            fn(row[0:1, h * 512:(h + 1) * 512], PS[h][0:1, :], ACT.Copy).then_inc(row_copied.sem, 1)
                        chain.end()
                    leave(act)
                if "norm1" in stages:
                    stream_norm("norm1", layer)
                for stage in ("swa_kv", "swa", "mla_c", "mla", "fox"):
                    if stage not in stages:
                        continue
                    enter(act, stage, layer)
                    with act.Fori(0, STEPS[stage]) as step:
                        chain.begin(stage, layer, step)
                        for u in range(len(norms(stage))):
                            norm(stage, layer, step, u)
                        if stage == "mla_c":
                            act.wait_ge(vector_chain.sem, vector_chain.at(stage, layer, 0, 2))
                            chain.link(fn(fgt[0:8, 2, :], fgt[0:8, 1, :], ACT.Exp, scale=-1.0))
                            chain.link(fn(fgt[0:8, 2, :], fgt[0:8, 2, :], ACT.Ln, bias=cst("one")[0:8, :]))
                        chain.end()
                        if stage in U8:
                            attention(stage, layer, step)
                    leave(act)
                if "gates" in stages:
                    enter(act, "gates", layer)
                    with act.Fori(0, 4) as step:
                        act.wait_ge(bias_copied.sem, bias_copied.at("gates", layer, step, 1))
                        for g in range(6):
                            t = [0, 1, 3, 4, 6, 7][g]
                            act.wait_ge(tile_used.sem, tile_used.at("gates", layer, step, t + 1))
                            act.wait_ge(branch_gated.sem, earlier(branch_gated, "gates", layer, step, g, 2))
                            fn(sig[:, g % 2, :], PS[g % 2][:], ACT.Sigmoid, bias=gate_b[:, g:g + 1]).then_inc(gate_open.sem, 1)
                    leave(act)
                if "w_out" in stages:
                    enter(act, "w_out", layer)
                    leave(act)
                if "norm2" in stages:
                    stream_norm("norm2", layer)
                if "query" in stages:
                    enter(act, "query", layer)
                    with act.Fori(0, 4) as step:
                        for e in range(2):
                            act.wait_ge(tile_used.sem, tile_used.at("query", layer, step, e + 1))
                            act.wait_ge(key_scores.sem, earlier(key_scores, "query", layer, step, e, 2))
                            fn(q_peer[:, e, :], PS[e][:], ACT.Copy).then_inc(query_copied.sem, 1)
                    leave(act)
                if "select" in stages:
                    enter(act, "select", layer)
                    with act.Fori(0, TT) as step:
                        act.wait_ge(pick_shifted.sem, pick_shifted.at("select", layer, step, 1))
                        t2 = top.rearrange("p h k -> p (h k)")
                        fn(t2, t2, ACT.Exp).then_inc(pick_exp.sem, 1)
                    leave(act)
                if "route" in stages:
                    enter(act, "route", layer)
                    with act.Fori(0, STEPS["route"]) as step:
                        for q in range(Q):
                            b = q // (Q // 2)
                            act.wait_ge(route_product.sem, route_product.at("route", layer, step, q + 1))
                            if q % (Q // 2) == 0:
                                act.wait_ge(route_free[b].sem, route_free[b].at("route", layer, step, 0))
                            t0 = (q % (Q // 2)) * 4
                            fn(route[b][:, :, t0:t0 + 4], PS[q % 4][:].rearrange("p (t j) -> p j t", t=4), ACT.Copy
                               ).then_inc(route_copied.sem, 1)
                    leave(act)
                if "dense" in stages:
                    enter(act, "dense", layer)
                    with act.Fori(0, STEPS["dense"]) as step:
                        for j in range(GROUP):
                            act.wait_ge(tile_used.sem, tile_used.at("dense", layer, step, j + 1))
                            fn(a_cur[:, j, :], PS[j][:], ACT.Gelu).then_inc(gelu_done.sem, 1)
                    leave(act)
                if "final" in stages:
                    enter(act, "final", layer)
                    leave(act)

        @block.gpsimd
        def _(pool):
            for s in signals:
                if s.credit:
                    pool.sem_inc(s.sem, s.credit)
            pool.sem_inc(boundary, 1)
            with pool.Fori(0, layers) as layer:
                for stage in stages:
                    enter(pool, stage, layer)
                    if stage == "route":
                        with pool.Fori(0, STEPS["route"]) as step:
                            for b in range(2):
                                pool.wait_ge(route_copied.sem, route_copied.at("route", layer, step, (Q // 2) * (b + 1)))
                                pool.dma_start(route_dram[:, ds(2 * step + b, 1), :].rearrange("p a n -> p (a n)"),
                                               route[b].rearrange("p j t -> p (j t)")
                                               ).then_inc(route_stored[b].sem, 16)
                            for b in range(2):
                                pool.wait_ge(route_stored[b].sem, route_stored[b].at("route", layer, step, 16))
                                pool.sem_inc(route_free[b].sem, 1)
                    if stage == "dense":
                        with pool.Fori(0, STEPS["dense"]) as step:
                            pool.wait_ge(weighted.sem, weighted.at("dense", layer, step, 0))
                            pool.dma_start(g_cur, route_dram[:, :, ds(step * (GROUP * TOKENS), GROUP * TOKENS)]
                                           ).then_inc(route_loaded.sem, 16)
                    leave(pool)

        @block.vector
        def _(dve):
            chain = Chain(dve, vector_chain)
            chain.held = held
            stt, tt, ts = nc.vector.scalar_tensor_tensor, nc.vector.tensor_tensor, nc.vector.tensor_scalar

            def stream_norm(stage, layer):
                enter(dve, stage, layer)
                chain.begin(stage, layer, 0)
                n1 = stage == "norm1"
                g = gain[:, 0:KT] if n1 else gain[:, KT:2 * KT]
                sc = modT[:, KT:2 * KT] if n1 else modT[:, 4 * KT:5 * KT]
                chain.link(stt(g, sc, 1.0, vec("norm1" if n1 else "norm2"), ALU.add, ALU.mult))
                dve.wait_ge(stream_rstd.sem, stream_rstd.at(stage, layer, 0, 1))
                for k in range(KT):
                    stt(hT[:, k, :], xT[:, k, :], g[:, k:k + 1], rstd[:, 0, :], ALU.mult, ALU.mult
                        ).then_inc(stream_scaled.sem, 1)
                chain.end()
                leave(dve)

            def norm(stage, layer, step, u):
                tiles_, parts, _, gains, dests, _, rot = norms(stage)[u]
                dve.wait_ge(proj_rstd.sem, proj_rstd.at(stage, layer, step, u + 1))
                for n, g, dst in zip(tiles_, gains, dests):
                    out = qn[0:parts, u % 2, :] if rot else dst[0:parts, :]
                    stt(out, P0[n % 2][0:parts, :], g[0:parts, :], rstd[0:parts, u % 2, :], ALU.mult, ALU.mult
                        ).then_inc(proj_drained.sem, 1)
                if rot:
                    n = tiles_[0]
                    dve.wait_ge(proj_drained.sem, proj_drained.at(stage, layer, step, n + 1))
                    chain.mark(tt(rope[0:parts, 0, :], qn[0:parts, u % 2, :], cst("cos_" + rot)[0:parts, :], ALU.mult))
                    dve.wait_ge(rotated.sem, rotated.at(stage, layer, step, u + 1))
                    tt(rope[0:parts, 1, :], NS[0:parts, :], cst("sin_" + rot)[0:parts, :], ALU.mult
                       ).then_inc(rotation_read.sem, 1)
                    chain.settle()
                    dve.wait_ge(rotation_read.sem, rotation_read.at(stage, layer, step, u + 1))
                    tt(dests[0][0:parts, :], rope[0:parts, 0, :], rope[0:parts, 1, :], ALU.add
                       ).then_inc(qk_ready.sem, 1)

            def copy_values(stage, layer, step, n):
                proj_wait(dve, stage, layer, step, n)
                nc.vector.tensor_copy(v_cur.rearrange("p t c -> p (t c)"), P0[n % 2][:]).then_inc(proj_drained.sem, 1)

            def attention(stage, layer, step, o):
                units = [(e, i) for e in range(2) for i in range(TT)]

                def maxi(u):
                    e, i = units[u]
                    width = len(key_tiles(stage, i)) * 128
                    dve.wait_ge(scores_ready.sem, scores_ready.at(stage, layer, step, u + 1))
                    nm = stat[:, u:u + 1]
                    if stage == "swa":
                        chain.link(nc.vector.tensor_reduce(nm, S0[u % 2][:, 0:width], AX.X, ALU.max))
                        ts(nm, nm, sinks[:, e:e + 1], -1.0, ALU.max, ALU.mult).then_inc(max_ready.sem, 1)
                    else:
                        nc.vector.tensor_reduce(nm, S0[u % 2][:, 0:width], AX.X, ALU.max, negate=True
                                                ).then_inc(max_ready.sem, 1)

                def scale(u):
                    e, i = units[u]
                    width = len(key_tiles(stage, i)) * 128
                    dve.wait_ge(probs_ready.sem, probs_ready.at(stage, layer, step, u + 1))
                    total = stat[:, 8 + u:9 + u]
                    if stage == "swa":
                        chain.link(tt(total, total, stat[:, 16 + u:17 + u], ALU.add))
                    chain.link(nc.vector.reciprocal(stat[:, 24 + u:25 + u], total))
                    dve.wait_ge(probs_turned.sem, earlier(probs_turned, stage, layer, step, u, 2))
                    ts(pnorm[:, u % 2, 0:width], probs[:, u % 2, 0:width], stat[:, 24 + u:25 + u], None, ALU.mult
                       ).then_inc(probs_scaled.sem, 1)

                for u in range(len(units) + 1):
                    if u < len(units):
                        maxi(u)
                    if u >= 1:
                        scale(u - 1)
                dve.wait_ge(unit_out.sem, unit_out.at(stage, layer, step, 8))
                nc.vector.tensor_copy(o[:, ds(step, 1), :].rearrange("p a t -> p (a t)"), O0[:]
                                      ).then_inc(pair_stored.sem, 1)

            dve.wait_ge(consts_loaded, 16)
            dve.wait_ge(x_loaded, 16)
            with dve.Fori(0, layers) as layer:
                if "ada" in stages:
                    enter(dve, "ada", layer)
                    dve.wait_ge(cond_sigmoid, layer + 1)
                    tt(cond[:, 1, :], vec("c"), cond[:, 0, :], ALU.mult).then_inc(cond_ready, 1)
                    with dve.Fori(0, STEPS["ada"]) as step:
                        dve.wait_ge(mod_columns.sem, mod_columns.at("ada", layer, step, 1))
                        tt(modT[:, ds(step * KT, KT)], PS[2][:, 0:KT], V[:, ds(step * KT, KT)], ALU.add
                           ).then_inc(mod_drained.sem, 1)
                    leave(dve)
                if "norm1" in stages:
                    stream_norm("norm1", layer)
                for stage in ("swa_kv", "swa", "mla_c", "mla", "fox"):
                    if stage not in stages:
                        continue
                    enter(dve, stage, layer)
                    with dve.Fori(0, STEPS[stage]) as step:
                        chain.begin(stage, layer, step)
                        if stage == "swa_kv":
                            for n, (name, dim) in enumerate((("swa_q", 64), ("mla_q", 96), ("fox_q", 64))):
                                chain.mark(ts(gq[:, n:n + 1], vec(name), float(dim) ** -0.5, None, ALU.mult))
                            norm(stage, layer, step, 0)
                            copy_values(stage, layer, step, 1)
                        if stage == "swa":
                            chain.link(nc.vector.tensor_copy(sinks, V[:, ds(VEC["sink"][0] + step * 2, 2)]))
                            norm(stage, layer, step, 0)
                            attention(stage, layer, step, oT[0])
                        if stage == "mla_c":
                            norm(stage, layer, step, 0)
                            proj_wait(dve, stage, layer, step, 4)
                            chain.link(ts(fgt[0:8, 0, :], T0[0][0:8, :], vec("b_forget")[0:8, :], None, ALU.add))
                            chain.mark(stt(fgt[0:8, 1, :], fgt[0:8, 0, :], -1.0, fgt[0:8, 0, :], ALU.mult, ALU.max))
                            norm(stage, layer, step, 1)
                            proj_wait(dve, stage, layer, step, 3)
                            nc.vector.tensor_copy(k_rot[64:96, :], P0[1][64:96, :]).then_inc(proj_drained.sem, 1)
                            dve.wait_ge(scalar_chain.sem, scalar_chain.at(stage, layer, 0, SCALAR_LINKS.get("mla_c", 0)))
                            chain.link(stt(fgt[0:8, 3, :], fgt[0:8, 0, :], 0.0, fgt[0:8, 2, :], ALU.min, ALU.subtract))
                            chain.link(nc.vector.tensor_tensor_scan(cst("fq")[0:8, :], cst("fk")[0:8, :], fgt[0:8, 3, :],
                                                                    0.0, ALU.mult, ALU.add))
                            chain.mark(ts(cst("fk")[32:40, :], cst("fq")[0:8, :], -1.0, None, ALU.mult))
                            chain.mark(nc.vector.tensor_copy(cst("fq")[64:72, :], cst("fq")[0:8, :]))
                            ts(cst("fk")[96:104, :], cst("fq")[0:8, :], -1.0, None, ALU.mult).then_inc(proj_drained.sem, 1)
                        if stage == "mla":
                            for u in range(4):
                                norm(stage, layer, step, u)
                            copy_values(stage, layer, step, 4)
                            attention(stage, layer, step, oT[1])
                        if stage == "fox":
                            for e in range(2):
                                r = slice(64 * e, 64 * e + 40)
                                ts(fq_head[r, e, :], cst("fq")[r, :],
                                   C[r, ds(CONST["head_pick"][0] + 2 * step + e, 1)], None, ALU.mult
                                   ).then_inc(forget_bias.sem, 1)
                            norm(stage, layer, step, 0)
                            norm(stage, layer, step, 1)
                            copy_values(stage, layer, step, 2)
                            attention(stage, layer, step, oT[2])
                        chain.end()
                    leave(dve)
                if "gates" in stages:
                    enter(dve, "gates", layer)
                    with dve.Fori(0, 4) as step:
                        chain.begin("gates", layer, step)
                        nc.vector.tensor_copy(gate_b[:, 0:6], V[:, ds(VEC["b_gate"][0] + step * 6, 6)]
                                              ).then_inc(bias_copied.sem, 1)
                        for g in range(6):
                            e, i = g // 3, g % 3
                            dve.wait_ge(gate_open.sem, gate_open.at("gates", layer, step, g + 1))
                            if g % 2 == 0:
                                dve.wait_ge(branch_ready.sem, branch_ready.at("gates", layer, step, g // 2 + 1))
                            else:
                                dve.wait_ge(tile_used.sem, tile_used.at("gates", layer, step, 3 * (g // 2) + 3))
                            tt(gated[:, g % 2, :], sig[:, g % 2, :], PS[2 + g % 2][:], ALU.mult).then_inc(branch_gated.sem, 1)
                            dve.wait_ge(branch_gated.sem, branch_gated.at("gates", layer, step, g + 1))
                            y = mixT[:, ds(2 * step + e, 1), :].rearrange("p a t -> p (a t)")
                            if i == 1:
                                chain.link(tt(gated[:, g % 2, :], gated[:, g % 2, :], gated[:, (g - 1) % 2, :], ALU.add))
                            if i == 2:
                                chain.link(tt(y, gated[:, g % 2, :], gated[:, (g - 1) % 2, :], ALU.add))
                        chain.end()
                    leave(dve)
                if "w_out" in stages:
                    enter(dve, "w_out", layer)
                    with dve.Fori(0, 2) as step:
                        for n in range(4):
                            dve.wait_ge(tile_used.sem, tile_used.at("w_out", layer, step, n + 1))
                            xk = xT[:, ds(step * 4 + n, 1), :].rearrange("p a t -> p (a t)")
                            stt(xk, PS[n][:], modT[:, ds(2 * KT + step * 4 + n, 1)], xk, ALU.mult, ALU.add
                                ).then_inc(mixed.sem, 1)
                    leave(dve)
                if "norm2" in stages:
                    stream_norm("norm2", layer)
                if "query" in stages:
                    enter(dve, "query", layer)
                    with dve.Fori(0, 4) as step:
                        chain.begin("query", layer, step)
                        for e in range(2):
                            cells = [(t, c) for t in range(TT) for c in range(2)]

                            def cell(t, c):
                                return PS[2 + 2 * e + c][:, t * 128:(t + 1) * 128], sval_cur[:, e, t, c, :], sidx_cur[:, e, t, c, :]

                            dve.wait_ge(key_scores.sem, key_scores.at("query", layer, step, e + 1))
                            dve.sem_inc(held, 1)
                            for t, c in cells:
                                s, v, _ = cell(t, c)
                                chain.mark(nc.vector.max(v[:, 0:8], s))
                            chain.settle_for_search()
                            for n, (t, c) in enumerate(cells):
                                s, v, x = cell(t, c)
                                chain.mark(nc.vector.match_replace(rest[:, n, :], v[:, 0:8], s, LOWEST))
                                chain.mark(nc.vector.max_index(x[:, 0:8], v[:, 0:8], s))
                            chain.settle_for_search()
                            for n, (t, c) in enumerate(cells):
                                s, v, x = cell(t, c)
                                chain.mark(nc.vector.max(v[:, 8:16], rest[:, n, :]))
                            chain.settle_for_search()
                            for n, (t, c) in enumerate(cells):
                                s, v, x = cell(t, c)
                                chain.mark(nc.vector.max_index(x[:, 8:16], v[:, 8:16], rest[:, n, :]))
                            chain.settle_for_search()
                            sv = sval.rearrange("p t h c k -> p t h (c k)")[:, :, ds(2 * step + e, 1), :]
                            si = sidx.rearrange("p t h c k -> p t h (c k)")[:, :, ds(2 * step + e, 1), :]
                            chain.mark(nc.vector.tensor_copy(sv.rearrange("p t h n -> p t (h n)"),
                                                             sval_cur[:, e].rearrange("p t c k -> p t (c k)")))
                            nc.vector.tensor_copy(si.rearrange("p t h n -> p t (h n)"),
                                                  sidx_cur[:, e].rearrange("p t c k -> p t (c k)")
                                                  ).then_inc(key_scores_read.sem, 1)
                            dve.wait_ge(key_scores_read.sem, key_scores_read.at("query", layer, step, e + 1))
                            chain.settle_for_search()
                        chain.end()
                    leave(dve)
                if "select" in stages:
                    enter(dve, "select", layer)
                    with dve.Fori(0, TT) as step:
                        chain.begin("select", layer, step)
                        sv = sval[:, ds(step, 1)].rearrange("p a h c k -> p (a h) c k")
                        si = sidx[:, ds(step, 1)].rearrange("p a h c k -> p (a h) c k")
                        chain.link(tt(cand.rearrange("p h (a b) -> p h a b", a=16),
                                      sv[:, :, 0, :].unsqueeze(3).broadcast_to([128, HEADS, 16, 16]),
                                      sv[:, :, 1, :].unsqueeze(2).broadcast_to([128, HEADS, 16, 16]), ALU.add))
                        dve.sem_inc(held, 1)
                        for h in range(HEADS):
                            chain.mark(nc.vector.max(top[:, h, 0:8], cand[:, h, :]))
                        chain.settle_for_search()
                        for h in range(HEADS):
                            chain.mark(nc.vector.max_index(pos[:, h, 0:8], top[:, h, 0:8], cand[:, h, :]))
                        chain.settle_for_search()
                        for h in range(HEADS):
                            chain.mark(nc.vector.match_replace(cand[:, h, :], top[:, h, 0:8], cand[:, h, :], LOWEST))
                        chain.settle_for_search()
                        for h in range(HEADS):
                            chain.mark(nc.vector.max(top[:, h, 8:16], cand[:, h, :]))
                        chain.settle_for_search()
                        for h in range(HEADS):
                            chain.mark(nc.vector.max_index(pos[:, h, 8:16], top[:, h, 8:16], cand[:, h, :]))
                        chain.link(nc.vector.tensor_copy(esum[:, 1, :], top[:, :, 0]))
                        tt(top, top, esum[:, 1, :].unsqueeze(2).broadcast_to([128, HEADS, 16]), ALU.subtract
                           ).then_inc(pick_shifted.sem, 1)
                        p2 = pos.rearrange("p h k -> p (h k)")
                        chain.mark(ts(pos_part[:, 0, :], p2, 4, None, ALU.logical_shift_right))
                        chain.link(ts(pos_part[:, 1, :], p2, 15, None, ALU.bitwise_and))
                        chain.link(nc.vector.tensor_copy(pos_f.rearrange("p a n -> p (a n)"),
                                                         pos_part.rearrange("p a n -> p (a n)")))
                        for half in range(2):
                            chain.link(tt(onehot16, pos_f[:, half, :].unsqueeze(2).broadcast_to([128, 128, 16]),
                                          cst("iota")[:, 0:16].unsqueeze(1).broadcast_to([128, 128, 16]), ALU.is_equal))
                            o4 = onehot16.rearrange("p (h k) c -> p h k c", h=HEADS)
                            chain.link(tt(o4, o4, si[:, :, half, :].unsqueeze(2).broadcast_to([128, HEADS, 16, 16]),
                                          ALU.mult))
                            if half == 0:
                                dve.wait_ge(picks_turned.sem, picks_turned.at("select", layer, step, 0))
                            nc.vector.tensor_reduce(pick[:, half, :], onehot16, AX.X, ALU.add).then_inc(picks_ready.sem, 1)
                            dve.wait_ge(picks_ready.sem, picks_ready.at("select", layer, step, half + 1))
                        dve.wait_ge(pick_exp.sem, pick_exp.at("select", layer, step, 1))
                        chain.link(nc.vector.tensor_reduce(esum[:, 0, :], top, AX.X, ALU.add))
                        chain.link(nc.vector.reciprocal(esum[:, 1, :], esum[:, 0, :]))
                        tt(pick[:, 2, :].rearrange("p (h k) -> p h k", h=HEADS), top,
                           esum[:, 1, :].unsqueeze(2).broadcast_to([128, HEADS, 16]), ALU.mult).then_inc(picks_ready.sem, 1)
                        dve.wait_ge(picks_turned.sem, picks_turned.at("select", layer, step, 1))
                        nc.vector.tensor_copy(pickT[:, :, ds(step * 128, 128)],
                                              PS[0][:, 0:384].rearrange("p (n t) -> p n t", n=3)
                                              ).then_inc(picks_copied.sem, 1)
                        chain.end()
                    leave(dve)
                if "route" in stages:
                    enter(dve, "route", layer)
                    with dve.Fori(0, STEPS["route"]) as step:
                        for q in range(Q):
                            dve.wait_ge(route_product.sem, earlier(route_product, "route", layer, step, q, 2))
                            for t in range(4):
                                tok = step * (2 * TOKENS) + (4 * q + t)
                                ts(oh_i[:, q % 2, t, :], cst("iota"), pickT[:, 0, ds(tok, 1)], None, ALU.is_equal)
                                last = ts(oh_j[:, q % 2, t, :], cst("iota"), pickT[:, 1, ds(tok, 1)],
                                          pickT[:, 2, ds(tok, 1)], ALU.is_equal, ALU.mult)
                            last.then_inc(onehots.sem, 1)
                    leave(dve)
                if "dense" in stages:
                    enter(dve, "dense", layer)
                    nc.vector.memset(mixT[:], 0.0).then_inc(sum_cleared, 1)
                    dve.wait_ge(sum_cleared, layer + 1)
                    dve.sem_inc(held, 1)
                    with dve.Fori(0, STEPS["dense"]) as step:
                        for j in range(GROUP):
                            if j == 0:
                                dve.wait_ge(route_loaded.sem, route_loaded.at("dense", layer, step, 16))
                            dve.wait_ge(gelu_done.sem, gelu_done.at("dense", layer, step, j + 1))
                            a3 = a_cur[:, j, :].rearrange("p (g t) -> p g t", t=TOKENS)
                            tt(a3, a3, g_cur[:, :, j * TOKENS:(j + 1) * TOKENS], ALU.mult).then_inc(weighted.sem, 1)
                        for m in range(KT):
                            if m < KT - 1:
                                dve.wait_ge(y_ready.sem, y_ready.at("dense", layer, step, m + 1))
                            else:
                                dve.wait_ge(tile_used.sem, tile_used.at("dense", layer, step, 2 * GROUP))
                            tt(mixT[:, m, :], mixT[:, m, :], PS[4 + m % 4][:], ALU.add).then_inc(y_added.sem, 1)
                    leave(dve)
                if "final" in stages:
                    enter(dve, "final", layer)
                    for k in range(KT):
                        stt(xT[:, k, :], mixT[:, k, :], modT[:, 5 * KT + k:5 * KT + k + 1], xT[:, k, :], ALU.mult, ALU.add)
                    leave(dve)
    assert not MISCOUNTED, MISCOUNTED


def lay_constants():
    c = np.zeros((128, CONST_COLS), np.float32)

    def put(name, a):
        a = np.asarray(a, np.float32)
        c[:a.shape[0], CONST[name][0]:CONST[name][0] + a.shape[1]] = a

    put("ident", np.eye(128))
    b = np.zeros((128, 128))
    b[:64, :64] = b[64:, 64:] = 1
    put("block64", b)
    put("ones", np.ones((128, 128)))

    def rotation(size, starts, half):
        r = np.zeros((size, size))
        for s in starts:
            for i in range(half):
                r[s + half + i, s + i] = -1
                r[s + i, s + half + i] = 1
        return r

    put("rot_a", rotation(128, (0, 64), 32))
    put("rot_b", rotation(128, (64,), 16))
    pos = np.arange(T, dtype=np.float32)
    for name, dim, starts in (("a", 64, (0, 64)), ("b", 32, (64,))):
        inv = np.float32(10000.0) ** (-np.arange(0, dim, 2, dtype=np.float32) / np.float32(dim))
        ang = (pos[:, None] * inv[None, :]).astype(np.float32).astype(np.float64)
        cos, sin = np.ones((128, T)), np.zeros((128, T))
        for s in starts:
            for h in range(2):
                cos[s + h * dim // 2:s + (h + 1) * dim // 2] = np.cos(ang).T
                sin[s + h * dim // 2:s + (h + 1) * dim // 2] = np.sin(ang).T
        put("cos_" + name, cos)
        put("sin_" + name, sin)
    q, k = np.arange(128)[:, None], np.arange(256)[None, :]
    put("mask_own_chunks", np.where(k[:, :128] // 64 <= q // 64, 0, NEG))
    qc = q // 64 + 2
    put("mask_window", np.where((k // 64 <= qc) & (k // 64 >= qc - 1), 0, NEG))
    put("mask_frames", np.where(k[:, :128] <= q, 0, NEG))
    put("iota", np.tile(np.arange(128), (128, 1)))
    e = np.zeros((104, 8))
    for r in (0, 32, 64, 96):
        e[r:r + 8] = np.eye(8)
    put("head_pick", e)
    put("eps", np.full((128, 1), EPS))
    put("one", np.ones((128, 1)))
    f = np.zeros((104, T))
    f[32:40] = f[96:104] = 1
    put("fq", f)
    put("fk", f[::-1])
    return c


def tiles_of(w):
    k, n = w.shape[0] // 128, w.shape[1] // 128
    return w.reshape(k, 128, n, 128).transpose(2, 1, 0, 3).reshape(n, 128, k * 128)


def lay_stream(w_ada, w_in, q_up, kv_up, w_branch, w_out, w_q):
    out = []

    def pad(a):
        t = np.zeros((128, 1024), np.float32)
        t[:, :a.shape[1]] = a
        return t

    for g in range(6):
        for k in range(KT):
            out.append(w_ada[k * 128:(k + 1) * 128, g * 1024:(g + 1) * 1024])
    cuts = np.cumsum([0, 512, 128, 128, 256, 128, 32, 512, 512, 512, 8, 3 * D])
    aq, ak, av, cq, ckv, kr, fq, fk, fv, ff, gate = [w_in[:, a:b] for a, b in zip(cuts[:-1], cuts[1:])]
    out += [tiles_of(ak)[0], tiles_of(av)[0]]
    for m in range(PAIRS):
        out.append(tiles_of(np.concatenate([aq[:, m * 64:m * 64 + 64], aq[:, (m + 4) * 64:(m + 5) * 64]], 1))[0])
    out += list(tiles_of(cq)) + list(tiles_of(ckv))
    misc = np.concatenate([kr, ff], 1)
    out.append(pad(misc.reshape(KT, 128, 40).transpose(1, 0, 2).reshape(128, KT * 40)))
    kv = kv_up.reshape(128, HEADS, 128)
    for m in range(PAIRS):
        q = q_up[:, m * 192:(m + 1) * 192].reshape(2, 128, 192).transpose(1, 0, 2).reshape(128, 384)
        out.append(pad(np.concatenate([q, kv[:, 2 * m, :64], kv[:, 2 * m + 1, :64],
                                       kv[:, 2 * m, 64:], kv[:, 2 * m + 1, 64:]], 1)))
    fq, fk, fv = tiles_of(fq), tiles_of(fk), tiles_of(fv)
    for m in range(PAIRS):
        out += [fq[m], fk[m], fv[m]]
    gates = tiles_of(gate)
    order = np.concatenate([np.r_[m * 64:m * 64 + 64, (m + 4) * 64:(m + 5) * 64] for m in range(PAIRS)])
    br = [tiles_of(w_branch[0][order]), tiles_of(w_branch[1]), tiles_of(w_branch[2])]
    for m in range(0, KT, 2):
        for a in range(3):
            pairs = [((2 * a + b) // 3 + m, (2 * a + b) % 3) for b in range(2)]
            out += [gates[i * KT + mm] for mm, i in pairs]
            out.append(np.concatenate([br[i][mm] for mm, i in pairs], 1))
    out += list(tiles_of(w_out)) + list(tiles_of(w_q))
    return out


def lay_vectors(c, b_ada, n1, n2, b_gate, b_forget, sink, aq, ak, cq, ckv, bq, bk, fq, fk, keys):
    v = np.zeros((128, VEC_COLS), np.float32)

    def put(name, a):
        v[:a.shape[0], VEC[name][0]:VEC[name][0] + a.shape[1]] = a

    put("b_ada", b_ada.reshape(48, 128).T)
    put("norm1", n1.reshape(KT, 128).T)
    put("norm2", n2.reshape(KT, 128).T)
    put("b_gate", b_gate.reshape(3, KT, 128).transpose(2, 1, 0).reshape(128, 24))
    put("sink", np.tile(sink.reshape(2, 4).T.reshape(1, 8), (128, 1)))
    put("swa_q", np.tile(aq, 2)[:, None])
    put("swa_k", np.tile(ak, 2)[:, None])
    put("cq", cq.reshape(2, 128).T)
    put("ckv", ckv[:, None])
    put("mla_q", bq[:, None])
    put("mla_k", bk[:, None])
    put("fox_q", np.tile(fq, 2)[:, None])
    put("fox_k", np.tile(fk, 2)[:, None])
    put("b_forget", b_forget[:, None])
    put("c", c.reshape(KT, 128).T)
    put("keys", keys.transpose(0, 2, 1).reshape(128, 128))
    return v


def kernel(**inputs):
    import concourse.bacc as bacc
    from concourse.bass_utils import run_bass_kernel_spmd as run

    arrays = lay_inputs(inputs)
    nc = bacc.Bacc("TRN2", target_bir_lowering=False, num_devices=1)
    build(nc, arrays)
    r = run(nc, [arrays], core_ids=[0])
    y = r.results[0]["out_t"]
    return np.ascontiguousarray(y.transpose(2, 1, 0)).reshape(1, T, D)


def lay_inputs(inputs):
    a = {k: np.asarray(v) for k, v in inputs.items()}
    L = LAYERS
    stream = np.stack([t for l in range(L) for t in lay_stream(
        a["w_ada"][l], a["w_in"][l], a["mla_w_q_up"][l], a["mla_w_kv_up"][l], a["w_branch"][l],
        a["w_out"][l], a["peer_w_q"][l])])
    vecs = np.stack([lay_vectors(a["c"][0], a["b_ada"][l], a["norm1_g"][l], a["norm2_g"][l], a["b_gate"][l],
                                 a["b_forget"][l], a["swa_sink"][l], a["swa_qnorm"][l], a["swa_knorm"][l],
                                 a["mla_q_norm"][l], a["mla_kv_norm"][l], a["mla_qnorm"][l], a["mla_knorm"][l],
                                 a["fox_qnorm"][l], a["fox_knorm"][l], a["peer_sub_keys"][l]) for l in range(L)])
    u = a["peer_u"].reshape(L, KEYS, KEYS, KT, 128).transpose(0, 2, 4, 3, 1)
    v = a["peer_v"].reshape(L, KEYS, KEYS, D).transpose(0, 2, 1, 3)
    return {
        "x_t": np.ascontiguousarray(a["x"][0].reshape(T, KT, 128).transpose(2, 1, 0)),
        "stream": np.ascontiguousarray(stream),
        "vecs": vecs,
        "consts": lay_constants(),
        "tab_u": np.ascontiguousarray(u).reshape(L * KEYS, 128, D),
        "tab_v": np.ascontiguousarray(v).reshape(L * KEYS, 128, D),
    }


def build(nc, arrays, **options):
    args = {n: nc.dram_tensor(n, a.shape, mybir.dt.from_np(a.dtype), kind="ExternalInput").ap()
            for n, a in arrays.items()}
    out_t = nc.dram_tensor("out_t", (128, KT, T), F32, kind="ExternalOutput").ap()
    route = nc.dram_tensor("route_scratch", (128, T // TOKENS, 128 * TOKENS), F32, kind="Internal").ap()
    build_trunk(nc, args["x_t"], args["stream"], args["vecs"], args["consts"], args["tab_u"], args["tab_v"],
                out_t, route, **options)
```

```python
from contextlib import ExitStack

import numpy as np

import concourse.bass as bass
from concourse import mybir

F32 = mybir.dt.float32
F32R = mybir.dt.float32r
BF16 = mybir.dt.bfloat16
U32 = mybir.dt.uint32
ALU = mybir.AluOpType
ACT = mybir.ActivationFunctionType
AX = mybir.AxisListType
ds = bass.ds

LAYERS = 2
D = 1024
T = 512
KT = D // 128
TT = T // 128
HEADS = 8
PAIRS = HEADS // 2
EPS = 1e-6
NEG = -1e30
LOWEST = -3.0e38
PICKS = 16
KEYS = 128
GROUP = 4
TOKENS = 32

SLOTS = 6


def ring(first, n):
    return [(first + i) % SLOTS for i in range(n)]


TILES = {
    "ada": (2, ring(0, KT)),
    "swa_kv": (1, ring(2, 2)),
    "swa": (PAIRS, ring(4, 1 + KT)),
    "mla_c": (1, ring(5, 4)),
    "mla": (PAIRS, ring(3, 1)),
    "fox": (PAIRS, ring(4, 3)),
    "gates": (4, ring(1, 9)),
    "w_out": (2, ring(4, 4)),
    "query": (4, ring(2, 2)),
    "dense": (KEYS // GROUP, [4, 5, 4, 5, 0, 1, 2, 3]),
}
STAGES = ["ada", "norm1", "swa_kv", "swa", "mla_c", "mla", "fox", "gates", "w_out",
          "norm2", "query", "select", "route", "dense", "final"]
STEPS = {"ada": 2, "norm1": 1, "swa_kv": 1, "swa": PAIRS, "mla_c": 1, "mla": PAIRS, "fox": PAIRS,
         "gates": 4, "w_out": 2, "norm2": 1, "query": 4, "select": TT, "route": T // (2 * TOKENS),
         "dense": KEYS // GROUP, "final": 1}
STREAM_TILES = sum(s * len(k) for n, (s, k) in TILES.items() if n != "dense")

CONST = {}
_n = 0
for _name, _w in (("ident", 128), ("block64", 128), ("ones", 128), ("rot_a", 128), ("rot_b", 128),
                  ("cos_a", T), ("sin_a", T), ("cos_b", T), ("sin_b", T),
                  ("mask_own_chunks", 128), ("mask_window", 256), ("mask_frames", 128),
                  ("iota", 128), ("head_pick", 8), ("eps", 1), ("one", 1), ("zero", 1), ("fq", T), ("fk", T)):
    CONST[_name] = (_n, _w)
    _n += _w
CONST_COLS = _n
VEC = {}
_n = 0
for _name, _w in (("b_ada", 48), ("norm1", 8), ("norm2", 8), ("b_gate", 24), ("sink", 8), ("swa_q", 1), ("swa_k", 1),
                  ("cq", 2), ("ckv", 1), ("mla_q", 1), ("mla_k", 1), ("fox_q", 1), ("fox_k", 1),
                  ("b_forget", 1), ("keys", 128)):
    VEC[_name] = (_n, _w)
    _n += _w
VEC_COLS = _n


class Signal:

    def __init__(self, sem, per_step, credit=1):
        self.sem = sem
        self.per_step = per_step
        self.credit = credit
        self.base, n = {}, credit
        for stage in STAGES:
            self.base[stage] = n
            n += STEPS[stage] * per_step.get(stage, 0)
        self.per_layer = n - credit

    def at(self, stage, layer, step, n):
        return layer * self.per_layer + step * self.per_step.get(stage, 0) + (self.base[stage] + n)


class Chain:

    def __init__(self, eng, own):
        self.eng, self.own = eng, own

    def begin(self, stage, layer, step):
        self.where, self.n = (stage, layer, step), 0

    def mark(self, ins):
        ins.then_inc(self.own.sem, 1)
        self.n += 1

    def settle(self):
        self.eng.wait_ge(self.own.sem, self.own.at(*self.where, self.n))

    def link(self, ins):
        self.mark(ins)
        self.settle()

    def settle_for_search(self):
        self.settle()
        self.eng.sem_inc(self.held, 1)

    def end(self):
        want = self.own.per_step.get(self.where[0], 0)
        if want != self.n:
            MISCOUNTED.append((self.own.sem.name, self.where[0], want, self.n))


MISCOUNTED = []

VECTOR_LINKS = {"ada": 1, "norm1": 1, "swa_kv": 4, "swa": 27, "mla_c": 6, "mla": 12, "fox": 8, "gates": 4, "norm2": 1,
                "query": 82, "select": 51}
SCALAR_LINKS = {"norm1": 1, "swa_kv": 1, "swa": 1, "mla_c": 4, "mla": 4, "fox": 2, "norm2": 1}


def build_trunk(nc, x_t, stream, vecs, consts, c_t, tab_u, tab_v, out_t, route_dram, stages=None, layers=LAYERS):
    stages = stages or STAGES
    ctx = ExitStack()
    with ctx:
        def sb(name, shape, dt=F32):
            return ctx.enter_context(nc.sbuf_tensor(name, shape, dt))

        def sem(name):
            return ctx.enter_context(nc.semaphore(name))

        signals = []

        def signal(name, per_step, credit=1):
            signals.append(Signal(sem(name), per_step, credit))
            return signals[-1]

        C = sb("C", [128, CONST_COLS])
        V = sb("V", [128, VEC_COLS])
        ident16 = sb("ident16", [128, 128], BF16)
        masks16 = sb("masks16", [128, 512], BF16)
        xT = sb("xT", [128, KT, T])
        mixT = sb("mixT", [128, KT, T])
        W = sb("W", [128, SLOTS, 1024])
        modT = sb("modT", [128, 6 * KT])
        gain = sb("gain", [128, 2 * KT])
        gq = sb("gq", [128, 3])

        mixer_memory = ExitStack()
        hT = mixer_memory.enter_context(nc.sbuf_tensor("hT", [128, KT, T], F32))
        arena = mixer_memory.enter_context(nc.sbuf_tensor("arena", [128, 22 * 1024], F32))
        at = [0]

        def carve(cols, shape, dt=F32):
            a = arena[:, at[0]:at[0] + cols]
            at[0] += cols
            if dt != F32:
                a = a.bitcast(dt)
            if len(shape) == 1:
                return a
            names = "abcdef"[:len(shape)]
            return a.rearrange(f"p ({' '.join(names)}) -> p {' '.join(names)}",
                               **{k: v for k, v in zip(names[1:], shape[1:])})

        oT = [carve(4 * T, [4, T]) for _ in range(3)]
        sq = carve(2 * T, [2, T])
        rstd = carve(2 * T, [2, T])
        lnv = carve(T, [T])
        qn = carve(2 * T, [2, T])
        rope = carve(2 * T, [2, T])
        q_cur = carve(2 * T, [2, T])
        k_cur = carve(2 * T, [2, T])
        v_cur = carve(T, [TT, 128])
        c_lat = carve(3 * T, [3, T])
        k_rot = carve(T, [T])
        probs = carve(2 * T, [2, T])
        pnorm = carve(2 * T, [2, T])
        probsT = carve(2 * T, [2, T])
        stat = carve(64, [64])
        fgt = carve(4 * T, [4, T])
        fq_head = carve(2 * T, [2, T])
        flat = fgt.rearrange("p a n -> p (a n)")
        c_rows, c_silu = flat[:, 0:D], flat[:, D:2 * D]
        mod_product = fq_head.rearrange("p a n -> p (a n)")
        sig, gated = probs, pnorm
        gate_b = carve(8, [8])
        sinks = carve(2, [2])
        mod_sum = carve(KT, [KT])
        assert at[0] <= 22 * 1024, at[0]

        at[0] = 0
        q_peer = carve(2 * T, [2, T])
        sval_cur = carve(2 * TT * 2 * 16, [2, TT, 2, 16])
        sidx_cur = carve(2 * TT * 2 * 16, [2, TT, 2, 16], U32)
        rest = carve(8 * 128, [8, 128])
        sval = carve(TT * HEADS * 32, [TT, HEADS, 2, 16])
        sidx = carve(TT * HEADS * 32, [TT, HEADS, 2, 16])
        cand = carve(HEADS * 256, [HEADS, 256])
        onehot16 = carve(HEADS * 256, [HEADS * 16, 16])
        top = carve(128, [HEADS, 16])
        pos = carve(128, [HEADS, 16], U32)
        pos_part = carve(2 * 128, [2, 128], U32)
        pos_f = carve(2 * 128, [2, 128])
        pick = carve(3 * 128, [3, 128])
        esum = carve(16, [2, 8])
        pickT = carve(3 * T, [3, T])
        keep = at[0]
        route = [carve(128 * TOKENS, [128, TOKENS]) for _ in range(2)]
        oh_j = carve(4 * 4 * 128, [4, 4, 128])
        oh_i = cand.rearrange("p h (b i) -> p (h b) i", i=128).rearrange("p (b t) i -> p b t i", t=4)
        oh_g = onehot16.rearrange("p n c -> p (n c)").rearrange("p (b t i) -> p b t i", b=4, t=4)
        assert at[0] <= 22 * 1024

        mixer_memory.close()
        h_lo = sb("h_lo", [128, KT, T], F32R)
        h_parts = [sb("h_hi", [128, KT, T], F32R), h_lo]
        u_parts = [sb("u_hi", [128, 2, 1024], F32R), sb("u_lo", [128, 2, 1024], F32R)]
        v_parts = [sb("v_hi", [128, GROUP, 1024], F32R), sb("v_lo", [128, GROUP, 1024], F32R)]
        a_parts = [sb("a_hi", [128, GROUP, T], F32R), sb("a_lo", [128, GROUP, T], F32R)]
        act_out = sb("act_out", [128, GROUP, T])
        g_cur = sb("g_cur", [128, T // TOKENS, GROUP * TOKENS])

        PS = [ctx.enter_context(nc.psum_tensor(f"bank{i}", [128, 512], F32)) for i in range(8)]
        P0, S0, T0, O0, NS = PS[0:2], PS[2:4], PS[4:6], PS[6], PS[7]

        def cst(name):
            a, w = CONST[name]
            return C[:, a:a + w]

        def vec(name):
            a, w = VEC[name]
            return V[:, a:a + w]

        consts_loaded = sem("consts_loaded")
        x_loaded = sem("x_loaded")
        out_stored = sem("out_stored")
        setup_done = sem("setup_done")
        vecs_loaded = sem("vecs_loaded")
        cond_sigmoid = sem("cond_sigmoid")
        cond_ready = sem("cond_ready")
        sum_cleared = sem("sum_cleared")
        tile_loaded = [signal(f"tile_loaded{s}", {n: 16 * k.count(s) for n, (_, k) in TILES.items()}, credit=0)
                       for s in range(SLOTS)]
        tile_used = signal("tile_used", {n: len(k) for n, (_, k) in TILES.items() if n != "dense"}, credit=8)
        boundary = sem("boundary")
        held = sem("held")
        mod_summed = signal("mod_summed", {"ada": KT, "swa": KT})
        squares = signal("squares", {"norm1": KT, "norm2": KT})
        square_sums = signal("square_sums", {"norm1": KT, "norm2": KT})
        stream_rstd = signal("stream_rstd", {"norm1": 1, "norm2": 1})
        stream_scaled = signal("stream_scaled", {"norm1": KT, "norm2": KT})
        tiles_n = {"swa_kv": 2, "swa": 1, "mla_c": 5, "mla": 5, "fox": 3}
        norms_n = {"swa_kv": 1, "swa": 1, "mla_c": 2, "mla": 4, "fox": 2}
        proj_ready = signal("proj_ready", {"mla_c": 1, "mla": 4})
        proj_squared = signal("proj_squared", {"swa_kv": 1, "swa": 1, "mla_c": 3, "mla": 4, "fox": 2})
        proj_sums = signal("proj_sums", norms_n)
        proj_rstd = signal("proj_rstd", norms_n)
        proj_drained = signal("proj_drained", tiles_n)
        rotated = signal("rotated", {"swa_kv": 1, "swa": 1, "mla": 4})
        rotation_read = signal("rotation_read", {"swa_kv": 1, "swa": 1, "mla": 4})
        qk_ready = signal("qk_ready", {"swa": 1, "mla": 4, "swa_kv": 1})
        forget_bias = signal("forget_bias", {"fox": 2})
        U8 = {"swa": 8, "mla": 8, "fox": 8}
        scores_ready = signal("scores_ready", U8)
        max_ready = signal("max_ready", U8)
        probs_ready = signal("probs_ready", U8)
        probs_scaled = signal("probs_scaled", U8)
        probs_turned = signal("probs_turned", U8)
        turned_copied = signal("turned_copied", U8)
        unit_out = signal("unit_out", U8)
        pair_stored = signal("pair_stored", {"swa": 1, "mla": 1, "fox": 1})
        branch_ready = signal("branch_ready", {"gates": 3})
        bias_copied = signal("bias_copied", {"gates": 1})
        gate_open = signal("gate_open", {"gates": 6})
        branch_gated = signal("branch_gated", {"gates": 6})
        mixed = signal("mixed", {"w_out": 4})
        query_copied = signal("query_copied", {"query": 2})
        key_scores = signal("key_scores", {"query": 2})
        key_scores_read = signal("key_scores_read", {"query": 2})
        pick_shifted = signal("pick_shifted", {"select": 1})
        pick_exp = signal("pick_exp", {"select": 1})
        picks_ready = signal("picks_ready", {"select": 3})
        picks_turned = signal("picks_turned", {"select": 1})
        picks_copied = signal("picks_copied", {"select": 1})
        Q = 2 * TOKENS // 4
        onehots_i = signal("onehots_i", {"route": Q})
        onehots_j = signal("onehots_j", {"route": Q})
        onehots_weighted = signal("onehots_weighted", {"route": Q}, credit=4)
        route_product = signal("route_product", {"route": Q})
        route_copied = signal("route_copied", {"route": Q})
        route_stored = [signal(f"route_stored{b}", {"route": 16}, credit=0) for b in range(2)]
        route_free = [signal(f"route_free{b}", {"route": 1}) for b in range(2)]
        route_loaded = signal("route_loaded", {"dense": 16}, credit=0)
        h_hi_done = sem("h_hi_done")
        h_lo_done = sem("h_lo_done")
        u_hi_done = signal("u_hi_done", {"dense": GROUP})
        u_lo_done = signal("u_lo_done", {"dense": GROUP}, credit=GROUP)
        v_hi_done = signal("v_hi_done", {"dense": GROUP})
        v_lo_done = signal("v_lo_done", {"dense": GROUP}, credit=GROUP)
        u_used = signal("u_used", {"dense": GROUP}, credit=GROUP)
        v_used = signal("v_used", {"dense": GROUP}, credit=GROUP)
        gelu_done = signal("gelu_done", {"dense": GROUP}, credit=GROUP)
        weighted = signal("weighted", {"dense": GROUP})
        a_hi_done = signal("a_hi_done", {"dense": GROUP})
        a_lo_done = signal("a_lo_done", {"dense": GROUP}, credit=GROUP)
        y_ready = signal("y_ready", {"dense": KT - 1})
        y_added = signal("y_added", {"dense": KT}, credit=GROUP)
        vector_chain = signal("vector_chain", VECTOR_LINKS)
        scalar_chain = signal("scalar_chain", SCALAR_LINKS)

        def used(stages_):
            return [s for s in STAGES if s in stages_]

        nstage = len(stages)

        def enter(eng, stage, layer):
            eng.wait_ge(boundary, (layer * nstage + stages.index(stage)) * 4 + 1)
            eng.sem_inc(held, 1)

        def leave(eng):
            eng.drain().then_inc(boundary, 1)

        def tile(stage, layer, step, n):
            slots = TILES[stage][1]
            slot, turn = slots[n], slots[:n + 1].count(slots[n])
            loaded = tile_loaded[slot]
            return W[:, slot, :], loaded.sem, loaded.at(stage, layer, step, 16 * turn)

        def earlier(signal, stage, layer, step, n, depth):
            return signal.at(stage, layer, step, max(n - depth + 1, 0))

        def proj_wait(eng, stage, layer, step, n):
            if stage == "mla" and n < 4:
                eng.wait_ge(proj_ready.sem, proj_ready.at(stage, layer, step, n + 1))
            elif stage == "mla_c" and n == 3:
                eng.wait_ge(proj_ready.sem, proj_ready.at(stage, layer, step, 1))
            else:
                t = {"mla": 0, "mla_c": min(n, 3)}.get(stage, n)
                eng.wait_ge(tile_used.sem, tile_used.at(stage, layer, step, t + 1))

        def norms(stage):
            if stage == "swa_kv":
                return [([0], 128, 64, [vec("swa_k")], [k_cur[:, 0, :]], cst("block64"), "a")]
            if stage == "swa":
                return [([0], 128, 64, [gq[:, 0:1]], [q_cur[:, 0, :]], cst("block64"), "a")]
            if stage == "mla_c":
                return [([0, 1], 128, 256, [vec("cq")[:, 0:1], vec("cq")[:, 1:2]],
                         [c_lat[:, 0, :], c_lat[:, 1, :]], cst("ones"), None),
                        ([2], 128, 128, [vec("ckv")], [c_lat[:, 2, :]], cst("ones"), None)]
            if stage == "mla":
                return [([2 * e + k], 96, 96, [(gq[:, 1:2], vec("mla_k"))[k]],
                         [(q_cur, k_cur)[k][:, e, :]], cst("ones"), "b")
                        for e in range(2) for k in range(2)]
            return [([k], 128, 64, [(gq[:, 2:3], vec("fox_k"))[k]], [(q_cur, k_cur)[k][:, 0, :]],
                     cst("block64"), None) for k in range(2)]

        def head(stage, e):
            if stage == "mla":
                return slice(0, 96), q_cur[:, e, :], k_cur[:, e, :]
            return slice(64 * e, 64 * e + 64), q_cur[:, 0, :], k_cur[:, 0, :]

        def key_tiles(stage, i):
            return range(max(i - 1, 0), i + 1) if stage == "swa" else range(i + 1)

        block = ctx.enter_context(nc.Block())

        @block.sync
        def _(sp):
            sp.dma_start(C[:], consts).then_inc(consts_loaded, 16)
            sp.dma_start(xT[:], x_t).then_inc(x_loaded, 16)
            with sp.Fori(0, layers) as layer:
                sp.dma_start(V[:], vecs[layer]).then_inc(vecs_loaded, 16)
                sp.dma_start(c_rows, c_t).then_inc(vecs_loaded, 16)
                tenant = {}
                count = 0
                for stage in [s for s in stages if s in TILES or s == "route"]:
                    if stage == "route":
                        with sp.Fori(0, STEPS["route"]) as step:
                            for b in range(2):
                                sp.wait_ge(route_copied.sem, route_copied.at("route", layer, step, (Q // 2) * (b + 1)))
                                sp.dma_start(route_dram[:, ds(2 * step + b, 1), :].rearrange("p a n -> p (a n)"),
                                             route[b].rearrange("p j t -> p (j t)")
                                             ).then_inc(route_stored[b].sem, 16)
                                sp.wait_ge(route_stored[b].sem, route_stored[b].at("route", layer, step, 16))
                                sp.sem_inc(route_free[b].sem, 1)
                        continue
                    steps, slots = TILES[stage]
                    before = [tenant[s] for s in slots if s in tenant]
                    if before:
                        sp.wait_ge(tile_used.sem, layer * tile_used.per_layer + (max(before) + 1))
                        sp.sem_inc(held, 1)
                    with sp.Fori(0, steps) as step:
                        for n, slot in enumerate(slots):
                            same = [i - len(slots) for i in range(len(slots)) if slots[i] == slot] + \
                                   [i for i in range(n) if slots[i] == slot]
                            if stage == "dense" and n < GROUP:
                                sp.wait_ge(u_lo_done.sem, u_lo_done.at("dense", layer, step, n - 1))
                            elif stage == "dense":
                                sp.wait_ge(v_lo_done.sem, v_lo_done.at("dense", layer, step, n + 1 - 2 * GROUP))
                            elif steps > 1 or same[-1] >= 0:
                                sp.wait_ge(tile_used.sem, tile_used.at(stage, layer, step, same[-1] + 1))
                            if stage == "dense":
                                tab = tab_u if n < GROUP else tab_v
                                src = tab[layer * KEYS + step * GROUP + n % GROUP]
                            else:
                                src = stream[layer * STREAM_TILES + step * len(slots) + (count + n)]
                            sp.dma_start(W[:, slot, :], src).then_inc(tile_loaded[slot].sem, 16)
                            if stage != "dense":
                                tenant[slot] = tile_used.base[stage] + (steps - 1) * len(slots) + n
                    count += steps * len(slots)
                sp.wait_ge(boundary, (layer + 1) * (nstage * 4) + 1)
                sp.sem_inc(held, 1)
            sp.dma_start(out_t, xT[:]).then_inc(out_stored, 16)
            sp.wait_ge(out_stored, 16)

        @block.tensor
        def _(pe):
            mm = nc.tensor.matmul

            def product3(out, w, a, first, last):
                mm(out, w[0], a[0], start=first, stop=False)
                mm(out, w[0], a[1], start=False, stop=False)
                return mm(out, w[1], a[0], start=False, stop=last)

            def load_wait(stage, layer, step, n):
                w, loaded, value = tile(stage, layer, step, n)
                pe.wait_ge(loaded, value)
                return w

            def project(out, w, act, width=128, off=0, pitch=128, kts=KT):
                for k in range(kts):
                    last = mm(out, w[:, k * pitch + off:k * pitch + off + width], act[:, k, :],
                              start=(k == 0), stop=(k == kts - 1))
                return last

            def release(stage, layer, step, m):
                pe.wait_ge(mod_summed.sem, mod_summed.at(stage, layer, step, m + 1))
                pe.sem_inc(tile_used.sem, 1)

            def stream_norm(stage, layer):
                enter(pe, stage, layer)
                for k in range(KT):
                    pe.wait_ge(squares.sem, squares.at(stage, layer, 0, k + 1))
                    mm(NS[:], cst("ones"), sq[:, k % 2, :], start=(k == 0), stop=(k == KT - 1)
                       ).then_inc(square_sums.sem, 1)
                leave(pe)

            def proj_bank(stage, layer, step, n):
                pe.wait_ge(proj_drained.sem, earlier(proj_drained, stage, layer, step, n, 2))
                return P0[n % 2]

            def norm_sums(stage, layer, step, u):
                tiles_, parts, _, _, _, ones, rot = norms(stage)[u]
                first = sum(len(x[0]) for x in norms(stage)[:u])
                for i, n in enumerate(tiles_):
                    pe.wait_ge(proj_squared.sem, proj_squared.at(stage, layer, step, first + i + 1))
                    if i == 0 and rot:
                        pe.wait_ge(rotation_read.sem, rotation_read.at(stage, layer, step, u))
                    elif i == 0:
                        pe.wait_ge(proj_rstd.sem, proj_rstd.at(stage, layer, step, u))
                    last = mm(NS[0:parts, :], ones[0:parts, 0:parts], sq[0:parts, (first + i) % 2, :],
                              start=(i == 0), stop=(i == len(tiles_) - 1))
                last.then_inc(proj_sums.sem, 1)

            def norm_rotate(stage, layer, step, u):
                tiles_, parts, _, _, _, _, rot = norms(stage)[u]
                pe.wait_ge(proj_drained.sem, proj_drained.at(stage, layer, step, tiles_[0] + 1))
                mm(NS[0:parts, :], cst("rot_" + rot)[0:parts, 0:parts], qn[0:parts, u % 2, :],
                   start=True, stop=True).then_inc(rotated.sem, 1)

            def values(stage, layer, step, n, w, act, off, pitch, kts, src=0):
                bank = proj_bank(stage, layer, step, n)
                for t in range(TT):
                    for k in range(kts):
                        last = mm(bank[:, t * 128:(t + 1) * 128], act[:, src + k, t * 128:(t + 1) * 128],
                                  w[:, k * pitch + off:k * pitch + off + 128], start=(k == 0), stop=(k == kts - 1))
                last.then_inc(tile_used.sem, 1)

            def attention(stage, layer, step):
                units = [(e, i) for e in range(2) for i in range(TT)]
                mask = {"swa": "mask_window", "mla": "mask_own_chunks", "fox": "mask_frames"}[stage]
                m0 = {"mask_own_chunks": 0, "mask_window": 128, "mask_frames": 384}[mask]

                def scores(u):
                    e, i = units[u]
                    rows, q, k = head(stage, e)
                    tiles_ = key_tiles(stage, i)
                    width = len(tiles_) * 128
                    pe.wait_ge(probs_ready.sem, earlier(probs_ready, stage, layer, step, u, 2))
                    if stage == "fox" and i == 0:
                        pe.wait_ge(forget_bias.sem, forget_bias.at(stage, layer, step, e + 1))
                    masked = width if stage == "swa" else 128
                    for lo, hi in ((0, width - masked), (width - masked, width)):
                        if lo == hi:
                            continue
                        out = S0[u % 2][:, lo:hi]
                        plain = hi < width
                        last = mm(out, q[rows, i * 128:(i + 1) * 128],
                                  k[rows, tiles_[0] * 128 + lo:tiles_[0] * 128 + hi],
                                  start=True, stop=plain and stage != "fox")
                        if stage == "fox":
                            bias_rows = slice(64 * e, 64 * e + 40)
                            last = mm(out, fq_head[bias_rows, e, i * 128:(i + 1) * 128], cst("fk")[bias_rows, lo:hi],
                                      start=False, stop=plain)
                    mlo = m0 + (256 - width if stage == "swa" else 0)
                    mm(out, ident16[:], masks16[:, mlo:mlo + masked], start=False, stop=True
                       ).then_inc(scores_ready.sem, 1)

                def turn(u):
                    e, i = units[u]
                    n = len(key_tiles(stage, i))
                    pe.wait_ge(probs_scaled.sem, probs_scaled.at(stage, layer, step, u + 1))
                    pe.wait_ge(turned_copied.sem, earlier(turned_copied, stage, layer, step, u, 2))
                    for b in range(n):
                        last = nc.tensor.transpose(T0[u % 2][:, b * 128:(b + 1) * 128],
                                                   pnorm[:, u % 2, b * 128:(b + 1) * 128], cst("ident"))
                    last.then_inc(probs_turned.sem, 1)

                def output(u):
                    e, i = units[u]
                    pe.wait_ge(turned_copied.sem, turned_copied.at(stage, layer, step, u + 1))
                    if u == 0:
                        pe.wait_ge(pair_stored.sem, pair_stored.at(stage, layer, step, 0))
                    tiles_ = list(key_tiles(stage, i))
                    for b, kt in enumerate(tiles_):
                        last = mm(O0[64 * e:64 * e + 64, i * 128:(i + 1) * 128], v_cur[:, kt, 64 * e:64 * e + 64],
                                  probsT[:, u % 2, b * 128:(b + 1) * 128], start=(b == 0), stop=(b == len(tiles_) - 1))
                    last.then_inc(unit_out.sem, 1)

                for u in range(len(units) + 3):
                    if u < len(units):
                        scores(u)
                    if 2 <= u <= len(units) + 1:
                        turn(u - 2)
                        if stage == "swa":
                            release(stage, layer, step, u - 2)
                    if u >= 3:
                        output(u - 3)

            pe.wait_ge(consts_loaded, 16)
            pe.wait_ge(setup_done, 2)
            with pe.Fori(0, layers) as layer:
                if "ada" in stages:
                    enter(pe, "ada", layer)
                    with pe.Fori(0, STEPS["ada"]) as step:
                        for m in range(KT):
                            release("ada", layer, step, m)
                    leave(pe)
                if "norm1" in stages:
                    stream_norm("norm1", layer)
                if "swa_kv" in stages:
                    enter(pe, "swa_kv", layer)
                    w = load_wait("swa_kv", layer, 0, 0)
                    project(proj_bank("swa_kv", layer, 0, 0)[:], w, hT).then_inc(tile_used.sem, 1)
                    w = load_wait("swa_kv", layer, 0, 1)
                    values("swa_kv", layer, 0, 1, w, hT, 0, 128, KT)
                    norm_sums("swa_kv", layer, 0, 0)
                    norm_rotate("swa_kv", layer, 0, 0)
                    leave(pe)
                if "swa" in stages:
                    enter(pe, "swa", layer)
                    with pe.Fori(0, PAIRS) as step:
                        w = load_wait("swa", layer, step, 0)
                        project(proj_bank("swa", layer, step, 0)[:], w, hT).then_inc(tile_used.sem, 1)
                        norm_sums("swa", layer, step, 0)
                        norm_rotate("swa", layer, step, 0)
                        pe.wait_ge(qk_ready.sem, qk_ready.at("swa", layer, step, 1))
                        attention("swa", layer, step)
                    leave(pe)
                if "mla_c" in stages:
                    enter(pe, "mla_c", layer)
                    for n in range(3):
                        w = load_wait("mla_c", layer, 0, n)
                        if n == 2:
                            norm_sums("mla_c", layer, 0, 0)
                        project(proj_bank("mla_c", layer, 0, n)[:], w, hT).then_inc(tile_used.sem, 1)
                    w = load_wait("mla_c", layer, 0, 3)
                    project(proj_bank("mla_c", layer, 0, 3)[64:96, :], w, hT, width=32, pitch=40).then_inc(proj_ready.sem, 1)
                    project(T0[0][0:8, :], w, hT, width=8, off=32, pitch=40).then_inc(tile_used.sem, 1)
                    norm_sums("mla_c", layer, 0, 1)
                    leave(pe)
                if "mla" in stages:
                    enter(pe, "mla", layer)
                    with pe.Fori(0, PAIRS) as step:
                        w = load_wait("mla", layer, step, 0)

                        def up(n):
                            e, k = n // 2, n % 2
                            bank = proj_bank("mla", layer, step, n)
                            if k == 0:
                                project(bank[0:96, :], w, c_lat, width=96, off=96 * e, pitch=192, kts=2
                                        ).then_inc(proj_ready.sem, 1)
                            else:
                                mm(bank[0:64, :], w[:, 384 + 64 * e:448 + 64 * e], c_lat[:, 2, :], start=True, stop=True)
                                mm(bank[64:96, :], cst("ident")[64:96, 64:96], k_rot[64:96, :],
                                   start=True, stop=True, skip_group_check=True).then_inc(proj_ready.sem, 1)

                        up(0)
                        up(1)
                        for u in range(4):
                            norm_sums("mla", layer, step, u)
                            norm_rotate("mla", layer, step, u)
                            if u + 2 < 4:
                                up(u + 2)
                            elif u == 2:
                                values("mla", layer, step, 4, w, c_lat, 512, 0, 1, src=2)
                        pe.wait_ge(qk_ready.sem, qk_ready.at("mla", layer, step, 4))
                        pe.wait_ge(proj_drained.sem, proj_drained.at("mla", layer, step, 5))
                        attention("mla", layer, step)
                    leave(pe)
                if "fox" in stages:
                    enter(pe, "fox", layer)
                    with pe.Fori(0, PAIRS) as step:
                        for n in range(2):
                            w = load_wait("fox", layer, step, n)
                            project(proj_bank("fox", layer, step, n)[:], w, hT).then_inc(tile_used.sem, 1)
                        norm_sums("fox", layer, step, 0)
                        norm_sums("fox", layer, step, 1)
                        w = load_wait("fox", layer, step, 2)
                        values("fox", layer, step, 2, w, hT, 0, 128, KT)
                        pe.wait_ge(proj_drained.sem, proj_drained.at("fox", layer, step, 3))
                        attention("fox", layer, step)
                    leave(pe)
                if "gates" in stages:
                    enter(pe, "gates", layer)
                    with pe.Fori(0, 4) as step:
                        tile_of = [0, 1, 3, 4, 6, 7]
                        wb = {}
                        for g in range(6):
                            i = g % 3
                            w = load_wait("gates", layer, step, tile_of[g])
                            pe.wait_ge(branch_gated.sem, earlier(branch_gated, "gates", layer, step, g, 2))
                            project(PS[g % 2][:], w, hT).then_inc(tile_used.sem, 1)
                            if g % 2 == 0:
                                wb[g // 2] = load_wait("gates", layer, step, 3 * (g // 2) + 2)
                            last = project(PS[2 + g % 2][:], wb[g // 2][:, (g % 2) * 512:(g % 2) * 512 + 512], oT[i], kts=4)
                            last.then_inc((branch_ready if g % 2 == 0 else tile_used).sem, 1)
                    leave(pe)
                if "w_out" in stages:
                    enter(pe, "w_out", layer)
                    with pe.Fori(0, 2) as step:
                        for n in range(4):
                            w = load_wait("w_out", layer, step, n)
                            pe.wait_ge(mixed.sem, earlier(mixed, "w_out", layer, step, n, 4))
                            project(PS[n][:], w, mixT).then_inc(tile_used.sem, 1)
                    leave(pe)
                if "norm2" in stages:
                    stream_norm("norm2", layer)
                if "query" in stages:
                    enter(pe, "query", layer)
                    with pe.Fori(0, 4) as step:
                        for e in range(2):
                            w = load_wait("query", layer, step, e)
                            pe.wait_ge(query_copied.sem, earlier(query_copied, "query", layer, step, e, 2))
                            project(PS[e][:], w, hT).then_inc(tile_used.sem, 1)
                        for e in range(2):
                            pe.wait_ge(query_copied.sem, query_copied.at("query", layer, step, e + 1))
                            pe.wait_ge(key_scores_read.sem, earlier(key_scores_read, "query", layer, step, e, 2))
                            for c in range(2):
                                for t in range(TT):
                                    last = mm(PS[2 + 2 * e + c][:, t * 128:(t + 1) * 128],
                                              q_peer[64 * c:64 * c + 64, e, t * 128:(t + 1) * 128],
                                              vec("keys")[64 * c:64 * c + 64, :], start=True, stop=True)
                            last.then_inc(key_scores.sem, 1)
                    leave(pe)
                if "select" in stages:
                    enter(pe, "select", layer)
                    with pe.Fori(0, TT) as step:
                        pe.wait_ge(picks_copied.sem, picks_copied.at("select", layer, step, 0))
                        pe.wait_ge(picks_ready.sem, picks_ready.at("select", layer, step, 3))
                        for n in range(3):
                            last = nc.tensor.transpose(PS[0][:, n * 128:(n + 1) * 128], pick[:, n, :], cst("ident"))
                        last.then_inc(picks_turned.sem, 1)
                    leave(pe)
                if "route" in stages:
                    enter(pe, "route", layer)
                    with pe.Fori(0, STEPS["route"]) as step:
                        for q in range(Q):
                            pe.wait_ge(onehots_i.sem, onehots_i.at("route", layer, step, q + 1))
                            pe.wait_ge(onehots_weighted.sem, onehots_weighted.at("route", layer, step, q + 1))
                            pe.wait_ge(route_copied.sem, earlier(route_copied, "route", layer, step, q, 8))
                            for t in range(4):
                                last = mm(PS[q % 8][:, t * 128:(t + 1) * 128], oh_i[:, q % 4, t, :], oh_g[:, q % 4, t, :],
                                          start=True, stop=True)
                            last.then_inc(route_product.sem, 1)
                    leave(pe)
                if "dense" in stages:
                    enter(pe, "dense", layer)
                    pe.wait_ge(h_lo_done, (layer + 1) * KT)
                    pe.sem_inc(held, 1)

                    def scores(step, ahead=0):
                        for j in range(GROUP):
                            n = ahead * GROUP + j + 1
                            pe.wait_ge(u_lo_done.sem, u_lo_done.at("dense", layer, step, n))
                            pe.wait_ge(gelu_done.sem, gelu_done.at("dense", layer, step, n - GROUP))
                            for k in range(KT):
                                last = product3(PS[j][:], [u[:, j % 2, k * 128:(k + 1) * 128] for u in u_parts],
                                                [h[:, k, :] for h in h_parts], k == 0, k == KT - 1)
                            last.then_inc(u_used.sem, 1)

                    def outputs(step):
                        for m in range(KT):
                            for j in range(GROUP):
                                if m == 0:
                                    pe.wait_ge(v_lo_done.sem, v_lo_done.at("dense", layer, step, j + 1))
                                    pe.wait_ge(a_lo_done.sem, a_lo_done.at("dense", layer, step, j + 1))
                                if j == 0:
                                    pe.wait_ge(y_added.sem, y_added.at("dense", layer, step, m - 3))
                                last = product3(PS[4 + m % 4][:], [v[:, j, m * 128:(m + 1) * 128] for v in v_parts],
                                                [a[:, j, :] for a in a_parts], j == 0, j == GROUP - 1)
                                if m == KT - 1:
                                    last.then_inc(v_used.sem, 1)
                                elif j == GROUP - 1:
                                    last.then_inc(y_ready.sem, 1)

                    scores(0)
                    with pe.Fori(0, STEPS["dense"] - 1) as step:
                        scores(step, ahead=1)
                        outputs(step)
                    outputs(STEPS["dense"] - 1)
                    leave(pe)
                if "final" in stages:
                    enter(pe, "final", layer)
                    leave(pe)

        @block.scalar
        def _(act):
            chain = Chain(act, scalar_chain)
            fn = nc.scalar.activation

            def stream_norm(stage, layer):
                enter(act, stage, layer)
                chain.begin(stage, layer, 0)
                for k in range(KT):
                    if k >= 2:
                        act.wait_ge(square_sums.sem, square_sums.at(stage, layer, 0, k - 1))
                    fn(sq[:, k % 2, :], xT[:, k, :], ACT.Square).then_inc(squares.sem, 1)
                act.wait_ge(square_sums.sem, square_sums.at(stage, layer, 0, KT))
                chain.link(fn(lnv, NS[:], ACT.Ln, bias=cst("eps"), scale=1.0 / D))
                fn(rstd[:, 0, :], lnv, ACT.Exp, scale=-0.5).then_inc(stream_rstd.sem, 1)
                b = 0 if stage == "norm1" else 3 * KT
                for k in range(KT):
                    act.wait_ge(stream_scaled.sem, stream_scaled.at(stage, layer, 0, k + 1))
                    fn(hT[:, k, :], hT[:, k, :], ACT.Identity, bias=modT[:, b + k:b + k + 1])
                chain.end()
                leave(act)

            def square(stage, layer, step, n, parts, slot):
                proj_wait(act, stage, layer, step, n)
                fn(sq[0:parts, slot % 2, :], P0[n % 2][0:parts, :], ACT.Square).then_inc(proj_squared.sem, 1)

            def norm(stage, layer, step, u):
                tiles_, parts, width, _, _, _, rot = norms(stage)[u]
                first = sum(len(x[0]) for x in norms(stage)[:u])
                for i, n in enumerate(tiles_):
                    square(stage, layer, step, n, parts, first + i)
                act.wait_ge(proj_sums.sem, proj_sums.at(stage, layer, step, u + 1))
                chain.link(fn(lnv[0:parts, :], NS[0:parts, :], ACT.Ln, bias=cst("eps")[0:parts, :], scale=1.0 / width))
                first_of = norms(stage)[u - 2][0][-1] + 1 if u >= 2 else 0
                act.wait_ge(proj_drained.sem, proj_drained.at(stage, layer, step, first_of))
                fn(rstd[0:parts, u % 2, :], lnv[0:parts, :], ACT.Exp, scale=-0.5).then_inc(proj_rstd.sem, 1)

            def attention(stage, layer, step):
                units = [(e, i) for e in range(2) for i in range(TT)]

                def expo(u):
                    e, i = units[u]
                    width = len(key_tiles(stage, i)) * 128
                    act.wait_ge(max_ready.sem, max_ready.at(stage, layer, step, u + 1))
                    nm = stat[:, u:u + 1]
                    if stage == "swa":
                        fn(stat[:, 16 + u:17 + u], sinks[:, e:e + 1], ACT.Exp, bias=nm)
                    fn(probs[:, u % 2, 0:width], S0[u % 2][:, 0:width], ACT.Exp, bias=nm,
                       accum_out=stat[:, 8 + u:9 + u]).then_inc(probs_ready.sem, 1)

                def copy(u):
                    e, i = units[u]
                    width = len(key_tiles(stage, i)) * 128
                    act.wait_ge(probs_turned.sem, probs_turned.at(stage, layer, step, u + 1))
                    act.wait_ge(unit_out.sem, earlier(unit_out, stage, layer, step, u, 2))
                    fn(probsT[:, u % 2, 0:width], T0[u % 2][:, 0:width], ACT.Copy).then_inc(turned_copied.sem, 1)

                for u in range(len(units) + 2):
                    if u < len(units):
                        expo(u)
                    if u >= 2:
                        copy(u - 2)

            act.wait_ge(consts_loaded, 16)
            fn(ident16[:], cst("ident"), ACT.Copy).then_inc(setup_done, 1)
            fn(masks16[:], C[:, CONST["mask_own_chunks"][0]:CONST["mask_own_chunks"][0] + 512], ACT.Copy
               ).then_inc(setup_done, 1)
            act.wait_ge(x_loaded, 16)
            with act.Fori(0, layers) as layer:
                if "ada" in stages:
                    enter(act, "ada", layer)
                    act.wait_ge(vecs_loaded, layer * 32 + 32)
                    fn(c_silu, c_rows, ACT.Sigmoid).then_inc(cond_sigmoid, 1)
                    leave(act)
                if "norm1" in stages:
                    stream_norm("norm1", layer)
                for stage in ("swa_kv", "swa", "mla_c", "mla", "fox"):
                    if stage not in stages:
                        continue
                    enter(act, stage, layer)
                    with act.Fori(0, STEPS[stage]) as step:
                        chain.begin(stage, layer, step)
                        for u in range(len(norms(stage))):
                            norm(stage, layer, step, u)
                        if stage == "mla_c":
                            act.wait_ge(vector_chain.sem, vector_chain.at(stage, layer, 0, 2))
                            chain.link(fn(fgt[0:8, 2, :], fgt[0:8, 1, :], ACT.Exp, scale=-1.0))
                            chain.link(fn(fgt[0:8, 2, :], fgt[0:8, 2, :], ACT.Ln, bias=cst("one")[0:8, :]))
                        chain.end()
                        if stage in U8:
                            attention(stage, layer, step)
                    leave(act)
                if "gates" in stages:
                    enter(act, "gates", layer)
                    with act.Fori(0, 4) as step:
                        act.wait_ge(bias_copied.sem, bias_copied.at("gates", layer, step, 1))
                        for g in range(6):
                            t = [0, 1, 3, 4, 6, 7][g]
                            act.wait_ge(tile_used.sem, tile_used.at("gates", layer, step, t + 1))
                            act.wait_ge(branch_gated.sem, earlier(branch_gated, "gates", layer, step, g, 2))
                            fn(sig[:, g % 2, :], PS[g % 2][:], ACT.Sigmoid, bias=gate_b[:, g:g + 1]).then_inc(gate_open.sem, 1)
                    leave(act)
                if "w_out" in stages:
                    enter(act, "w_out", layer)
                    leave(act)
                if "norm2" in stages:
                    stream_norm("norm2", layer)
                if "query" in stages:
                    enter(act, "query", layer)
                    with act.Fori(0, 4) as step:
                        for e in range(2):
                            act.wait_ge(tile_used.sem, tile_used.at("query", layer, step, e + 1))
                            act.wait_ge(key_scores.sem, earlier(key_scores, "query", layer, step, e, 2))
                            fn(q_peer[:, e, :], PS[e][:], ACT.Copy).then_inc(query_copied.sem, 1)
                    leave(act)
                if "select" in stages:
                    enter(act, "select", layer)
                    with act.Fori(0, TT) as step:
                        act.wait_ge(pick_shifted.sem, pick_shifted.at("select", layer, step, 1))
                        t2 = top.rearrange("p h k -> p (h k)")
                        fn(t2, t2, ACT.Exp).then_inc(pick_exp.sem, 1)
                    leave(act)
                if "route" in stages:
                    enter(act, "route", layer)
                    with act.Fori(0, STEPS["route"]) as step:
                        for q in range(Q):
                            b = q // (Q // 2)
                            act.wait_ge(route_product.sem, route_product.at("route", layer, step, q + 1))
                            if q % (Q // 2) == 0:
                                act.wait_ge(route_free[b].sem, route_free[b].at("route", layer, step, 0))
                            t0 = (q % (Q // 2)) * 4
                            fn(route[b][:, :, t0:t0 + 4], PS[q % 8][:].rearrange("p (t j) -> p j t", t=4), ACT.Copy
                               ).then_inc(route_copied.sem, 1)
                    leave(act)
                if "dense" in stages:
                    enter(act, "dense", layer)
                    for k in range(KT):
                        fn(h_parts[0][:, k, :], hT[:, k, :], ACT.Copy).then_inc(h_hi_done, 1)

                    def lead_u(step, j, ahead=0):
                        raw, loaded, _ = tile("dense", layer, step, j)
                        act.wait_ge(loaded, tile_loaded[TILES["dense"][1][j]].at(
                            "dense", layer, step, 32 * ahead + 16 * (j // 2 + 1)))
                        act.wait_ge(u_used.sem, u_used.at("dense", layer, step, ahead * GROUP + j - 1))
                        fn(u_parts[0][:, j % 2, :], raw, ACT.Copy).then_inc(u_hi_done.sem, 1)

                    def lead_v(step, j):
                        raw, loaded, value = tile("dense", layer, step, GROUP + j)
                        act.wait_ge(loaded, value)
                        act.wait_ge(v_used.sem, v_used.at("dense", layer, step, j + 1 - GROUP))
                        fn(v_parts[0][:, j, :], raw, ACT.Copy).then_inc(v_hi_done.sem, 1)

                    def gelu(step, j, ahead=0):
                        n = ahead * GROUP + j + 1
                        act.wait_ge(u_used.sem, u_used.at("dense", layer, step, n))
                        act.wait_ge(a_lo_done.sem, a_lo_done.at("dense", layer, step, n - GROUP))
                        fn(act_out[:, j, :], PS[j][:], ACT.Gelu).then_inc(gelu_done.sem, 1)

                    def lead_next(step, j, ahead=0):
                        if j < GROUP - 2:
                            lead_u(step, j + 2, ahead)
                        else:
                            lead_u(step, j + 2 - GROUP, ahead + 1)

                    def lead_vs(step, j):
                        if j < GROUP - 1:
                            lead_v(step, j)
                        if j == GROUP - 2:
                            lead_v(step, j + 1)

                    lead_u(0, 0)
                    lead_u(0, 1)
                    for j in range(GROUP):
                        gelu(0, j)
                        lead_next(0, j)
                    with act.Fori(0, STEPS["dense"] - 2) as step:
                        for j in range(GROUP):
                            lead_vs(step, j)
                            gelu(step, j, ahead=1)
                            lead_next(step, j, ahead=1)
                    step = STEPS["dense"] - 2
                    for j in range(GROUP):
                        lead_vs(step, j)
                        gelu(step, j, ahead=1)
                        if j < GROUP - 2:
                            lead_next(step, j, ahead=1)
                    for j in range(GROUP):
                        lead_v(step + 1, j)
                    leave(act)
                if "final" in stages:
                    enter(act, "final", layer)
                    leave(act)

        @block.gpsimd
        def _(pool):
            def load_routes(layer, step):
                pool.wait_ge(weighted.sem, weighted.at("dense", layer, step, 0))
                pool.dma_start(g_cur[:], route_dram[:, :, ds(step * (GROUP * TOKENS), GROUP * TOKENS)]
                               ).then_inc(route_loaded.sem, 16)

            for s in signals:
                if s.credit:
                    pool.sem_inc(s.sem, s.credit)
            pool.sem_inc(boundary, 1)
            with pool.Fori(0, layers) as layer:
                for stage in stages:
                    enter(pool, stage, layer)
                    if stage == "route":
                        with pool.Fori(0, STEPS["route"]) as step:
                            for q in range(Q):
                                pool.wait_ge(onehots_j.sem, onehots_j.at("route", layer, step, q + 1))
                                pool.wait_ge(route_product.sem, earlier(route_product, "route", layer, step, q, 4))
                                g4 = pickT[:, 2, ds(step * (2 * TOKENS) + 4 * q, 4)]
                                nc.gpsimd.tensor_tensor(oh_g[:, q % 4], oh_j[:, q % 4],
                                                        g4.unsqueeze(2).broadcast_to([128, 4, 128]), ALU.mult
                                                        ).then_inc(onehots_weighted.sem, 1)
                    if stage == "dense":
                        with pool.Fori(0, STEPS["dense"]) as step:
                            for j in range(GROUP):
                                pool.wait_ge(u_hi_done.sem, u_hi_done.at("dense", layer, step, j + 1))
                                raw, _, _ = tile("dense", layer, step, j)
                                nc.gpsimd.tensor_tensor(u_parts[1][:, j % 2, :], raw, u_parts[0][:, j % 2, :].bitcast(F32),
                                                        ALU.subtract).then_inc(u_lo_done.sem, 1)
                                if j == 1:
                                    load_routes(layer, step)
                    leave(pool)

        @block.vector
        def _(dve):
            chain = Chain(dve, vector_chain)
            chain.held = held
            stt, tt, ts = nc.vector.scalar_tensor_tensor, nc.vector.tensor_tensor, nc.vector.tensor_scalar

            def modulation(stage, layer, step, n, m):
                w, loaded, value = tile(stage, layer, step, n)
                dve.wait_ge(loaded, value)
                dve.wait_ge(mod_summed.sem, mod_summed.at(stage, layer, step, m))
                stt(mod_product, w, 1.0, c_silu, ALU.mult, ALU.mult, accum_out=mod_sum[:, m:m + 1]
                    ).then_inc(mod_summed.sem, 1)

            def add_bias(stage, layer, step, first):
                dve.wait_ge(mod_summed.sem, mod_summed.at(stage, layer, step, KT))
                chunk = ds((step + first) * KT, KT)
                chain.link(tt(modT[:, chunk], mod_sum, V[:, chunk], ALU.add))

            def stream_norm(stage, layer):
                enter(dve, stage, layer)
                chain.begin(stage, layer, 0)
                n1 = stage == "norm1"
                g = gain[:, 0:KT] if n1 else gain[:, KT:2 * KT]
                sc = modT[:, KT:2 * KT] if n1 else modT[:, 4 * KT:5 * KT]
                chain.link(stt(g, sc, 1.0, vec("norm1" if n1 else "norm2"), ALU.add, ALU.mult))
                dve.wait_ge(stream_rstd.sem, stream_rstd.at(stage, layer, 0, 1))
                for k in range(KT):
                    stt(hT[:, k, :], xT[:, k, :], g[:, k:k + 1], rstd[:, 0, :], ALU.mult, ALU.mult
                        ).then_inc(stream_scaled.sem, 1)
                chain.end()
                leave(dve)

            def norm(stage, layer, step, u):
                tiles_, parts, _, gains, dests, _, rot = norms(stage)[u]
                dve.wait_ge(proj_rstd.sem, proj_rstd.at(stage, layer, step, u + 1))
                for n, g, dst in zip(tiles_, gains, dests):
                    out = qn[0:parts, u % 2, :] if rot else dst[0:parts, :]
                    stt(out, P0[n % 2][0:parts, :], g[0:parts, :], rstd[0:parts, u % 2, :], ALU.mult, ALU.mult
                        ).then_inc(proj_drained.sem, 1)
                if rot:
                    n = tiles_[0]
                    dve.wait_ge(proj_drained.sem, proj_drained.at(stage, layer, step, n + 1))
                    chain.mark(tt(rope[0:parts, 0, :], qn[0:parts, u % 2, :], cst("cos_" + rot)[0:parts, :], ALU.mult))
                    dve.wait_ge(rotated.sem, rotated.at(stage, layer, step, u + 1))
                    tt(rope[0:parts, 1, :], NS[0:parts, :], cst("sin_" + rot)[0:parts, :], ALU.mult
                       ).then_inc(rotation_read.sem, 1)
                    chain.settle()
                    dve.wait_ge(rotation_read.sem, rotation_read.at(stage, layer, step, u + 1))
                    tt(dests[0][0:parts, :], rope[0:parts, 0, :], rope[0:parts, 1, :], ALU.add
                       ).then_inc(qk_ready.sem, 1)

            def copy_values(stage, layer, step, n):
                proj_wait(dve, stage, layer, step, n)
                nc.vector.tensor_copy(v_cur.rearrange("p t c -> p (t c)"), P0[n % 2][:]).then_inc(proj_drained.sem, 1)

            def attention(stage, layer, step, o):
                units = [(e, i) for e in range(2) for i in range(TT)]

                def maxi(u):
                    e, i = units[u]
                    width = len(key_tiles(stage, i)) * 128
                    dve.wait_ge(scores_ready.sem, scores_ready.at(stage, layer, step, u + 1))
                    nm = stat[:, u:u + 1]
                    if stage == "swa":
                        chain.link(nc.vector.tensor_reduce(nm, S0[u % 2][:, 0:width], AX.X, ALU.max))
                        ts(nm, nm, sinks[:, e:e + 1], -1.0, ALU.max, ALU.mult).then_inc(max_ready.sem, 1)
                    else:
                        nc.vector.tensor_reduce(nm, S0[u % 2][:, 0:width], AX.X, ALU.max, negate=True
                                                ).then_inc(max_ready.sem, 1)

                def scale(u):
                    e, i = units[u]
                    width = len(key_tiles(stage, i)) * 128
                    dve.wait_ge(probs_ready.sem, probs_ready.at(stage, layer, step, u + 1))
                    total = stat[:, 8 + u:9 + u]
                    if stage == "swa":
                        chain.link(tt(total, total, stat[:, 16 + u:17 + u], ALU.add))
                    chain.link(nc.vector.reciprocal(stat[:, 24 + u:25 + u], total))
                    dve.wait_ge(probs_turned.sem, earlier(probs_turned, stage, layer, step, u, 2))
                    ts(pnorm[:, u % 2, 0:width], probs[:, u % 2, 0:width], stat[:, 24 + u:25 + u], None, ALU.mult
                       ).then_inc(probs_scaled.sem, 1)

                for u in range(len(units) + 1):
                    if u < len(units):
                        maxi(u)
                        if stage == "swa":
                            modulation(stage, layer, step, 1 + u, u)
                    if u >= 1:
                        scale(u - 1)
                if stage == "swa":
                    add_bias(stage, layer, step, 2)
                dve.wait_ge(unit_out.sem, unit_out.at(stage, layer, step, 8))
                nc.vector.tensor_copy(o[:, ds(step, 1), :].rearrange("p a t -> p (a t)"), O0[:]
                                      ).then_inc(pair_stored.sem, 1)

            dve.wait_ge(consts_loaded, 16)
            dve.wait_ge(x_loaded, 16)
            with dve.Fori(0, layers) as layer:
                if "ada" in stages:
                    enter(dve, "ada", layer)
                    dve.wait_ge(cond_sigmoid, layer + 1)
                    tt(c_silu, c_rows, c_silu, ALU.mult).then_inc(cond_ready, 1)
                    dve.wait_ge(cond_ready, layer + 1)
                    dve.sem_inc(held, 1)
                    with dve.Fori(0, STEPS["ada"]) as step:
                        chain.begin("ada", layer, step)
                        for m in range(KT):
                            modulation("ada", layer, step, m, m)
                        add_bias("ada", layer, step, 0)
                        chain.end()
                    leave(dve)
                if "norm1" in stages:
                    stream_norm("norm1", layer)
                for stage in ("swa_kv", "swa", "mla_c", "mla", "fox"):
                    if stage not in stages:
                        continue
                    enter(dve, stage, layer)
                    with dve.Fori(0, STEPS[stage]) as step:
                        chain.begin(stage, layer, step)
                        if stage == "swa_kv":
                            for n, (name, dim) in enumerate((("swa_q", 64), ("mla_q", 96), ("fox_q", 64))):
                                chain.mark(ts(gq[:, n:n + 1], vec(name), float(dim) ** -0.5, None, ALU.mult))
                            norm(stage, layer, step, 0)
                            copy_values(stage, layer, step, 1)
                        if stage == "swa":
                            chain.link(nc.vector.tensor_copy(sinks, V[:, ds(VEC["sink"][0] + step * 2, 2)]))
                            norm(stage, layer, step, 0)
                            attention(stage, layer, step, oT[0])
                        if stage == "mla_c":
                            norm(stage, layer, step, 0)
                            proj_wait(dve, stage, layer, step, 4)
                            chain.link(ts(fgt[0:8, 0, :], T0[0][0:8, :], vec("b_forget")[0:8, :], None, ALU.add))
                            chain.mark(stt(fgt[0:8, 1, :], fgt[0:8, 0, :], -1.0, fgt[0:8, 0, :], ALU.mult, ALU.max))
                            norm(stage, layer, step, 1)
                            proj_wait(dve, stage, layer, step, 3)
                            nc.vector.tensor_copy(k_rot[64:96, :], P0[1][64:96, :]).then_inc(proj_drained.sem, 1)
                            dve.wait_ge(scalar_chain.sem, scalar_chain.at(stage, layer, 0, SCALAR_LINKS.get("mla_c", 0)))
                            chain.link(stt(fgt[0:8, 3, :], fgt[0:8, 0, :], 0.0, fgt[0:8, 2, :], ALU.min, ALU.subtract))
                            chain.link(nc.vector.tensor_tensor_scan(cst("fq")[0:8, :], cst("fk")[0:8, :], fgt[0:8, 3, :],
                                                                    0.0, ALU.mult, ALU.add))
                            chain.mark(ts(cst("fk")[32:40, :], cst("fq")[0:8, :], -1.0, None, ALU.mult))
                            chain.mark(nc.vector.tensor_copy(cst("fq")[64:72, :], cst("fq")[0:8, :]))
                            ts(cst("fk")[96:104, :], cst("fq")[0:8, :], -1.0, None, ALU.mult).then_inc(proj_drained.sem, 1)
                        if stage == "mla":
                            for u in range(4):
                                norm(stage, layer, step, u)
                            copy_values(stage, layer, step, 4)
                            attention(stage, layer, step, oT[1])
                        if stage == "fox":
                            for e in range(2):
                                r = slice(64 * e, 64 * e + 40)
                                ts(fq_head[r, e, :], cst("fq")[r, :],
                                   C[r, ds(CONST["head_pick"][0] + 2 * step + e, 1)], None, ALU.mult
                                   ).then_inc(forget_bias.sem, 1)
                            norm(stage, layer, step, 0)
                            norm(stage, layer, step, 1)
                            copy_values(stage, layer, step, 2)
                            attention(stage, layer, step, oT[2])
                        chain.end()
                    leave(dve)
                if "gates" in stages:
                    enter(dve, "gates", layer)
                    with dve.Fori(0, 4) as step:
                        chain.begin("gates", layer, step)
                        nc.vector.tensor_copy(gate_b[:, 0:6], V[:, ds(VEC["b_gate"][0] + step * 6, 6)]
                                              ).then_inc(bias_copied.sem, 1)
                        for g in range(6):
                            e, i = g // 3, g % 3
                            dve.wait_ge(gate_open.sem, gate_open.at("gates", layer, step, g + 1))
                            if g % 2 == 0:
                                dve.wait_ge(branch_ready.sem, branch_ready.at("gates", layer, step, g // 2 + 1))
                            else:
                                dve.wait_ge(tile_used.sem, tile_used.at("gates", layer, step, 3 * (g // 2) + 3))
                            tt(gated[:, g % 2, :], sig[:, g % 2, :], PS[2 + g % 2][:], ALU.mult).then_inc(branch_gated.sem, 1)
                            dve.wait_ge(branch_gated.sem, branch_gated.at("gates", layer, step, g + 1))
                            y = mixT[:, ds(2 * step + e, 1), :].rearrange("p a t -> p (a t)")
                            if i == 1:
                                chain.link(tt(gated[:, g % 2, :], gated[:, g % 2, :], gated[:, (g - 1) % 2, :], ALU.add))
                            if i == 2:
                                chain.link(tt(y, gated[:, g % 2, :], gated[:, (g - 1) % 2, :], ALU.add))
                        chain.end()
                    leave(dve)
                if "w_out" in stages:
                    enter(dve, "w_out", layer)
                    with dve.Fori(0, 2) as step:
                        for n in range(4):
                            dve.wait_ge(tile_used.sem, tile_used.at("w_out", layer, step, n + 1))
                            xk = xT[:, ds(step * 4 + n, 1), :].rearrange("p a t -> p (a t)")
                            stt(xk, PS[n][:], modT[:, ds(2 * KT + step * 4 + n, 1)], xk, ALU.mult, ALU.add
                                ).then_inc(mixed.sem, 1)
                    leave(dve)
                if "norm2" in stages:
                    stream_norm("norm2", layer)
                if "query" in stages:
                    enter(dve, "query", layer)
                    with dve.Fori(0, 4) as step:
                        chain.begin("query", layer, step)
                        for e in range(2):
                            cells = [(t, c) for t in range(TT) for c in range(2)]

                            def cell(t, c):
                                return PS[2 + 2 * e + c][:, t * 128:(t + 1) * 128], sval_cur[:, e, t, c, :], sidx_cur[:, e, t, c, :]

                            dve.wait_ge(key_scores.sem, key_scores.at("query", layer, step, e + 1))
                            dve.sem_inc(held, 1)
                            for t, c in cells:
                                s, v, _ = cell(t, c)
                                chain.mark(nc.vector.max(v[:, 0:8], s))
                            chain.settle_for_search()
                            for n, (t, c) in enumerate(cells):
                                s, v, x = cell(t, c)
                                chain.mark(nc.vector.match_replace(rest[:, n, :], v[:, 0:8], s, LOWEST))
                                chain.mark(nc.vector.max_index(x[:, 0:8], v[:, 0:8], s))
                            chain.settle_for_search()
                            for n, (t, c) in enumerate(cells):
                                s, v, x = cell(t, c)
                                chain.mark(nc.vector.max(v[:, 8:16], rest[:, n, :]))
                            chain.settle_for_search()
                            for n, (t, c) in enumerate(cells):
                                s, v, x = cell(t, c)
                                chain.mark(nc.vector.max_index(x[:, 8:16], v[:, 8:16], rest[:, n, :]))
                            chain.settle_for_search()
                            sv = sval.rearrange("p t h c k -> p t h (c k)")[:, :, ds(2 * step + e, 1), :]
                            si = sidx.rearrange("p t h c k -> p t h (c k)")[:, :, ds(2 * step + e, 1), :]
                            chain.mark(nc.vector.tensor_copy(sv.rearrange("p t h n -> p t (h n)"),
                                                             sval_cur[:, e].rearrange("p t c k -> p t (c k)")))
                            nc.vector.tensor_copy(si.rearrange("p t h n -> p t (h n)"),
                                                  sidx_cur[:, e].rearrange("p t c k -> p t (c k)")
                                                  ).then_inc(key_scores_read.sem, 1)
                            dve.wait_ge(key_scores_read.sem, key_scores_read.at("query", layer, step, e + 1))
                            chain.settle_for_search()
                        chain.end()
                    leave(dve)
                if "select" in stages:
                    enter(dve, "select", layer)
                    with dve.Fori(0, TT) as step:
                        chain.begin("select", layer, step)
                        sv = sval[:, ds(step, 1)].rearrange("p a h c k -> p (a h) c k")
                        si = sidx[:, ds(step, 1)].rearrange("p a h c k -> p (a h) c k")
                        chain.link(tt(cand.rearrange("p h (a b) -> p h a b", a=16),
                                      sv[:, :, 0, :].unsqueeze(3).broadcast_to([128, HEADS, 16, 16]),
                                      sv[:, :, 1, :].unsqueeze(2).broadcast_to([128, HEADS, 16, 16]), ALU.add))
                        dve.sem_inc(held, 1)
                        for h in range(HEADS):
                            chain.mark(nc.vector.max(top[:, h, 0:8], cand[:, h, :]))
                        chain.settle_for_search()
                        for h in range(HEADS):
                            chain.mark(nc.vector.max_index(pos[:, h, 0:8], top[:, h, 0:8], cand[:, h, :]))
                        chain.settle_for_search()
                        for h in range(HEADS):
                            chain.mark(nc.vector.match_replace(cand[:, h, :], top[:, h, 0:8], cand[:, h, :], LOWEST))
                        chain.settle_for_search()
                        for h in range(HEADS):
                            chain.mark(nc.vector.max(top[:, h, 8:16], cand[:, h, :]))
                        chain.settle_for_search()
                        for h in range(HEADS):
                            chain.mark(nc.vector.max_index(pos[:, h, 8:16], top[:, h, 8:16], cand[:, h, :]))
                        chain.link(nc.vector.tensor_copy(esum[:, 1, :], top[:, :, 0]))
                        tt(top, top, esum[:, 1, :].unsqueeze(2).broadcast_to([128, HEADS, 16]), ALU.subtract
                           ).then_inc(pick_shifted.sem, 1)
                        p2 = pos.rearrange("p h k -> p (h k)")
                        chain.mark(ts(pos_part[:, 0, :], p2, 4, None, ALU.logical_shift_right))
                        chain.link(ts(pos_part[:, 1, :], p2, 15, None, ALU.bitwise_and))
                        chain.link(nc.vector.tensor_copy(pos_f.rearrange("p a n -> p (a n)"),
                                                         pos_part.rearrange("p a n -> p (a n)")))
                        for half in range(2):
                            chain.link(tt(onehot16, pos_f[:, half, :].unsqueeze(2).broadcast_to([128, 128, 16]),
                                          cst("iota")[:, 0:16].unsqueeze(1).broadcast_to([128, 128, 16]), ALU.is_equal))
                            o4 = onehot16.rearrange("p (h k) c -> p h k c", h=HEADS)
                            chain.link(tt(o4, o4, si[:, :, half, :].unsqueeze(2).broadcast_to([128, HEADS, 16, 16]),
                                          ALU.mult))
                            if half == 0:
                                dve.wait_ge(picks_turned.sem, picks_turned.at("select", layer, step, 0))
                            nc.vector.tensor_reduce(pick[:, half, :], onehot16, AX.X, ALU.add).then_inc(picks_ready.sem, 1)
                            dve.wait_ge(picks_ready.sem, picks_ready.at("select", layer, step, half + 1))
                        dve.wait_ge(pick_exp.sem, pick_exp.at("select", layer, step, 1))
                        chain.link(nc.vector.tensor_reduce(esum[:, 0, :], top, AX.X, ALU.add))
                        chain.link(nc.vector.reciprocal(esum[:, 1, :], esum[:, 0, :]))
                        tt(pick[:, 2, :].rearrange("p (h k) -> p h k", h=HEADS), top,
                           esum[:, 1, :].unsqueeze(2).broadcast_to([128, HEADS, 16]), ALU.mult).then_inc(picks_ready.sem, 1)
                        dve.wait_ge(picks_turned.sem, picks_turned.at("select", layer, step, 1))
                        nc.vector.tensor_copy(pickT[:, :, ds(step * 128, 128)],
                                              PS[0][:, 0:384].rearrange("p (n t) -> p n t", n=3)
                                              ).then_inc(picks_copied.sem, 1)
                        chain.end()
                    leave(dve)
                if "route" in stages:
                    enter(dve, "route", layer)
                    with dve.Fori(0, STEPS["route"]) as step:
                        for q in range(Q):
                            dve.wait_ge(route_product.sem, earlier(route_product, "route", layer, step, q, 4))
                            four = step * (2 * TOKENS) + 4 * q
                            iota4 = cst("iota").unsqueeze(1).broadcast_to([128, 4, 128])
                            tt(oh_i[:, q % 4], pickT[:, 0, ds(four, 4)].unsqueeze(2).broadcast_to([128, 4, 128]), iota4,
                               ALU.is_equal).then_inc(onehots_i.sem, 1)
                            dve.wait_ge(onehots_weighted.sem, onehots_weighted.at("route", layer, step, q - 3))
                            tt(oh_j[:, q % 4], pickT[:, 1, ds(four, 4)].unsqueeze(2).broadcast_to([128, 4, 128]), iota4,
                               ALU.is_equal).then_inc(onehots_j.sem, 1)
                    leave(dve)
                if "dense" in stages:
                    enter(dve, "dense", layer)
                    for k in range(KT):
                        dve.wait_ge(h_hi_done, layer * KT + (k + 1))
                        tt(h_parts[1][:, k, :], hT[:, k, :], h_parts[0][:, k, :].bitcast(F32), ALU.subtract
                           ).then_inc(h_lo_done, 1)
                    nc.vector.memset(mixT[:], 0.0).then_inc(sum_cleared, 1)
                    dve.wait_ge(sum_cleared, layer + 1)
                    dve.sem_inc(held, 1)

                    def weigh(step, j, ahead=0):
                        n = ahead * GROUP + j + 1
                        if j == 0:
                            dve.wait_ge(route_loaded.sem, route_loaded.at("dense", layer, step, 16 * (ahead + 1)))
                        dve.wait_ge(gelu_done.sem, gelu_done.at("dense", layer, step, n))
                        a3 = act_out[:, j, :].rearrange("p (g t) -> p g t", t=TOKENS)
                        tt(a3, a3, g_cur[:, :, j * TOKENS:(j + 1) * TOKENS], ALU.mult).then_inc(weighted.sem, 1)

                    def split(step, j):
                        dve.wait_ge(weighted.sem, weighted.at("dense", layer, step, j + 1))
                        dve.wait_ge(v_used.sem, v_used.at("dense", layer, step, j + 1 - GROUP))
                        nc.vector.tensor_copy(a_parts[0][:, j, :], act_out[:, j, :]).then_inc(a_hi_done.sem, 1)
                        dve.wait_ge(a_hi_done.sem, a_hi_done.at("dense", layer, step, j + 1))
                        tt(a_parts[1][:, j, :], act_out[:, j, :], a_parts[0][:, j, :].bitcast(F32),
                           ALU.subtract).then_inc(a_lo_done.sem, 1)
                        dve.wait_ge(v_hi_done.sem, v_hi_done.at("dense", layer, step, j + 1))
                        raw, _, _ = tile("dense", layer, step, GROUP + j)
                        tt(v_parts[1][:, j, :], raw, v_parts[0][:, j, :].bitcast(F32), ALU.subtract
                           ).then_inc(v_lo_done.sem, 1)

                    def add_up(step):
                        for m in range(KT):
                            if m < KT - 1:
                                dve.wait_ge(y_ready.sem, y_ready.at("dense", layer, step, m + 1))
                            else:
                                dve.wait_ge(v_used.sem, v_used.at("dense", layer, step, GROUP))
                            tt(mixT[:, m, :], mixT[:, m, :], PS[4 + m % 4][:], ALU.add).then_inc(y_added.sem, 1)

                    for j in range(GROUP):
                        weigh(0, j)
                    with dve.Fori(0, STEPS["dense"] - 1) as step:
                        for j in range(GROUP):
                            split(step, j)
                            weigh(step, j, ahead=1)
                        add_up(step)
                    for j in range(GROUP):
                        split(STEPS["dense"] - 1, j)
                    add_up(STEPS["dense"] - 1)
                    leave(dve)
                if "final" in stages:
                    enter(dve, "final", layer)
                    for k in range(KT):
                        stt(xT[:, k, :], mixT[:, k, :], modT[:, 5 * KT + k:5 * KT + k + 1], xT[:, k, :], ALU.mult, ALU.add)
                    leave(dve)
    assert not MISCOUNTED, MISCOUNTED


def lay_constants():
    c = np.zeros((128, CONST_COLS), np.float32)

    def put(name, a):
        a = np.asarray(a, np.float32)
        c[:a.shape[0], CONST[name][0]:CONST[name][0] + a.shape[1]] = a

    put("ident", np.eye(128))
    b = np.zeros((128, 128))
    b[:64, :64] = b[64:, 64:] = 1
    put("block64", b)
    put("ones", np.ones((128, 128)))

    def rotation(size, starts, half):
        r = np.zeros((size, size))
        for s in starts:
            for i in range(half):
                r[s + half + i, s + i] = -1
                r[s + i, s + half + i] = 1
        return r

    put("rot_a", rotation(128, (0, 64), 32))
    put("rot_b", rotation(128, (64,), 16))
    pos = np.arange(T, dtype=np.float32)
    for name, dim, starts in (("a", 64, (0, 64)), ("b", 32, (64,))):
        inv = np.float32(10000.0) ** (-np.arange(0, dim, 2, dtype=np.float32) / np.float32(dim))
        ang = (pos[:, None] * inv[None, :]).astype(np.float32).astype(np.float64)
        cos, sin = np.ones((128, T)), np.zeros((128, T))
        for s in starts:
            for h in range(2):
                cos[s + h * dim // 2:s + (h + 1) * dim // 2] = np.cos(ang).T
                sin[s + h * dim // 2:s + (h + 1) * dim // 2] = np.sin(ang).T
        put("cos_" + name, cos)
        put("sin_" + name, sin)
    q, k = np.arange(128)[:, None], np.arange(256)[None, :]
    put("mask_own_chunks", np.where(k[:, :128] // 64 <= q // 64, 0, NEG))
    qc = q // 64 + 2
    put("mask_window", np.where((k // 64 <= qc) & (k // 64 >= qc - 1), 0, NEG))
    put("mask_frames", np.where(k[:, :128] <= q, 0, NEG))
    put("iota", np.tile(np.arange(128), (128, 1)))
    e = np.zeros((104, 8))
    for r in (0, 32, 64, 96):
        e[r:r + 8] = np.eye(8)
    put("head_pick", e)
    put("eps", np.full((128, 1), EPS))
    put("one", np.ones((128, 1)))
    f = np.zeros((104, T))
    f[32:40] = f[96:104] = 1
    put("fq", f)
    put("fk", f[::-1])
    return c


def tiles_of(w):
    k, n = w.shape[0] // 128, w.shape[1] // 128
    return w.reshape(k, 128, n, 128).transpose(2, 1, 0, 3).reshape(n, 128, k * 128)


def lay_stream(w_ada, w_in, q_up, kv_up, w_branch, w_out, w_q):
    out = []

    def pad(a):
        t = np.zeros((128, 1024), np.float32)
        t[:, :a.shape[1]] = a
        return t

    mod = w_ada.T.reshape(6 * KT, 128, D)
    out += list(mod[:2 * KT])
    cuts = np.cumsum([0, 512, 128, 128, 256, 128, 32, 512, 512, 512, 8, 3 * D])
    aq, ak, av, cq, ckv, kr, fq, fk, fv, ff, gate = [w_in[:, a:b] for a, b in zip(cuts[:-1], cuts[1:])]
    out += [tiles_of(ak)[0], tiles_of(av)[0]]
    for m in range(PAIRS):
        out.append(tiles_of(np.concatenate([aq[:, m * 64:m * 64 + 64], aq[:, (m + 4) * 64:(m + 5) * 64]], 1))[0])
        out += list(mod[(2 + m) * KT:(3 + m) * KT])
    out += list(tiles_of(cq)) + list(tiles_of(ckv))
    misc = np.concatenate([kr, ff], 1)
    out.append(pad(misc.reshape(KT, 128, 40).transpose(1, 0, 2).reshape(128, KT * 40)))
    kv = kv_up.reshape(128, HEADS, 128)
    for m in range(PAIRS):
        q = q_up[:, m * 192:(m + 1) * 192].reshape(2, 128, 192).transpose(1, 0, 2).reshape(128, 384)
        out.append(pad(np.concatenate([q, kv[:, 2 * m, :64], kv[:, 2 * m + 1, :64],
                                       kv[:, 2 * m, 64:], kv[:, 2 * m + 1, 64:]], 1)))
    fq, fk, fv = tiles_of(fq), tiles_of(fk), tiles_of(fv)
    for m in range(PAIRS):
        out += [fq[m], fk[m], fv[m]]
    gates = tiles_of(gate)
    order = np.concatenate([np.r_[m * 64:m * 64 + 64, (m + 4) * 64:(m + 5) * 64] for m in range(PAIRS)])
    br = [tiles_of(w_branch[0][order]), tiles_of(w_branch[1]), tiles_of(w_branch[2])]
    for m in range(0, KT, 2):
        for a in range(3):
            pairs = [((2 * a + b) // 3 + m, (2 * a + b) % 3) for b in range(2)]
            out += [gates[i * KT + mm] for mm, i in pairs]
            out.append(np.concatenate([br[i][mm] for mm, i in pairs], 1))
    out += list(tiles_of(w_out)) + list(tiles_of(w_q))
    return out


def lay_vectors(b_ada, n1, n2, b_gate, b_forget, sink, aq, ak, cq, ckv, bq, bk, fq, fk, keys):
    v = np.zeros((128, VEC_COLS), np.float32)

    def put(name, a):
        v[:a.shape[0], VEC[name][0]:VEC[name][0] + a.shape[1]] = a

    put("b_ada", b_ada.reshape(48, 128).T)
    put("norm1", n1.reshape(KT, 128).T)
    put("norm2", n2.reshape(KT, 128).T)
    put("b_gate", b_gate.reshape(3, KT, 128).transpose(2, 1, 0).reshape(128, 24))
    put("sink", np.tile(sink.reshape(2, 4).T.reshape(1, 8), (128, 1)))
    put("swa_q", np.tile(aq, 2)[:, None])
    put("swa_k", np.tile(ak, 2)[:, None])
    put("cq", cq.reshape(2, 128).T)
    put("ckv", ckv[:, None])
    put("mla_q", bq[:, None])
    put("mla_k", bk[:, None])
    put("fox_q", np.tile(fq, 2)[:, None])
    put("fox_k", np.tile(fk, 2)[:, None])
    put("b_forget", b_forget[:, None])
    put("keys", keys.transpose(0, 2, 1).reshape(128, 128))
    return v


def kernel(**inputs):
    import concourse.bacc as bacc
    from concourse.bass_utils import run_bass_kernel_spmd as run

    arrays = lay_inputs(inputs)
    nc = bacc.Bacc("TRN2", target_bir_lowering=False, num_devices=1)
    build(nc, arrays)
    r = run(nc, [arrays], core_ids=[0])
    y = r.results[0]["out_t"]
    return np.ascontiguousarray(y.transpose(2, 1, 0)).reshape(1, T, D)


def lay_inputs(inputs):
    a = {k: np.asarray(v) for k, v in inputs.items()}
    L = LAYERS
    stream = np.stack([t for l in range(L) for t in lay_stream(
        a["w_ada"][l], a["w_in"][l], a["mla_w_q_up"][l], a["mla_w_kv_up"][l], a["w_branch"][l],
        a["w_out"][l], a["peer_w_q"][l])])
    vecs = np.stack([lay_vectors(a["b_ada"][l], a["norm1_g"][l], a["norm2_g"][l], a["b_gate"][l],
                                 a["b_forget"][l], a["swa_sink"][l], a["swa_qnorm"][l], a["swa_knorm"][l],
                                 a["mla_q_norm"][l], a["mla_kv_norm"][l], a["mla_qnorm"][l], a["mla_knorm"][l],
                                 a["fox_qnorm"][l], a["fox_knorm"][l], a["peer_sub_keys"][l]) for l in range(L)])
    u = a["peer_u"].reshape(L, KEYS, KEYS, KT, 128).transpose(0, 2, 4, 3, 1)
    v = a["peer_v"].reshape(L, KEYS, KEYS, D).transpose(0, 2, 1, 3)
    return {
        "x_t": np.ascontiguousarray(a["x"][0].reshape(T, KT, 128).transpose(2, 1, 0)),
        "stream": np.ascontiguousarray(stream),
        "vecs": vecs,
        "c_rows": np.ascontiguousarray(np.broadcast_to(a["c"][0], (128, D))),
        "consts": lay_constants(),
        "tab_u": np.ascontiguousarray(u).reshape(L * KEYS, 128, D),
        "tab_v": np.ascontiguousarray(v).reshape(L * KEYS, 128, D),
    }


def build(nc, arrays, **options):
    args = {n: nc.dram_tensor(n, a.shape, mybir.dt.from_np(a.dtype), kind="ExternalInput").ap()
            for n, a in arrays.items()}
    out_t = nc.dram_tensor("out_t", (128, KT, T), F32, kind="ExternalOutput").ap()
    route = nc.dram_tensor("route_scratch", (128, T // TOKENS, 128 * TOKENS), F32, kind="Internal").ap()
    build_trunk(nc, args["x_t"], args["stream"], args["vecs"], args["consts"], args["c_rows"], args["tab_u"], args["tab_v"],
                out_t, route, **options)
```

```python
from contextlib import ExitStack

import numpy as np

import concourse.bass as bass
from concourse import mybir

F32 = mybir.dt.float32
F32R = mybir.dt.float32r
BF16 = mybir.dt.bfloat16
U32 = mybir.dt.uint32
ALU = mybir.AluOpType
ACT = mybir.ActivationFunctionType
AX = mybir.AxisListType
ds = bass.ds

LAYERS = 2
D = 1024
T = 512
KT = D // 128
TT = T // 128
HEADS = 8
PAIRS = HEADS // 2
EPS = 1e-6
NEG = -1e30
LOWEST = -3.0e38
PICKS = 16
KEYS = 128
GROUP = 4
TOKENS = 32

SLOTS = 6


def ring(first, n):
    return [(first + i) % SLOTS for i in range(n)]


EARLY = 28
EXP_AFTER = 3

EARLY_BUFFER = [0, 1, 2, 0, 1, 0, 2]
assert len(EARLY_BUFFER) == EARLY // TT

TILES = {
    "ada": (2, ring(0, KT)),
    "swa_kv": (1, ring(2, 3)),
    "swa": (PAIRS, ring(5, 1 + KT)),
    "mla_c": (1, ring(2, 4)),
    "mla": (PAIRS, ring(0, 1)),
    "fox": (PAIRS, ring(4, 3)),
    "gates": (4, ring(1, 9)),
    "w_out": (2, ring(4, 4)),
    "query": (4, ring(2, 2)),
    "select": (TT, [0, 1, 2, 3, 4, 5, 2]),
    "early": (EARLY // GROUP, [0, 1, 2, 3]),
    "dense": ((KEYS - EARLY) // GROUP, [4, 5, 4, 5, 0, 1, 2, 3]),
}
STAGES = ["ada", "norm1", "swa_kv", "swa", "mla_c", "mla", "fox", "gates", "w_out",
          "norm2", "query", "select", "route", "early", "dense", "final"]
STEPS = {"ada": 2, "norm1": 1, "swa_kv": 1, "swa": PAIRS, "mla_c": 1, "mla": PAIRS, "fox": PAIRS,
         "gates": 4, "w_out": 2, "norm2": 1, "query": 4, "select": TT, "route": T // (2 * TOKENS),
         "early": EARLY // GROUP, "dense": (KEYS - EARLY) // GROUP, "final": 1}
EXPERT_STAGES = ("select", "early", "dense")
STREAM_TILES = sum(s * len(k) for n, (s, k) in TILES.items() if n not in EXPERT_STAGES)

CONST = {}
_n = 0
for _name, _w in (("ident", 128), ("block64", 128), ("ones", 128), ("rot_a", 128), ("rot_b", 128),
                  ("cos_a", T), ("sin_a", T), ("cos_b", T), ("sin_b", T),
                  ("mask_own_chunks", 128), ("mask_window", 256), ("mask_frames", 128),
                  ("iota", 128), ("head_pick", 8), ("eps", 1), ("one", 1), ("zero", 1), ("fq", T), ("fk", T)):
    CONST[_name] = (_n, _w)
    _n += _w
CONST_COLS = _n
VEC = {}
_n = 0
for _name, _w in (("b_ada", 48), ("norm1", 8), ("norm2", 8), ("b_gate", 24), ("sink", 8), ("swa_q", 1), ("swa_k", 1),
                  ("cq", 2), ("ckv", 1), ("mla_q", 1), ("mla_k", 1), ("fox_q", 1), ("fox_k", 1),
                  ("b_forget", 1), ("keys", 128)):
    VEC[_name] = (_n, _w)
    _n += _w
VEC_COLS = _n


class Signal:

    def __init__(self, sem, per_step, credit=8):
        self.sem = sem
        self.per_step = per_step
        self.credit = credit
        self.base, n = {}, credit
        for stage in STAGES:
            self.base[stage] = n
            n += STEPS[stage] * per_step.get(stage, 0)
        self.per_layer = n - credit

    def at(self, stage, layer, step, n):
        return layer * self.per_layer + step * self.per_step.get(stage, 0) + (self.base[stage] + n)


class Chain:

    def __init__(self, eng, own):
        self.eng, self.own = eng, own

    def begin(self, stage, layer, step, start=0):
        self.where, self.n, self.start = (stage, layer, step), start, start

    def mark(self, ins):
        ins.then_inc(self.own.sem, 1)
        self.n += 1

    def settle(self):
        self.eng.wait_ge(self.own.sem, self.own.at(*self.where, self.n))

    def link(self, ins):
        self.mark(ins)
        self.settle()

    def settle_for_search(self):
        self.settle()
        self.eng.sem_inc(self.held, 1)

    def end(self, without=0):
        want = self.own.per_step.get(self.where[0], 0) - without
        if want != self.n - self.start:
            MISCOUNTED.append((self.own.sem.name, self.where[0], want, self.n - self.start))


MISCOUNTED = []

VECTOR_LINKS = {"ada": 1, "norm1": 1, "swa_kv": 4, "swa": 27, "mla_c": 6, "mla": 12, "fox": 8, "gates": 4, "norm2": 1,
                "query": 82, "select": 51}
PREPARE_LINKS = {"swa": 2, "mla": 4, "fox": 0}
SCALAR_LINKS = {"norm1": 1, "mla_c": 2, "norm2": 1}


def build_trunk(nc, x_t, stream, vecs, consts, c_t, tab_u, tab_v, out_t, route_dram, early_dram, stages=None, layers=LAYERS):
    stages = stages or [s for s in STAGES if s != "early"]
    ctx = ExitStack()
    with ctx:
        def sb(name, shape, dt=F32):
            return ctx.enter_context(nc.sbuf_tensor(name, shape, dt))

        def sem(name):
            return ctx.enter_context(nc.semaphore(name))

        signals = []

        def signal(name, per_step, credit=8):
            signals.append(Signal(sem(name), per_step, credit))
            return signals[-1]

        C = sb("C", [128, CONST_COLS])
        V = sb("V", [128, VEC_COLS])
        ident16 = sb("ident16", [128, 128], BF16)
        masks16 = sb("masks16", [128, 512], BF16)
        xT = sb("xT", [128, KT, T])
        W = sb("W", [128, SLOTS, 1024])
        modT = sb("modT", [128, 6 * KT])
        gain = sb("gain", [128, 2 * KT])
        spare = sb("spare", [128, 2, 16])
        gq = sb("gq", [128, 3])

        mixer_memory = ExitStack()
        hT = mixer_memory.enter_context(nc.sbuf_tensor("hT", [128, KT, T], F32))
        mixT = mixer_memory.enter_context(nc.sbuf_tensor("mixT", [128, KT, T], F32))
        arena = mixer_memory.enter_context(nc.sbuf_tensor("arena", [128, 22 * 1024], F32))
        at = [0]

        def carve(cols, shape, dt=F32):
            a = arena[:, at[0]:at[0] + cols]
            at[0] += cols
            if dt != F32:
                a = a.bitcast(dt)
            if len(shape) == 1:
                return a
            names = "abcdef"[:len(shape)]
            return a.rearrange(f"p ({' '.join(names)}) -> p {' '.join(names)}",
                               **{k: v for k, v in zip(names[1:], shape[1:])})

        oT = [carve(4 * T, [4, T]) for _ in range(3)]
        sq = carve(2 * T, [2, T])
        rstd = carve(2 * T, [2, T])
        lnv = carve(2 * T, [2, T])
        qn = carve(2 * T, [2, T])
        rope = carve(2 * T, [2, T])
        q_cur = carve(2 * T, [2, T])
        k_cur = carve(2 * T, [2, T])
        v_cur = carve(T, [TT, 128])
        c_lat = carve(3 * T, [3, T])
        k_rot = carve(T, [T])
        probs = carve(2 * T, [2, T])
        pnorm = carve(2 * T, [2, T])
        probsT = carve(2 * T, [2, T])
        stat = carve(64, [64])
        fgt = carve(4 * T, [4, T])
        fq_head = carve(2 * T, [2, T])
        flat = fgt.rearrange("p a n -> p (a n)")
        c_rows, c_silu = flat[:, 0:D], flat[:, D:2 * D]
        mod_product = fq_head.rearrange("p a n -> p (a n)")
        sig, gated = probs, pnorm
        q_next = {"swa": oT[2][:, 0:1, :], "mla": oT[2][:, 0:2, :], "fox": c_lat[:, 0:1, :]}
        k_next = {"mla": oT[2][:, 2:4, :], "fox": c_lat[:, 1:2, :]}
        v_next = {"mla": fq_head[:, 0, :], "fox": c_lat[:, 2, :]}
        gate_b = carve(8, [8])
        sinks = carve(2, [2])
        mod_sum = carve(KT, [KT])
        assert at[0] <= 22 * 1024, at[0]

        at[0] = 0
        q_peer = carve(2 * T, [2, T])
        sval_cur = carve(2 * TT * 2 * 16, [2, TT, 2, 16])
        sidx_cur = carve(2 * TT * 2 * 16, [2, TT, 2, 16], U32)
        rest = carve(8 * 128, [8, 128])
        sval = carve(TT * HEADS * 32, [TT, HEADS, 2, 16])
        sidx = carve(TT * HEADS * 32, [TT, HEADS, 2, 16])
        cand = carve(HEADS * 256, [HEADS, 256])
        onehot16 = carve(HEADS * 256, [HEADS * 16, 16])
        top = carve(128, [HEADS, 16])
        pos = carve(128, [HEADS, 16], U32)
        pos_part = carve(2 * 128, [2, 128], U32)
        pos_f = carve(2 * 128, [2, 128])
        pick = carve(3 * 128, [3, 128])
        esum = carve(16, [2, 8])
        pickT = carve(3 * T, [3, T])
        keep = at[0]
        route = [carve(128 * TOKENS, [128, TOKENS]) for _ in range(2)]
        oh_j = carve(4 * 4 * 128, [4, 4, 128])
        oh_i = cand.rearrange("p h (b i) -> p (h b) i", i=128).rearrange("p (b t) i -> p b t i", t=4)
        oh_g = onehot16.rearrange("p n c -> p (n c)").rearrange("p (b t i) -> p b t i", b=4, t=4)
        assert at[0] <= 22 * 1024

        mixer_memory.close()
        gates_memory = ExitStack()

        def gates_sb(name, shape, dt=F32R):
            return gates_memory.enter_context(nc.sbuf_tensor(name, shape, dt))

        gate_h = [gates_sb("gate_h_lo", [128, KT, T])]
        gates_sb("mix_and_branches", [128, (KT + 3 * 4) * T], F32)
        gate_h.insert(0, gates_sb("gate_h_hi", [128, KT, T]))
        gate_w = [gates_sb("gate_w_hi", [128, 2, 1024]), gates_sb("gate_w_lo", [128, 2, 1024])]
        gates_memory.close()

        h_lo = sb("h_lo", [128, KT, T], F32R)
        h_parts = [sb("h_hi", [128, KT, T], F32R), h_lo]
        early_memory = ExitStack()

        def early_sb(name, shape, dt):
            return early_memory.enter_context(nc.sbuf_tensor(name, shape, dt))

        early_sb("selection", [128, keep], F32)
        early_u = [early_sb("early_u_hi", [128, 3, 1024], F32R), early_sb("early_u_lo", [128, 3, 1024], F32R)]
        early_act = early_sb("early_act", [128, EARLY // TT, T], F32)
        early_memory.close()
        act_out = sb("act_out", [128, GROUP, T])
        u_parts = [sb("u_hi", [128, 2, 1024], F32R), sb("u_lo", [128, 2, 1024], F32R)]
        v_parts = [sb("v_hi", [128, GROUP, 1024], F32R), sb("v_lo", [128, GROUP, 1024], F32R)]
        a_parts = [sb("a_hi", [128, GROUP, T], F32R), sb("a_lo", [128, GROUP, T], F32R)]
        g_cur = sb("g_cur", [128, T // TOKENS, GROUP * TOKENS])
        y_sum = sb("y_sum", [128, KT, T])

        PS = [ctx.enter_context(nc.psum_tensor(f"bank{i}", [128, 512], F32)) for i in range(8)]
        P0, S0, T0, O0, NS = PS[0:2], PS[2:4], PS[4:6], PS[6], PS[7]

        def cst(name):
            a, w = CONST[name]
            return C[:, a:a + w]

        def vec(name):
            a, w = VEC[name]
            return V[:, a:a + w]

        consts_loaded = sem("consts_loaded")
        x_loaded = sem("x_loaded")
        out_stored = sem("out_stored")
        setup_done = sem("setup_done")
        vecs_loaded = sem("vecs_loaded")
        cond_sigmoid = sem("cond_sigmoid")
        cond_ready = sem("cond_ready")
        tile_loaded = [signal(f"tile_loaded{s}", {n: 16 * k.count(s) for n, (_, k) in TILES.items()}, credit=0)
                       for s in range(SLOTS)]
        tile_used = signal("tile_used", {n: len(k) for n, (_, k) in TILES.items() if n not in ("early", "dense")}, credit=8)
        boundary = sem("boundary")
        held = sem("held")
        mod_summed = signal("mod_summed", {"ada": KT, "swa": KT})
        squares = signal("squares", {"norm1": KT, "norm2": KT})
        square_sums = signal("square_sums", {"norm1": KT, "norm2": KT})
        stream_rstd = signal("stream_rstd", {"norm1": 1, "norm2": 1})
        stream_scaled = signal("stream_scaled", {"norm1": KT, "norm2": KT})
        tiles_n = {"swa_kv": 2, "swa": 1, "mla_c": 5, "mla": 5, "fox": 3}
        norms_n = {"swa_kv": 1, "swa": 1, "mla_c": 2, "mla": 4, "fox": 2}
        proj_ready = signal("proj_ready", {"mla_c": 1, "mla": 4, "swa": 1})
        proj_squared = signal("proj_squared", {"swa_kv": 1, "swa": 1, "mla_c": 3, "mla": 4, "fox": 2})
        proj_sums = signal("proj_sums", norms_n)
        sums_read = signal("sums_read", norms_n)
        proj_rstd = signal("proj_rstd", norms_n)
        proj_drained = signal("proj_drained", tiles_n)
        rotated = signal("rotated", {"swa_kv": 1, "swa": 1, "mla": 4})
        rotation_read = signal("rotation_read", {"swa_kv": 1, "swa": 1, "mla": 4})
        qk_ready = signal("qk_ready", {"swa": 1, "mla": 4, "swa_kv": 1})
        operands_installed = signal("operands_installed", {"swa": 1, "mla": 1, "fox": 1})
        values_installed = signal("values_installed", {"mla": 1, "fox": 1})
        U8 = {"swa": 8, "mla": 8, "fox": 8}
        scores_ready = signal("scores_ready", U8)
        max_ready = signal("max_ready", U8)
        probs_ready = signal("probs_ready", U8)
        probs_scaled = signal("probs_scaled", U8)
        probs_turned = signal("probs_turned", U8)
        turned_copied = signal("turned_copied", U8)
        unit_out = signal("unit_out", U8)
        pair_stored = signal("pair_stored", {"swa": 1, "mla": 1, "fox": 1})
        branch_ready = signal("branch_ready", {"gates": 3})
        bias_copied = signal("bias_copied", {"gates": 1})
        gate_h_hi_done = sem("gate_h_hi_done")
        gate_h_lo_done = sem("gate_h_lo_done")
        gate_hi_done = signal("gate_hi_done", {"gates": 6})
        gate_lo_done = signal("gate_lo_done", {"gates": 6})
        gate_open = signal("gate_open", {"gates": 6})
        branch_gated = signal("branch_gated", {"gates": 6})
        mixed = signal("mixed", {"w_out": 4})
        query_copied = signal("query_copied", {"query": 2})
        key_scores = signal("key_scores", {"query": 2})
        key_scores_read = signal("key_scores_read", {"query": 2})
        pick_shifted = signal("pick_shifted", {"select": 1})
        pick_exp = signal("pick_exp", {"select": 1})
        picks_ready = signal("picks_ready", {"select": 3})
        picks_turned = signal("picks_turned", {"select": 1})
        picks_copied = signal("picks_copied", {"select": 1})
        Q = 2 * TOKENS // 4
        onehots_i = signal("onehots_i", {"route": Q})
        onehots_j = signal("onehots_j", {"route": Q})
        onehots_weighted = signal("onehots_weighted", {"route": Q}, credit=4)
        route_product = signal("route_product", {"route": Q})
        route_copied = signal("route_copied", {"route": Q})
        route_stored = [signal(f"route_stored{b}", {"route": 16}, credit=0) for b in range(2)]
        route_free = [signal(f"route_free{b}", {"route": 1}) for b in range(2)]
        route_loaded = signal("route_loaded", {"early": 16, "dense": 16}, credit=0)
        early_hi_done = signal("early_hi_done", {"select": EARLY // TT})
        early_lo_done = signal("early_lo_done", {"select": EARLY // TT})
        early_gelu = signal("early_gelu", {"select": EARLY // TT})
        early_stored = [Signal(sem(f"early_stored{b}"), {"select": 16}, credit=16) for b in range(2)]
        early_loaded = signal("early_loaded", {"early": 16}, credit=0)
        early_added = sem("early_added")
        h_hi_done = sem("h_hi_done")
        h_lo_done = sem("h_lo_done")
        u_hi_done = signal("u_hi_done", {"dense": GROUP})
        u_lo_done = signal("u_lo_done", {"dense": GROUP}, credit=GROUP)
        v_hi_done = signal("v_hi_done", {"early": GROUP, "dense": GROUP})
        v_lo_done = signal("v_lo_done", {"early": GROUP, "dense": GROUP}, credit=GROUP)
        u_used = signal("u_used", {"dense": GROUP}, credit=GROUP)
        v_used = signal("v_used", {"early": GROUP, "dense": GROUP}, credit=GROUP)
        gelu_done = signal("gelu_done", {"dense": GROUP}, credit=GROUP)
        weighted = signal("weighted", {"early": GROUP, "dense": GROUP})
        a_hi_done = signal("a_hi_done", {"early": GROUP, "dense": GROUP})
        a_lo_done = signal("a_lo_done", {"early": GROUP, "dense": GROUP}, credit=GROUP)
        y_ready = signal("y_ready", {"dense": KT - 1})
        y_added = signal("y_added", {"dense": KT}, credit=GROUP)
        vector_chain = signal("vector_chain", VECTOR_LINKS)
        scalar_chain = signal("scalar_chain", SCALAR_LINKS)

        nstage = len(stages)
        GATE_TILES = [0, 1, 3, 4, 6, 7]

        def enter(eng, stage, layer):
            eng.wait_ge(boundary, (layer * nstage + stages.index(stage)) * 4 + 1)
            eng.sem_inc(held, 1)

        def leave(eng):
            eng.drain().then_inc(boundary, 1)

        def tile(stage, layer, step, n):
            slots = TILES[stage][1]
            slot, turn = slots[n], slots[:n + 1].count(slots[n])
            loaded = tile_loaded[slot]
            return W[:, slot, :], loaded.sem, loaded.at(stage, layer, step, 16 * turn)

        def earlier(signal, stage, layer, step, n, depth):
            n = n - depth + 1
            if signal.per_step[stage] % depth:
                n = max(n, 0)
            return signal.at(stage, layer, step, n)

        def proj_wait(eng, stage, layer, step, n):
            if stage == "swa" or stage == "mla" and n < 4:
                eng.wait_ge(proj_ready.sem, proj_ready.at(stage, layer, step, n + 1))
            elif stage == "mla_c" and n == 3:
                eng.wait_ge(proj_ready.sem, proj_ready.at(stage, layer, step, 1))
            else:
                t = {"mla": 0, "mla_c": min(n, 3)}.get(stage, n)
                eng.wait_ge(tile_used.sem, tile_used.at(stage, layer, step, t + 1))

        def norms(stage):
            if stage == "swa_kv":
                return [([0], 128, 64, [vec("swa_k")], [k_cur[:, 0, :]], cst("block64"), "a")]
            if stage == "swa":
                return [([0], 128, 64, [gq[:, 0:1]], [q_next["swa"][:, 0, :]], cst("block64"), "a")]
            if stage == "mla_c":
                return [([0, 1], 128, 256, [vec("cq")[:, 0:1], vec("cq")[:, 1:2]],
                         [c_lat[:, 0, :], c_lat[:, 1, :]], cst("ones"), None),
                        ([2], 128, 128, [vec("ckv")], [c_lat[:, 2, :]], cst("ones"), None)]
            if stage == "mla":
                return [([2 * e + k], 96, 96, [(gq[:, 1:2], vec("mla_k"))[k]],
                         [(q_next, k_next)[k]["mla"][:, e, :]], cst("ones"), "b")
                        for e in range(2) for k in range(2)]
            return [([k], 128, 64, [(gq[:, 2:3], vec("fox_k"))[k]], [(q_next, k_next)[k]["fox"][:, 0, :]],
                     cst("block64"), None) for k in range(2)]

        def head(stage, e):
            if stage == "mla":
                return slice(0, 96), q_cur[:, e, :], k_cur[:, e, :]
            return slice(64 * e, 64 * e + 64), q_cur[:, 0, :], k_cur[:, 0, :]

        def key_tiles(stage, i):
            return range(max(i - 1, 0), i + 1) if stage == "swa" else range(i + 1)

        block = ctx.enter_context(nc.Block())

        @block.sync
        def _(sp):
            sp.dma_start(C[:], consts).then_inc(consts_loaded, 16)
            sp.dma_start(xT[:], x_t).then_inc(x_loaded, 16)
            for b in range(2):
                sp.dma_start(spare[:, b, :], consts[:, 0:16]).then_inc(early_stored[b].sem, 16)
            with sp.Fori(0, layers) as layer:
                sp.dma_start(V[:], vecs[layer]).then_inc(vecs_loaded, 16)
                sp.dma_start(c_rows, c_t).then_inc(vecs_loaded, 16)
                tenant = {}
                count = 0
                for stage in [s for s in STAGES if (s in stages or s == "early" and "dense" in stages)
                              and (s in TILES or s == "route")]:
                    if stage == "route":
                        with sp.Fori(0, STEPS["route"]) as step:
                            for b in range(2):
                                sp.wait_ge(route_copied.sem, route_copied.at("route", layer, step, (Q // 2) * (b + 1)))
                                sp.dma_start(route_dram[:, ds(2 * step + b, 1), :].rearrange("p a n -> p (a n)"),
                                             route[b].rearrange("p j t -> p (j t)")
                                             ).then_inc(route_stored[b].sem, 16)
                                sp.wait_ge(route_stored[b].sem, route_stored[b].at("route", layer, step, 16))
                                sp.sem_inc(route_free[b].sem, 1)
                        continue
                    steps, slots = TILES[stage]
                    before = [tenant[s] for s in slots if s in tenant]
                    if before:
                        sp.wait_ge(tile_used.sem, layer * tile_used.per_layer + (max(before) + 1))
                        sp.sem_inc(held, 1)
                    with sp.Fori(0, steps) as step:
                        for n, slot in enumerate(slots):
                            same = [i - len(slots) for i in range(len(slots)) if slots[i] == slot] + \
                                   [i for i in range(n) if slots[i] == slot]
                            if stage == "early":
                                sp.wait_ge(v_lo_done.sem, v_lo_done.at("early", layer, step, n + 1 - GROUP))
                            elif stage == "dense" and n < GROUP:
                                sp.wait_ge(u_lo_done.sem, u_lo_done.at("dense", layer, step, n - 1))
                            elif stage == "dense":
                                sp.wait_ge(v_lo_done.sem, v_lo_done.at("dense", layer, step, n + 1 - 2 * GROUP))
                            elif steps > 1 or same[-1] >= 0:
                                sp.wait_ge(tile_used.sem, tile_used.at(stage, layer, step, same[-1] + 1))
                            if stage == "select":
                                src = tab_u[layer * KEYS + step * (EARLY // TT) + n]
                            elif stage == "early":
                                src = tab_v[layer * KEYS + step * GROUP + n]
                            elif stage == "dense":
                                tab = tab_u if n < GROUP else tab_v
                                src = tab[layer * KEYS + step * GROUP + (EARLY + n % GROUP)]
                            else:
                                src = stream[layer * STREAM_TILES + step * len(slots) + (count + n)]
                            sp.dma_start(W[:, slot, :], src).then_inc(tile_loaded[slot].sem, 16)
                            if stage not in ("early", "dense"):
                                tenant[slot] = tile_used.base[stage] + (steps - 1) * len(slots) + n
                    if stage not in EXPERT_STAGES:
                        count += steps * len(slots)
                sp.wait_ge(boundary, (layer + 1) * (nstage * 4) + 1)
                sp.sem_inc(held, 1)
            sp.dma_start(out_t, xT[:]).then_inc(out_stored, 16)
            sp.wait_ge(out_stored, 16)

        @block.tensor
        def _(pe):
            mm = nc.tensor.matmul

            def product3(out, w, a, first, last):
                mm(out, w[0], a[0], start=first, stop=False)
                mm(out, w[0], a[1], start=False, stop=False)
                return mm(out, w[1], a[0], start=False, stop=last)

            def load_wait(stage, layer, step, n):
                w, loaded, value = tile(stage, layer, step, n)
                pe.wait_ge(loaded, value)
                return w

            def project(out, w, act, width=128, off=0, pitch=128, kts=KT):
                for k in range(kts):
                    last = mm(out, w[:, k * pitch + off:k * pitch + off + width], act[:, k, :],
                              start=(k == 0), stop=(k == kts - 1))
                return last

            def release(stage, layer, step, m):
                pe.wait_ge(mod_summed.sem, mod_summed.at(stage, layer, step, m + 1))
                pe.sem_inc(tile_used.sem, 1)

            def stream_norm(stage, layer):
                enter(pe, stage, layer)
                for k in range(KT):
                    pe.wait_ge(squares.sem, squares.at(stage, layer, 0, k + 1))
                    mm(NS[:], cst("ones"), sq[:, k % 2, :], start=(k == 0), stop=(k == KT - 1)
                       ).then_inc(square_sums.sem, 1)
                leave(pe)

            def proj_bank(stage, layer, step, n):
                pe.wait_ge(proj_drained.sem, earlier(proj_drained, stage, layer, step, n, 2))
                if stage in ("swa", "mla"):
                    pe.wait_ge(rotation_read.sem, rotation_read.at(stage, layer, step, max(n - 1, 0)))
                return P0[n % 2]

            def norm_sums(stage, layer, step, u):
                tiles_, parts, _, _, _, ones, rot = norms(stage)[u]
                first = sum(len(x[0]) for x in norms(stage)[:u])
                for i, n in enumerate(tiles_):
                    pe.wait_ge(proj_squared.sem, proj_squared.at(stage, layer, step, first + i + 1))
                    if i == 0:
                        pe.wait_ge(sums_read.sem, sums_read.at(stage, layer, step, u))
                    last = mm(NS[0:parts, :], ones[0:parts, 0:parts], sq[0:parts, (first + i) % 2, :],
                              start=(i == 0), stop=(i == len(tiles_) - 1))
                last.then_inc(proj_sums.sem, 1)

            def norm_rotate(stage, layer, step, u):
                tiles_, parts, _, _, _, _, rot = norms(stage)[u]
                pe.wait_ge(proj_drained.sem, proj_drained.at(stage, layer, step, tiles_[0] + 1))
                mm(P0[tiles_[0] % 2][0:parts, :], cst("rot_" + rot)[0:parts, 0:parts], qn[0:parts, u % 2, :],
                   start=True, stop=True).then_inc(rotated.sem, 1)

            def values(stage, layer, step, n, w, act, off, pitch, kts, src=0):
                bank = proj_bank(stage, layer, step, n)
                for t in range(TT):
                    for k in range(kts):
                        last = mm(bank[:, t * 128:(t + 1) * 128], act[:, src + k, t * 128:(t + 1) * 128],
                                  w[:, k * pitch + off:k * pitch + off + 128], start=(k == 0), stop=(k == kts - 1))
                last.then_inc(tile_used.sem, 1)

            def attention(stage, layer, step, beside=()):
                units = [(e, i) for e in range(2) for i in range(TT)]
                mask = {"swa": "mask_window", "mla": "mask_own_chunks", "fox": "mask_frames"}[stage]
                m0 = {"mask_own_chunks": 0, "mask_window": 128, "mask_frames": 384}[mask]

                def scores(u):
                    e, i = units[u]
                    rows, q, k = head(stage, e)
                    tiles_ = key_tiles(stage, i)
                    width = len(tiles_) * 128
                    pe.wait_ge(probs_ready.sem, earlier(probs_ready, stage, layer, step, u, 2))
                    if u == 0:
                        pe.wait_ge(operands_installed.sem, operands_installed.at(stage, layer, step, 1))
                    masked = width if stage == "swa" else 128
                    for lo, hi in ((0, width - masked), (width - masked, width)):
                        if lo == hi:
                            continue
                        out = S0[u % 2][:, lo:hi]
                        plain = hi < width
                        last = mm(out, q[rows, i * 128:(i + 1) * 128],
                                  k[rows, tiles_[0] * 128 + lo:tiles_[0] * 128 + hi],
                                  start=True, stop=plain and stage != "fox")
                        if stage == "fox":
                            bias_rows = slice(64 * e, 64 * e + 40)
                            last = mm(out, fq_head[bias_rows, e, i * 128:(i + 1) * 128], cst("fk")[bias_rows, lo:hi],
                                      start=False, stop=plain)
                    mlo = m0 + (256 - width if stage == "swa" else 0)
                    mm(out, ident16[:], masks16[:, mlo:mlo + masked], start=False, stop=True
                       ).then_inc(scores_ready.sem, 1)

                def turn(u):
                    e, i = units[u]
                    n = len(key_tiles(stage, i))
                    pe.wait_ge(probs_scaled.sem, probs_scaled.at(stage, layer, step, u + 1))
                    pe.wait_ge(turned_copied.sem, earlier(turned_copied, stage, layer, step, u, 2))
                    for b in range(n):
                        last = nc.tensor.transpose(T0[u % 2][:, b * 128:(b + 1) * 128],
                                                   pnorm[:, u % 2, b * 128:(b + 1) * 128], cst("ident"))
                    last.then_inc(probs_turned.sem, 1)

                def output(u):
                    e, i = units[u]
                    pe.wait_ge(turned_copied.sem, turned_copied.at(stage, layer, step, u + 1))
                    if u == 0:
                        pe.wait_ge(pair_stored.sem, pair_stored.at(stage, layer, step, 0))
                        if stage in v_next:
                            pe.wait_ge(values_installed.sem, values_installed.at(stage, layer, step, 1))
                    tiles_ = list(key_tiles(stage, i))
                    for b, kt in enumerate(tiles_):
                        last = mm(O0[64 * e:64 * e + 64, i * 128:(i + 1) * 128], v_cur[:, kt, 64 * e:64 * e + 64],
                                  probsT[:, u % 2, b * 128:(b + 1) * 128], start=(b == 0), stop=(b == len(tiles_) - 1))
                    last.then_inc(unit_out.sem, 1)

                for u in range(len(units) + 3):
                    if u < len(units):
                        scores(u)
                    if 2 <= u <= len(units) + 1:
                        turn(u - 2)
                        if stage == "swa":
                            release(stage, layer, step, u - 2)
                    if u >= 3:
                        output(u - 3)
                    for part in [p for after, p in beside if after == u]:
                        part()
                    if stage == "swa" and u == 0 and not beside:
                        load_wait("swa", layer, step, 0)
                        pe.sem_inc(tile_used.sem, 1)

            def prepare(stage, layer, step, source=None):
                def do(f, *a, **k):
                    return lambda: f(*a, **k)

                def rotate(u):
                    return do(norm_rotate, stage, layer, step, u)

                def sums_of(u):
                    return do(norm_sums, stage, layer, step, u)

                if stage == "swa":
                    def queries():
                        w = load_wait(*source)
                        project(proj_bank("swa", layer, step, 0)[:], w, hT).then_inc(proj_ready.sem, 1)

                    def hand_back():
                        pe.wait_ge(proj_ready.sem, proj_ready.at("swa", layer, step, 1))
                        pe.sem_inc(tile_used.sem, 1)

                    return [(0, queries), (1, hand_back), (1, sums_of(0)), (2, rotate(0))]
                if stage == "mla":
                    w = tile("mla", layer, step, 0)[0]

                    def up(n):
                        e, k = n // 2, n % 2
                        if n == 0:
                            load_wait("mla", layer, step, 0)
                        bank = proj_bank("mla", layer, step, n)
                        if k == 0:
                            project(bank[0:96, :], w, c_lat, width=96, off=96 * e, pitch=192, kts=2
                                    ).then_inc(proj_ready.sem, 1)
                        else:
                            mm(bank[0:64, :], w[:, 384 + 64 * e:448 + 64 * e], c_lat[:, 2, :], start=True, stop=True)
                            mm(bank[64:96, :], cst("ident")[64:96, 64:96], k_rot[64:96, :],
                               start=True, stop=True, skip_group_check=True).then_inc(proj_ready.sem, 1)

                    return [(0, do(up, 0)), (1, do(up, 1)), (2, sums_of(0)), (2, sums_of(1)),
                            (3, rotate(0)), (3, rotate(1)), (4, do(up, 2)), (4, do(up, 3)),
                            (5, sums_of(2)), (5, sums_of(3)), (6, rotate(2)), (6, rotate(3)),
                            (7, do(values, "mla", layer, step, 4, w, c_lat, 512, 0, 1, src=2))]

                def up(n):
                    w = load_wait("fox", layer, step, n)
                    if n < 2:
                        project(proj_bank("fox", layer, step, n)[:], w, hT).then_inc(tile_used.sem, 1)
                    else:
                        values("fox", layer, step, 2, w, hT, 0, 128, KT)

                return [(0, do(up, 0)), (1, sums_of(0)), (2, do(up, 1)), (3, sums_of(1)), (4, do(up, 2))]

            def pairs(stage, layer):
                enter(pe, stage, layer)
                for _, part in prepare(stage, layer, 0, ("swa_kv", layer, 0, 2)):
                    part()
                with pe.Fori(0, PAIRS - 1) as step:
                    attention(stage, layer, step, prepare(stage, layer, step + 1, (stage, layer, step, 0)))
                attention(stage, layer, PAIRS - 1)
                leave(pe)

            pe.wait_ge(consts_loaded, 16)
            pe.wait_ge(setup_done, 2)
            with pe.Fori(0, layers) as layer:
                if "ada" in stages:
                    enter(pe, "ada", layer)
                    with pe.Fori(0, STEPS["ada"]) as step:
                        for m in range(KT):
                            release("ada", layer, step, m)
                    leave(pe)
                if "norm1" in stages:
                    stream_norm("norm1", layer)
                if "swa_kv" in stages:
                    enter(pe, "swa_kv", layer)
                    w = load_wait("swa_kv", layer, 0, 0)
                    project(proj_bank("swa_kv", layer, 0, 0)[:], w, hT).then_inc(tile_used.sem, 1)
                    w = load_wait("swa_kv", layer, 0, 1)
                    values("swa_kv", layer, 0, 1, w, hT, 0, 128, KT)
                    norm_sums("swa_kv", layer, 0, 0)
                    norm_rotate("swa_kv", layer, 0, 0)
                    leave(pe)
                if "swa" in stages:
                    pairs("swa", layer)
                if "mla_c" in stages:
                    enter(pe, "mla_c", layer)
                    for n in range(3):
                        w = load_wait("mla_c", layer, 0, n)
                        if n == 2:
                            norm_sums("mla_c", layer, 0, 0)
                        project(proj_bank("mla_c", layer, 0, n)[:], w, hT).then_inc(tile_used.sem, 1)
                    w = load_wait("mla_c", layer, 0, 3)
                    project(proj_bank("mla_c", layer, 0, 3)[64:96, :], w, hT, width=32, pitch=40).then_inc(proj_ready.sem, 1)
                    project(T0[0][0:8, :], w, hT, width=8, off=32, pitch=40).then_inc(tile_used.sem, 1)
                    norm_sums("mla_c", layer, 0, 1)
                    leave(pe)
                if "mla" in stages:
                    pairs("mla", layer)
                if "fox" in stages:
                    pairs("fox", layer)
                if "gates" in stages:
                    enter(pe, "gates", layer)
                    pe.wait_ge(gate_h_lo_done, (layer + 1) * KT)
                    pe.sem_inc(held, 1)
                    with pe.Fori(0, 4) as step:
                        wb = {}
                        for g in range(6):
                            i = g % 3
                            pe.wait_ge(gate_lo_done.sem, gate_lo_done.at("gates", layer, step, g + 1))
                            pe.wait_ge(branch_gated.sem, earlier(branch_gated, "gates", layer, step, g, 2))
                            for k in range(KT):
                                last = product3(PS[g % 2][:], [w[:, g % 2, k * 128:(k + 1) * 128] for w in gate_w],
                                                [h[:, k, :] for h in gate_h], k == 0, k == KT - 1)
                            last.then_inc(tile_used.sem, 1)
                            if g % 2 == 0:
                                wb[g // 2] = load_wait("gates", layer, step, 3 * (g // 2) + 2)
                            last = project(PS[2 + g % 2][:], wb[g // 2][:, (g % 2) * 512:(g % 2) * 512 + 512], oT[i], kts=4)
                            last.then_inc((branch_ready if g % 2 == 0 else tile_used).sem, 1)
                    leave(pe)
                if "w_out" in stages:
                    enter(pe, "w_out", layer)
                    with pe.Fori(0, 2) as step:
                        for n in range(4):
                            w = load_wait("w_out", layer, step, n)
                            pe.wait_ge(mixed.sem, earlier(mixed, "w_out", layer, step, n, 4))
                            project(PS[n][:], w, mixT).then_inc(tile_used.sem, 1)
                    leave(pe)
                if "norm2" in stages:
                    stream_norm("norm2", layer)
                if "query" in stages:
                    enter(pe, "query", layer)
                    with pe.Fori(0, 4) as step:
                        for e in range(2):
                            w = load_wait("query", layer, step, e)
                            pe.wait_ge(query_copied.sem, earlier(query_copied, "query", layer, step, e, 2))
                            project(PS[e][:], w, hT).then_inc(tile_used.sem, 1)
                        for e in range(2):
                            pe.wait_ge(query_copied.sem, query_copied.at("query", layer, step, e + 1))
                            pe.wait_ge(key_scores_read.sem, earlier(key_scores_read, "query", layer, step, e, 2))
                            for c in range(2):
                                for t in range(TT):
                                    last = mm(PS[2 + 2 * e + c][:, t * 128:(t + 1) * 128],
                                              q_peer[64 * c:64 * c + 64, e, t * 128:(t + 1) * 128],
                                              vec("keys")[64 * c:64 * c + 64, :], start=True, stop=True)
                            last.then_inc(key_scores.sem, 1)
                    leave(pe)
                if "select" in stages:
                    enter(pe, "select", layer)
                    pe.wait_ge(h_lo_done, (layer + 1) * KT)
                    pe.sem_inc(held, 1)
                    with pe.Fori(0, TT) as step:
                        for n in range(EARLY // TT):
                            pe.wait_ge(early_lo_done.sem, early_lo_done.at("select", layer, step, n + 1))
                            if n == 0:
                                pe.wait_ge(early_gelu.sem, early_gelu.at("select", layer, step, 0))
                            for k in range(KT):
                                last = product3(PS[1 + n][:], [u[:, EARLY_BUFFER[n], k * 128:(k + 1) * 128] for u in early_u],
                                                [h[:, k, :] for h in h_parts], k == 0, k == KT - 1)
                            last.then_inc(tile_used.sem, 1)
                        pe.wait_ge(picks_copied.sem, picks_copied.at("select", layer, step, 0))
                        pe.wait_ge(picks_ready.sem, picks_ready.at("select", layer, step, 3))
                        for n in range(3):
                            last = nc.tensor.transpose(PS[0][:, n * 128:(n + 1) * 128], pick[:, n, :], cst("ident"))
                        last.then_inc(picks_turned.sem, 1)
                    leave(pe)
                if "route" in stages:
                    enter(pe, "route", layer)
                    with pe.Fori(0, STEPS["route"]) as step:
                        for q in range(Q):
                            pe.wait_ge(onehots_i.sem, onehots_i.at("route", layer, step, q + 1))
                            pe.wait_ge(onehots_weighted.sem, onehots_weighted.at("route", layer, step, q + 1))
                            pe.wait_ge(route_copied.sem, earlier(route_copied, "route", layer, step, q, 8))
                            for t in range(4):
                                last = mm(PS[q % 8][:, t * 128:(t + 1) * 128], oh_i[:, q % 4, t, :], oh_g[:, q % 4, t, :],
                                          start=True, stop=True)
                            last.then_inc(route_product.sem, 1)
                    leave(pe)
                if "dense" in stages:
                    enter(pe, "dense", layer)

                    def early_outputs(step, first=False, last_step=False):
                        for j in range(GROUP):
                            pe.wait_ge(v_lo_done.sem, v_lo_done.at("early", layer, step, j + 1))
                            pe.wait_ge(a_lo_done.sem, a_lo_done.at("early", layer, step, j + 1))
                            for m in range(KT):
                                last = product3(PS[m][:], [v[:, j, m * 128:(m + 1) * 128] for v in v_parts],
                                                [a[:, j, :] for a in a_parts], first and j == 0,
                                                last_step and j == GROUP - 1)
                            last.then_inc(v_used.sem, 1)

                    def scores(step, ahead=0):
                        for j in range(GROUP):
                            n = ahead * GROUP + j + 1
                            pe.wait_ge(u_lo_done.sem, u_lo_done.at("dense", layer, step, n))
                            if not ahead:
                                pe.wait_ge(early_added, layer * KT + (j + 1))
                            pe.wait_ge(gelu_done.sem, gelu_done.at("dense", layer, step, n - GROUP))
                            for k in range(KT):
                                last = product3(PS[j][:], [u[:, j % 2, k * 128:(k + 1) * 128] for u in u_parts],
                                                [h[:, k, :] for h in h_parts], k == 0, k == KT - 1)
                            last.then_inc(u_used.sem, 1)

                    def outputs(step):
                        for m in range(KT):
                            for j in range(GROUP):
                                if m == 0:
                                    pe.wait_ge(v_lo_done.sem, v_lo_done.at("dense", layer, step, j + 1))
                                    pe.wait_ge(a_lo_done.sem, a_lo_done.at("dense", layer, step, j + 1))
                                if j == 0:
                                    pe.wait_ge(y_added.sem, y_added.at("dense", layer, step, m - 3))
                                last = product3(PS[4 + m % 4][:], [v[:, j, m * 128:(m + 1) * 128] for v in v_parts],
                                                [a[:, j, :] for a in a_parts], j == 0, j == GROUP - 1)
                                if m == KT - 1:
                                    last.then_inc(v_used.sem, 1)
                                elif j == GROUP - 1:
                                    last.then_inc(y_ready.sem, 1)

                    early_outputs(0, first=True)
                    with pe.Fori(1, STEPS["early"] - 1) as step:
                        early_outputs(step)
                    early_outputs(STEPS["early"] - 1, last_step=True)
                    scores(0)
                    pe.wait_ge(early_added, (layer + 1) * KT)
                    pe.sem_inc(held, 1)
                    with pe.Fori(0, STEPS["dense"] - 1) as step:
                        scores(step, ahead=1)
                        outputs(step)
                    outputs(STEPS["dense"] - 1)
                    leave(pe)
                if "final" in stages:
                    enter(pe, "final", layer)
                    leave(pe)

        @block.scalar
        def _(act):
            chain = Chain(act, scalar_chain)
            fn = nc.scalar.activation

            def stream_norm(stage, layer):
                enter(act, stage, layer)
                chain.begin(stage, layer, 0)
                for k in range(KT):
                    if k >= 2:
                        act.wait_ge(square_sums.sem, square_sums.at(stage, layer, 0, k - 1))
                    fn(sq[:, k % 2, :], xT[:, k, :], ACT.Square).then_inc(squares.sem, 1)
                act.wait_ge(square_sums.sem, square_sums.at(stage, layer, 0, KT))
                chain.link(fn(lnv[:, 0, :], NS[:], ACT.Ln, bias=cst("eps"), scale=1.0 / D))
                fn(rstd[:, 0, :], lnv[:, 0, :], ACT.Exp, scale=-0.5).then_inc(stream_rstd.sem, 1)
                b = 0 if stage == "norm1" else 3 * KT
                for k in range(KT):
                    act.wait_ge(stream_scaled.sem, stream_scaled.at(stage, layer, 0, k + 1))
                    fn(hT[:, k, :], hT[:, k, :], ACT.Identity, bias=modT[:, b + k:b + k + 1])
                chain.end()
                leave(act)

            def square(stage, layer, step, n, parts, slot):
                proj_wait(act, stage, layer, step, n)
                fn(sq[0:parts, slot % 2, :], P0[n % 2][0:parts, :], ACT.Square).then_inc(proj_squared.sem, 1)

            def squares_of(stage, layer, step, u):
                tiles_, parts, _, _, _, _, _ = norms(stage)[u]
                first = sum(len(x[0]) for x in norms(stage)[:u])
                for i, n in enumerate(tiles_):
                    square(stage, layer, step, n, parts, first + i)

            def log_mean(stage, layer, step, u):
                tiles_, parts, width, _, _, _, rot = norms(stage)[u]
                act.wait_ge(proj_sums.sem, proj_sums.at(stage, layer, step, u + 1))
                fn(lnv[0:parts, u % 2, :], NS[0:parts, :], ACT.Ln, bias=cst("eps")[0:parts, :], scale=1.0 / width
                   ).then_inc(sums_read.sem, 1)

            def inverse_rms(stage, layer, step, u):
                parts = norms(stage)[u][1]
                act.wait_ge(sums_read.sem, sums_read.at(stage, layer, step, u + 1))
                first_of = norms(stage)[u - 2][0][-1] + 1 if u >= 2 else 0
                act.wait_ge(proj_drained.sem, proj_drained.at(stage, layer, step, first_of))
                fn(rstd[0:parts, u % 2, :], lnv[0:parts, u % 2, :], ACT.Exp, scale=-0.5).then_inc(proj_rstd.sem, 1)

            def prepare(stage):
                def both(after, u):
                    return [(after, part, n) for part in (log_mean, inverse_rms) for n in (u, u + 1)]

                return {"swa": [(0, squares_of, 0), (1, log_mean, 0), (1, inverse_rms, 0)],
                        "mla": [(0, squares_of, 0), (1, squares_of, 1), *both(2, 0),
                                (4, squares_of, 2), (4, squares_of, 3), *both(5, 2)],
                        "fox": [(0, squares_of, 0), (1, log_mean, 0), (1, inverse_rms, 0),
                                (2, squares_of, 1), (3, log_mean, 1), (3, inverse_rms, 1)]}[stage]

            def attention(stage, layer, step, beside=()):
                units = [(e, i) for e in range(2) for i in range(TT)]

                def expo(u):
                    e, i = units[u]
                    width = len(key_tiles(stage, i)) * 128
                    act.wait_ge(max_ready.sem, max_ready.at(stage, layer, step, u + 1))
                    nm = stat[:, u:u + 1]
                    if stage == "swa":
                        fn(stat[:, 16 + u:17 + u], sinks[:, e:e + 1], ACT.Exp, bias=nm)
                    fn(probs[:, u % 2, 0:width], S0[u % 2][:, 0:width], ACT.Exp, bias=nm,
                       accum_out=stat[:, 8 + u:9 + u]).then_inc(probs_ready.sem, 1)

                def copy(u):
                    e, i = units[u]
                    width = len(key_tiles(stage, i)) * 128
                    act.wait_ge(probs_turned.sem, probs_turned.at(stage, layer, step, u + 1))
                    act.wait_ge(unit_out.sem, earlier(unit_out, stage, layer, step, u, 2))
                    fn(probsT[:, u % 2, 0:width], T0[u % 2][:, 0:width], ACT.Copy).then_inc(turned_copied.sem, 1)

                for u in range(len(units) + 2):
                    if u < len(units):
                        expo(u)
                    if u >= 2:
                        copy(u - 2)
                    for _, part, n in [b for b in beside if b[0] == u]:
                        part(stage, layer, step + 1, n)

            def pairs(stage, layer):
                chain.begin(stage, layer, 0)
                for _, part, n in prepare(stage):
                    part(stage, layer, 0, n)
                chain.end()
                with act.Fori(0, PAIRS - 1) as step:
                    chain.begin(stage, layer, step + 1)
                    attention(stage, layer, step, prepare(stage))
                    chain.end()
                attention(stage, layer, PAIRS - 1)

            act.wait_ge(consts_loaded, 16)
            fn(ident16[:], cst("ident"), ACT.Copy).then_inc(setup_done, 1)
            fn(masks16[:], C[:, CONST["mask_own_chunks"][0]:CONST["mask_own_chunks"][0] + 512], ACT.Copy
               ).then_inc(setup_done, 1)
            act.wait_ge(x_loaded, 16)
            with act.Fori(0, layers) as layer:
                if "ada" in stages:
                    enter(act, "ada", layer)
                    act.wait_ge(vecs_loaded, layer * 32 + 32)
                    fn(c_silu, c_rows, ACT.Sigmoid).then_inc(cond_sigmoid, 1)
                    leave(act)
                if "norm1" in stages:
                    stream_norm("norm1", layer)
                for stage in ("swa_kv", "swa", "mla_c", "mla", "fox"):
                    if stage not in stages:
                        continue
                    enter(act, stage, layer)
                    if stage in U8:
                        pairs(stage, layer)
                    else:
                        chain.begin(stage, layer, 0)
                        for u in range(len(norms(stage))):
                            squares_of(stage, layer, 0, u)
                            log_mean(stage, layer, 0, u)
                            inverse_rms(stage, layer, 0, u)
                        if stage == "mla_c":
                            act.wait_ge(vector_chain.sem, vector_chain.at(stage, layer, 0, 2))
                            chain.link(fn(fgt[0:8, 2, :], fgt[0:8, 1, :], ACT.Exp, scale=-1.0))
                            chain.link(fn(fgt[0:8, 2, :], fgt[0:8, 2, :], ACT.Ln, bias=cst("one")[0:8, :]))
                            act.sem_inc(held, 1)
                        chain.end()
                    leave(act)
                if "gates" in stages:
                    enter(act, "gates", layer)
                    for k in range(KT):
                        fn(gate_h[0][:, k, :], hT[:, k, :], ACT.Copy).then_inc(gate_h_hi_done, 1)

                    def lead_gate(step, g):
                        raw, loaded, value = tile("gates", layer, step, GATE_TILES[g])
                        act.wait_ge(loaded, value)
                        former = GATE_TILES[g - 2] - (0 if g >= 2 else len(TILES["gates"][1]))
                        act.wait_ge(tile_used.sem, tile_used.at("gates", layer, step, former + 1))
                        fn(gate_w[0][:, g % 2, :], raw, ACT.Copy).then_inc(gate_hi_done.sem, 1)

                    def gates(step, last=False):
                        act.wait_ge(bias_copied.sem, bias_copied.at("gates", layer, step, 1))
                        for g in range(6):
                            act.wait_ge(tile_used.sem, tile_used.at("gates", layer, step, GATE_TILES[g] + 1))
                            act.wait_ge(branch_gated.sem, earlier(branch_gated, "gates", layer, step, g, 2))
                            fn(sig[:, g % 2, :], PS[g % 2][:], ACT.Sigmoid, bias=gate_b[:, g:g + 1]).then_inc(gate_open.sem, 1)
                            if g + 2 < 6:
                                lead_gate(step, g + 2)
                            elif not last:
                                lead_gate(step + 1, g + 2 - 6)

                    lead_gate(0, 0)
                    lead_gate(0, 1)
                    with act.Fori(0, 3) as step:
                        gates(step)
                    gates(3, last=True)
                    leave(act)
                if "w_out" in stages:
                    enter(act, "w_out", layer)
                    leave(act)
                if "norm2" in stages:
                    stream_norm("norm2", layer)
                if "query" in stages:
                    enter(act, "query", layer)
                    with act.Fori(0, 4) as step:
                        for e in range(2):
                            act.wait_ge(tile_used.sem, tile_used.at("query", layer, step, e + 1))
                            act.wait_ge(key_scores.sem, earlier(key_scores, "query", layer, step, e, 2))
                            fn(q_peer[:, e, :], PS[e][:], ACT.Copy).then_inc(query_copied.sem, 1)
                    leave(act)
                if "select" in stages:
                    enter(act, "select", layer)
                    for k in range(KT):
                        fn(h_parts[0][:, k, :], hT[:, k, :], ACT.Copy).then_inc(h_hi_done, 1)

                    def exponentials(step):
                        act.wait_ge(pick_shifted.sem, pick_shifted.at("select", layer, step, 1))
                        t2 = top.rearrange("p h k -> p (h k)")
                        fn(t2, t2, ACT.Exp).then_inc(pick_exp.sem, 1)

                    def lead_early(step, n):
                        raw, loaded, value = tile("select", layer, step, n)
                        act.wait_ge(loaded, value)
                        former = max(k for k in range(-len(EARLY_BUFFER), n) if EARLY_BUFFER[k] == EARLY_BUFFER[n])
                        act.wait_ge(tile_used.sem, tile_used.at("select", layer, step, former + 1))
                        fn(early_u[0][:, EARLY_BUFFER[n], :], raw, ACT.Copy).then_inc(early_hi_done.sem, 1)

                    def early_columns(step, last=False):
                        for n in range(EARLY // TT):
                            if n in (0, 4):
                                act.wait_ge(early_stored[n // 4].sem, early_stored[n // 4].at("select", layer, step, 0))
                            act.wait_ge(tile_used.sem, tile_used.at("select", layer, step, n + 1))
                            fn(early_act[:, n, :], PS[1 + n][:], ACT.Gelu).then_inc(early_gelu.sem, 1)
                            if n + 2 < EARLY // TT:
                                lead_early(step, n + 2)
                            elif not last:
                                lead_early(step + 1, n + 2 - EARLY // TT)
                            if n == EXP_AFTER:
                                exponentials(step)
                            if n in (3, EARLY // TT - 1):
                                a = n // 4 * 4
                                act.wait_ge(early_gelu.sem, early_gelu.at("select", layer, step, n + 1))
                                act.dma_start(early_dram[:, ds(step * (EARLY // TT * T) + a * T, (n + 1 - a) * T)],
                                              early_act[:, a:n + 1, :].rearrange("p n t -> p (n t)")
                                              ).then_inc(early_stored[n // 4].sem, 16)

                    lead_early(0, 0)
                    lead_early(0, 1)
                    with act.Fori(0, TT - 1) as step:
                        early_columns(step)
                    early_columns(TT - 1, last=True)
                    for b in range(2):
                        act.wait_ge(early_stored[b].sem, early_stored[b].at("select", layer, TT - 1, 16))
                        act.sem_inc(held, 1)
                    leave(act)
                if "route" in stages:
                    enter(act, "route", layer)
                    with act.Fori(0, STEPS["route"]) as step:
                        for q in range(Q):
                            b = q // (Q // 2)
                            act.wait_ge(route_product.sem, route_product.at("route", layer, step, q + 1))
                            if q % (Q // 2) == 0:
                                act.wait_ge(route_free[b].sem, route_free[b].at("route", layer, step, 0))
                            t0 = (q % (Q // 2)) * 4
                            fn(route[b][:, :, t0:t0 + 4], PS[q % 8][:].rearrange("p (t j) -> p j t", t=4), ACT.Copy
                               ).then_inc(route_copied.sem, 1)
                    leave(act)
                if "dense" in stages:
                    enter(act, "dense", layer)

                    def lead_u(step, j, ahead=0):
                        raw, loaded, _ = tile("dense", layer, step, j)
                        act.wait_ge(loaded, tile_loaded[TILES["dense"][1][j]].at(
                            "dense", layer, step, 32 * ahead + 16 * (j // 2 + 1)))
                        act.wait_ge(u_used.sem, u_used.at("dense", layer, step, ahead * GROUP + j - 1))
                        fn(u_parts[0][:, j % 2, :], raw, ACT.Copy).then_inc(u_hi_done.sem, 1)

                    def lead_v(step, j, stage="dense"):
                        raw, loaded, value = tile(stage, layer, step, j + (GROUP if stage == "dense" else 0))
                        act.wait_ge(loaded, value)
                        act.wait_ge(v_used.sem, v_used.at(stage, layer, step, j + 1 - GROUP))
                        fn(v_parts[0][:, j, :], raw, ACT.Copy).then_inc(v_hi_done.sem, 1)

                    def gelu(step, j, ahead=0):
                        n = ahead * GROUP + j + 1
                        act.wait_ge(u_used.sem, u_used.at("dense", layer, step, n))
                        act.wait_ge(a_lo_done.sem, a_lo_done.at("dense", layer, step, n - GROUP))
                        fn(act_out[:, j, :], PS[j][:], ACT.Gelu).then_inc(gelu_done.sem, 1)

                    def lead_next(step, j, ahead=0):
                        if j < GROUP - 2:
                            lead_u(step, j + 2, ahead)
                        else:
                            lead_u(step, j + 2 - GROUP, ahead + 1)

                    def lead_vs(step, j):
                        if j < GROUP - 1:
                            lead_v(step, j)
                        if j == GROUP - 2:
                            lead_v(step, j + 1)

                    with act.Fori(0, STEPS["early"]) as step:
                        for j in range(GROUP):
                            lead_v(step, j, "early")
                    lead_u(0, 0)
                    lead_u(0, 1)
                    for j in range(GROUP):
                        gelu(0, j)
                        lead_next(0, j)
                    with act.Fori(0, STEPS["dense"] - 2) as step:
                        for j in range(GROUP):
                            lead_vs(step, j)
                            gelu(step, j, ahead=1)
                            lead_next(step, j, ahead=1)
                    step = STEPS["dense"] - 2
                    for j in range(GROUP):
                        lead_vs(step, j)
                        gelu(step, j, ahead=1)
                        if j < GROUP - 2:
                            lead_next(step, j, ahead=1)
                    for j in range(GROUP):
                        lead_v(step + 1, j)
                    leave(act)
                if "final" in stages:
                    enter(act, "final", layer)
                    leave(act)

        @block.gpsimd
        def _(pool):
            def load_routes(stage, layer, step, first):
                pool.wait_ge(weighted.sem, weighted.at(stage, layer, step, 0))
                pool.dma_start(g_cur[:], route_dram[:, :, ds(step * (GROUP * TOKENS) + first * TOKENS, GROUP * TOKENS)]
                               ).then_inc(route_loaded.sem, 16)

            for s in signals:
                if s.credit:
                    pool.sem_inc(s.sem, s.credit)
            pool.sem_inc(boundary, 1)
            with pool.Fori(0, layers) as layer:
                for stage in stages:
                    enter(pool, stage, layer)
                    if stage == "route":
                        with pool.Fori(0, STEPS["route"]) as step:
                            for q in range(Q):
                                pool.wait_ge(onehots_j.sem, onehots_j.at("route", layer, step, q + 1))
                                pool.wait_ge(route_product.sem, earlier(route_product, "route", layer, step, q, 4))
                                g4 = pickT[:, 2, ds(step * (2 * TOKENS) + 4 * q, 4)]
                                nc.gpsimd.tensor_tensor(oh_g[:, q % 4], oh_j[:, q % 4],
                                                        g4.unsqueeze(2).broadcast_to([128, 4, 128]), ALU.mult
                                                        ).then_inc(onehots_weighted.sem, 1)
                    if stage == "gates":
                        with pool.Fori(0, 4) as step:
                            for g in range(6):
                                pool.wait_ge(gate_hi_done.sem, gate_hi_done.at("gates", layer, step, g + 1))
                                raw, _, _ = tile("gates", layer, step, GATE_TILES[g])
                                nc.gpsimd.tensor_tensor(gate_w[1][:, g % 2, :], raw, gate_w[0][:, g % 2, :].bitcast(F32),
                                                        ALU.subtract).then_inc(gate_lo_done.sem, 1)
                    if stage == "select":
                        with pool.Fori(0, TT) as step:
                            for n in range(EARLY // TT):
                                pool.wait_ge(early_hi_done.sem, early_hi_done.at("select", layer, step, n + 1))
                                raw, _, _ = tile("select", layer, step, n)
                                b = EARLY_BUFFER[n]
                                nc.gpsimd.tensor_tensor(early_u[1][:, b, :], raw, early_u[0][:, b, :].bitcast(F32),
                                                        ALU.subtract).then_inc(early_lo_done.sem, 1)
                    if stage == "dense":
                        with pool.Fori(0, STEPS["early"]) as step:
                            pool.wait_ge(a_lo_done.sem, a_lo_done.at("early", layer, step, 0))
                            pool.dma_start(act_out.rearrange("p n t -> p (n t)"),
                                           early_dram[:, ds(step * (GROUP * T), GROUP * T)]
                                           ).then_inc(early_loaded.sem, 16)
                            for b in range(2):
                                pool.wait_ge(route_stored[b].sem,
                                             route_stored[b].at("route", layer, STEPS["route"] - 1, 16))
                                pool.sem_inc(held, 1)
                            load_routes("early", layer, step, 0)
                        with pool.Fori(0, STEPS["dense"]) as step:
                            for j in range(GROUP):
                                pool.wait_ge(u_hi_done.sem, u_hi_done.at("dense", layer, step, j + 1))
                                raw, _, _ = tile("dense", layer, step, j)
                                nc.gpsimd.tensor_tensor(u_parts[1][:, j % 2, :], raw, u_parts[0][:, j % 2, :].bitcast(F32),
                                                        ALU.subtract).then_inc(u_lo_done.sem, 1)
                                if j == 1:
                                    load_routes("dense", layer, step, EARLY)
                    leave(pool)

        @block.vector
        def _(dve):
            chain = Chain(dve, vector_chain)
            chain.held = held
            stt, tt, ts = nc.vector.scalar_tensor_tensor, nc.vector.tensor_tensor, nc.vector.tensor_scalar

            def modulation(stage, layer, step, n, m):
                w, loaded, value = tile(stage, layer, step, n)
                dve.wait_ge(loaded, value)
                dve.wait_ge(mod_summed.sem, mod_summed.at(stage, layer, step, m))
                stt(mod_product, w, 1.0, c_silu, ALU.mult, ALU.mult, accum_out=mod_sum[:, m:m + 1]
                    ).then_inc(mod_summed.sem, 1)

            def add_bias(stage, layer, step, first):
                dve.wait_ge(mod_summed.sem, mod_summed.at(stage, layer, step, KT))
                chunk = ds((step + first) * KT, KT)
                chain.link(tt(modT[:, chunk], mod_sum, V[:, chunk], ALU.add))

            def stream_norm(stage, layer):
                enter(dve, stage, layer)
                chain.begin(stage, layer, 0)
                n1 = stage == "norm1"
                g = gain[:, 0:KT] if n1 else gain[:, KT:2 * KT]
                sc = modT[:, KT:2 * KT] if n1 else modT[:, 4 * KT:5 * KT]
                chain.link(stt(g, sc, 1.0, vec("norm1" if n1 else "norm2"), ALU.add, ALU.mult))
                dve.wait_ge(stream_rstd.sem, stream_rstd.at(stage, layer, 0, 1))
                for k in range(KT):
                    stt(hT[:, k, :], xT[:, k, :], g[:, k:k + 1], rstd[:, 0, :], ALU.mult, ALU.mult
                        ).then_inc(stream_scaled.sem, 1)
                chain.end()
                leave(dve)

            def gain_and_rms(stage, layer, step, u):
                tiles_, parts, _, gains, dests, _, rot = norms(stage)[u]
                dve.wait_ge(proj_rstd.sem, proj_rstd.at(stage, layer, step, u + 1))
                for n, g, dst in zip(tiles_, gains, dests):
                    out = qn[0:parts, u % 2, :] if rot else dst[0:parts, :]
                    stt(out, P0[n % 2][0:parts, :], g[0:parts, :], rstd[0:parts, u % 2, :], ALU.mult, ALU.mult
                        ).then_inc(proj_drained.sem, 1)

            def rotation(stage, layer, step, u):
                tiles_, parts, _, _, dests, _, rot = norms(stage)[u]
                n = tiles_[0]
                dve.wait_ge(proj_drained.sem, proj_drained.at(stage, layer, step, n + 1))
                dve.wait_ge(qk_ready.sem, qk_ready.at(stage, layer, step, u))
                chain.mark(tt(rope[0:parts, 0, :], qn[0:parts, u % 2, :], cst("cos_" + rot)[0:parts, :], ALU.mult))
                dve.wait_ge(rotated.sem, rotated.at(stage, layer, step, u + 1))
                tt(rope[0:parts, 1, :], P0[n % 2][0:parts, :], cst("sin_" + rot)[0:parts, :], ALU.mult
                   ).then_inc(rotation_read.sem, 1)
                chain.settle()
                dve.wait_ge(rotation_read.sem, rotation_read.at(stage, layer, step, u + 1))
                tt(dests[0][0:parts, :], rope[0:parts, 0, :], rope[0:parts, 1, :], ALU.add
                   ).then_inc(qk_ready.sem, 1)

            def norm(stage, layer, step, u):
                gain_and_rms(stage, layer, step, u)
                if norms(stage)[u][6]:
                    rotation(stage, layer, step, u)

            def copy_values(stage, layer, step, n):
                proj_wait(dve, stage, layer, step, n)
                dst = v_next[stage] if stage in v_next else v_cur.rearrange("p t c -> p (t c)")
                nc.vector.tensor_copy(dst, P0[n % 2][:]).then_inc(proj_drained.sem, 1)

            def prepare(stage):
                g, r, v = gain_and_rms, rotation, copy_values
                return {"swa": [(2, g, 0), (3, r, 0)],
                        "mla": [(3, g, 0), (3, g, 1), (4, r, 0), (4, r, 1), (6, g, 2), (6, g, 3), (7, r, 2),
                                (7, r, 3), (8, v, 4)],
                        "fox": [(2, g, 0), (4, g, 1), (5, v, 2)]}[stage]

            def install(stage, layer, step):
                if stage == "swa":
                    chain.link(nc.vector.tensor_copy(sinks, V[:, ds(VEC["sink"][0] + step * 2, 2)]))
                if stage == "fox":
                    dve.wait_ge(proj_drained.sem, proj_drained.at(stage, layer, step, 2))
                    for e in range(2):
                        r = slice(64 * e, 64 * e + 40)
                        ts(fq_head[r, e, :], cst("fq")[r, :],
                           C[r, ds(CONST["head_pick"][0] + 2 * step + e, 1)], None, ALU.mult)
                else:
                    dve.wait_ge(qk_ready.sem, qk_ready.at(stage, layer, step, len(norms(stage))))
                rows = slice(0, 96) if stage == "mla" else slice(0, 128)
                n = q_next[stage].shape[1]
                last = nc.vector.tensor_copy(q_cur[rows, 0:n, :], q_next[stage][rows])
                if stage in k_next:
                    last = nc.vector.tensor_copy(k_cur[rows, 0:n, :], k_next[stage][rows])
                last.then_inc(operands_installed.sem, 1)

            def install_values(stage, layer, step):
                dve.wait_ge(proj_drained.sem, proj_drained.at(stage, layer, step, tiles_n[stage]))
                nc.vector.tensor_copy(v_cur.rearrange("p t c -> p (t c)"), v_next[stage]
                                      ).then_inc(values_installed.sem, 1)

            def attention(stage, layer, step, o, beside=()):
                units = [(e, i) for e in range(2) for i in range(TT)]

                def maxi(u):
                    e, i = units[u]
                    width = len(key_tiles(stage, i)) * 128
                    dve.wait_ge(scores_ready.sem, scores_ready.at(stage, layer, step, u + 1))
                    nm = stat[:, u:u + 1]
                    if stage == "swa":
                        chain.link(nc.vector.tensor_reduce(nm, S0[u % 2][:, 0:width], AX.X, ALU.max))
                        ts(nm, nm, sinks[:, e:e + 1], -1.0, ALU.max, ALU.mult).then_inc(max_ready.sem, 1)
                    else:
                        nc.vector.tensor_reduce(nm, S0[u % 2][:, 0:width], AX.X, ALU.max, negate=True
                                                ).then_inc(max_ready.sem, 1)

                def scale(u):
                    e, i = units[u]
                    width = len(key_tiles(stage, i)) * 128
                    dve.wait_ge(probs_ready.sem, probs_ready.at(stage, layer, step, u + 1))
                    total = stat[:, 8 + u:9 + u]
                    if stage == "swa":
                        chain.link(tt(total, total, stat[:, 16 + u:17 + u], ALU.add))
                    chain.link(nc.vector.reciprocal(stat[:, 24 + u:25 + u], total))
                    dve.wait_ge(probs_turned.sem, earlier(probs_turned, stage, layer, step, u, 2))
                    ts(pnorm[:, u % 2, 0:width], probs[:, u % 2, 0:width], stat[:, 24 + u:25 + u], None, ALU.mult
                       ).then_inc(probs_scaled.sem, 1)

                for u in range(len(units) + 1):
                    if u < len(units):
                        maxi(u)
                        for _, part, n in [b for b in beside if b[0] == u]:
                            part(stage, layer, step + 1, n)
                    if u >= 1:
                        scale(u - 1)
                    if stage == "swa" and u < len(units):
                        modulation(stage, layer, step, 1 + u, u)
                if beside:
                    install(stage, layer, step + 1)
                    for _, part, n in [b for b in beside if b[0] == len(units)]:
                        part(stage, layer, step + 1, n)
                if stage == "swa":
                    add_bias(stage, layer, step, 2)
                dve.wait_ge(unit_out.sem, unit_out.at(stage, layer, step, 8))
                nc.vector.tensor_copy(o[:, ds(step, 1), :].rearrange("p a t -> p (a t)"), O0[:]
                                      ).then_inc(pair_stored.sem, 1)
                if beside and stage in v_next:
                    install_values(stage, layer, step + 1)

            def pairs(stage, layer, o):
                links = PREPARE_LINKS[stage]
                chain.begin(stage, layer, 0)
                for _, part, n in prepare(stage):
                    part(stage, layer, 0, n)
                install(stage, layer, 0)
                if stage in v_next:
                    install_values(stage, layer, 0)
                chain.end(without=VECTOR_LINKS[stage] - links)
                with dve.Fori(0, PAIRS - 1) as step:
                    chain.begin(stage, layer, step, start=links)
                    attention(stage, layer, step, o, prepare(stage))
                    chain.end()
                chain.begin(stage, layer, PAIRS - 1, start=links)
                attention(stage, layer, PAIRS - 1, o)
                chain.end(without=links)

            dve.wait_ge(consts_loaded, 16)
            dve.wait_ge(x_loaded, 16)
            with dve.Fori(0, layers) as layer:
                if "ada" in stages:
                    enter(dve, "ada", layer)
                    dve.wait_ge(cond_sigmoid, layer + 1)
                    tt(c_silu, c_rows, c_silu, ALU.mult).then_inc(cond_ready, 1)
                    dve.wait_ge(cond_ready, layer + 1)
                    dve.sem_inc(held, 1)
                    with dve.Fori(0, STEPS["ada"]) as step:
                        chain.begin("ada", layer, step)
                        for m in range(KT):
                            modulation("ada", layer, step, m, m)
                        add_bias("ada", layer, step, 0)
                        chain.end()
                    leave(dve)
                if "norm1" in stages:
                    stream_norm("norm1", layer)
                for stage in ("swa_kv", "swa", "mla_c", "mla", "fox"):
                    if stage not in stages:
                        continue
                    enter(dve, stage, layer)
                    if stage in U8:
                        pairs(stage, layer, oT[{"swa": 0, "mla": 1, "fox": 2}[stage]])
                    else:
                        step = 0
                        chain.begin(stage, layer, step)
                        if stage == "swa_kv":
                            for n, (name, dim) in enumerate((("swa_q", 64), ("mla_q", 96), ("fox_q", 64))):
                                chain.mark(ts(gq[:, n:n + 1], vec(name), float(dim) ** -0.5, None, ALU.mult))
                            norm(stage, layer, step, 0)
                            copy_values(stage, layer, step, 1)
                        if stage == "mla_c":
                            norm(stage, layer, step, 0)
                            proj_wait(dve, stage, layer, step, 4)
                            chain.link(ts(fgt[0:8, 0, :], T0[0][0:8, :], vec("b_forget")[0:8, :], None, ALU.add))
                            chain.mark(stt(fgt[0:8, 1, :], fgt[0:8, 0, :], -1.0, fgt[0:8, 0, :], ALU.mult, ALU.max))
                            norm(stage, layer, step, 1)
                            proj_wait(dve, stage, layer, step, 3)
                            nc.vector.tensor_copy(k_rot[64:96, :], P0[1][64:96, :]).then_inc(proj_drained.sem, 1)
                            dve.wait_ge(scalar_chain.sem, scalar_chain.at(stage, layer, 0, SCALAR_LINKS.get("mla_c", 0)))
                            chain.link(stt(fgt[0:8, 3, :], fgt[0:8, 0, :], 0.0, fgt[0:8, 2, :], ALU.min, ALU.subtract))
                            chain.link(nc.vector.tensor_tensor_scan(cst("fq")[0:8, :], cst("fk")[0:8, :], fgt[0:8, 3, :],
                                                                    0.0, ALU.mult, ALU.add))
                            chain.mark(ts(cst("fk")[32:40, :], cst("fq")[0:8, :], -1.0, None, ALU.mult))
                            chain.mark(nc.vector.tensor_copy(cst("fq")[64:72, :], cst("fq")[0:8, :]))
                            ts(cst("fk")[96:104, :], cst("fq")[0:8, :], -1.0, None, ALU.mult).then_inc(proj_drained.sem, 1)
                        chain.end()
                    leave(dve)
                if "gates" in stages:
                    enter(dve, "gates", layer)
                    for k in range(KT):
                        dve.wait_ge(gate_h_hi_done, layer * KT + (k + 1))
                        tt(gate_h[1][:, k, :], hT[:, k, :], gate_h[0][:, k, :].bitcast(F32), ALU.subtract
                           ).then_inc(gate_h_lo_done, 1)
                    with dve.Fori(0, 4) as step:
                        chain.begin("gates", layer, step)
                        nc.vector.tensor_copy(gate_b[:, 0:6], V[:, ds(VEC["b_gate"][0] + step * 6, 6)]
                                              ).then_inc(bias_copied.sem, 1)
                        for g in range(6):
                            e, i = g // 3, g % 3
                            dve.wait_ge(gate_open.sem, gate_open.at("gates", layer, step, g + 1))
                            if g % 2 == 0:
                                dve.wait_ge(branch_ready.sem, branch_ready.at("gates", layer, step, g // 2 + 1))
                            else:
                                dve.wait_ge(tile_used.sem, tile_used.at("gates", layer, step, 3 * (g // 2) + 3))
                            tt(gated[:, g % 2, :], sig[:, g % 2, :], PS[2 + g % 2][:], ALU.mult).then_inc(branch_gated.sem, 1)
                            dve.wait_ge(branch_gated.sem, branch_gated.at("gates", layer, step, g + 1))
                            y = mixT[:, ds(2 * step + e, 1), :].rearrange("p a t -> p (a t)")
                            if i == 1:
                                chain.link(tt(gated[:, g % 2, :], gated[:, g % 2, :], gated[:, (g - 1) % 2, :], ALU.add))
                            if i == 2:
                                chain.link(tt(y, gated[:, g % 2, :], gated[:, (g - 1) % 2, :], ALU.add))
                        chain.end()
                    leave(dve)
                if "w_out" in stages:
                    enter(dve, "w_out", layer)
                    with dve.Fori(0, 2) as step:
                        for n in range(4):
                            dve.wait_ge(tile_used.sem, tile_used.at("w_out", layer, step, n + 1))
                            xk = xT[:, ds(step * 4 + n, 1), :].rearrange("p a t -> p (a t)")
                            stt(xk, PS[n][:], modT[:, ds(2 * KT + step * 4 + n, 1)], xk, ALU.mult, ALU.add
                                ).then_inc(mixed.sem, 1)
                    leave(dve)
                if "norm2" in stages:
                    stream_norm("norm2", layer)
                if "query" in stages:
                    enter(dve, "query", layer)
                    with dve.Fori(0, 4) as step:
                        chain.begin("query", layer, step)
                        for e in range(2):
                            cells = [(t, c) for t in range(TT) for c in range(2)]

                            def cell(t, c):
                                return PS[2 + 2 * e + c][:, t * 128:(t + 1) * 128], sval_cur[:, e, t, c, :], sidx_cur[:, e, t, c, :]

                            dve.wait_ge(key_scores.sem, key_scores.at("query", layer, step, e + 1))
                            dve.sem_inc(held, 1)
                            for t, c in cells:
                                s, v, _ = cell(t, c)
                                chain.mark(nc.vector.max(v[:, 0:8], s))
                            chain.settle_for_search()
                            for n, (t, c) in enumerate(cells):
                                s, v, x = cell(t, c)
                                chain.mark(nc.vector.match_replace(rest[:, n, :], v[:, 0:8], s, LOWEST))
                                chain.mark(nc.vector.max_index(x[:, 0:8], v[:, 0:8], s))
                            chain.settle_for_search()
                            for n, (t, c) in enumerate(cells):
                                s, v, x = cell(t, c)
                                chain.mark(nc.vector.max(v[:, 8:16], rest[:, n, :]))
                            chain.settle_for_search()
                            for n, (t, c) in enumerate(cells):
                                s, v, x = cell(t, c)
                                chain.mark(nc.vector.max_index(x[:, 8:16], v[:, 8:16], rest[:, n, :]))
                            chain.settle_for_search()
                            sv = sval.rearrange("p t h c k -> p t h (c k)")[:, :, ds(2 * step + e, 1), :]
                            si = sidx.rearrange("p t h c k -> p t h (c k)")[:, :, ds(2 * step + e, 1), :]
                            chain.mark(nc.vector.tensor_copy(sv.rearrange("p t h n -> p t (h n)"),
                                                             sval_cur[:, e].rearrange("p t c k -> p t (c k)")))
                            nc.vector.tensor_copy(si.rearrange("p t h n -> p t (h n)"),
                                                  sidx_cur[:, e].rearrange("p t c k -> p t (c k)")
                                                  ).then_inc(key_scores_read.sem, 1)
                            dve.wait_ge(key_scores_read.sem, key_scores_read.at("query", layer, step, e + 1))
                            chain.settle_for_search()
                        chain.end()
                    leave(dve)
                if "select" in stages:
                    enter(dve, "select", layer)
                    for k in range(KT):
                        dve.wait_ge(h_hi_done, layer * KT + (k + 1))
                        tt(h_parts[1][:, k, :], hT[:, k, :], h_parts[0][:, k, :].bitcast(F32), ALU.subtract
                           ).then_inc(h_lo_done, 1)
                    with dve.Fori(0, TT) as step:
                        chain.begin("select", layer, step)
                        sv = sval[:, ds(step, 1)].rearrange("p a h c k -> p (a h) c k")
                        si = sidx[:, ds(step, 1)].rearrange("p a h c k -> p (a h) c k")
                        chain.link(tt(cand.rearrange("p h (a b) -> p h a b", a=16),
                                      sv[:, :, 0, :].unsqueeze(3).broadcast_to([128, HEADS, 16, 16]),
                                      sv[:, :, 1, :].unsqueeze(2).broadcast_to([128, HEADS, 16, 16]), ALU.add))
                        dve.sem_inc(held, 1)
                        for h in range(HEADS):
                            chain.mark(nc.vector.max(top[:, h, 0:8], cand[:, h, :]))
                        chain.settle_for_search()
                        for h in range(HEADS):
                            chain.mark(nc.vector.max_index(pos[:, h, 0:8], top[:, h, 0:8], cand[:, h, :]))
                        chain.settle_for_search()
                        for h in range(HEADS):
                            chain.mark(nc.vector.match_replace(cand[:, h, :], top[:, h, 0:8], cand[:, h, :], LOWEST))
                        chain.settle_for_search()
                        for h in range(HEADS):
                            chain.mark(nc.vector.max(top[:, h, 8:16], cand[:, h, :]))
                        chain.settle_for_search()
                        for h in range(HEADS):
                            chain.mark(nc.vector.max_index(pos[:, h, 8:16], top[:, h, 8:16], cand[:, h, :]))
                        chain.link(nc.vector.tensor_copy(esum[:, 1, :], top[:, :, 0]))
                        tt(top, top, esum[:, 1, :].unsqueeze(2).broadcast_to([128, HEADS, 16]), ALU.subtract
                           ).then_inc(pick_shifted.sem, 1)
                        p2 = pos.rearrange("p h k -> p (h k)")
                        chain.mark(ts(pos_part[:, 0, :], p2, 4, None, ALU.logical_shift_right))
                        chain.link(ts(pos_part[:, 1, :], p2, 15, None, ALU.bitwise_and))
                        chain.link(nc.vector.tensor_copy(pos_f.rearrange("p a n -> p (a n)"),
                                                         pos_part.rearrange("p a n -> p (a n)")))
                        for half in range(2):
                            chain.link(tt(onehot16, pos_f[:, half, :].unsqueeze(2).broadcast_to([128, 128, 16]),
                                          cst("iota")[:, 0:16].unsqueeze(1).broadcast_to([128, 128, 16]), ALU.is_equal))
                            o4 = onehot16.rearrange("p (h k) c -> p h k c", h=HEADS)
                            chain.link(tt(o4, o4, si[:, :, half, :].unsqueeze(2).broadcast_to([128, HEADS, 16, 16]),
                                          ALU.mult))
                            if half == 0:
                                dve.wait_ge(picks_turned.sem, picks_turned.at("select", layer, step, 0))
                            nc.vector.tensor_reduce(pick[:, half, :], onehot16, AX.X, ALU.add).then_inc(picks_ready.sem, 1)
                            dve.wait_ge(picks_ready.sem, picks_ready.at("select", layer, step, half + 1))
                        dve.wait_ge(pick_exp.sem, pick_exp.at("select", layer, step, 1))
                        chain.link(nc.vector.tensor_reduce(esum[:, 0, :], top, AX.X, ALU.add))
                        chain.link(nc.vector.reciprocal(esum[:, 1, :], esum[:, 0, :]))
                        tt(pick[:, 2, :].rearrange("p (h k) -> p h k", h=HEADS), top,
                           esum[:, 1, :].unsqueeze(2).broadcast_to([128, HEADS, 16]), ALU.mult).then_inc(picks_ready.sem, 1)
                        dve.wait_ge(picks_turned.sem, picks_turned.at("select", layer, step, 1))
                        nc.vector.tensor_copy(pickT[:, :, ds(step * 128, 128)],
                                              PS[0][:, 0:384].rearrange("p (n t) -> p n t", n=3)
                                              ).then_inc(picks_copied.sem, 1)
                        chain.end()
                    leave(dve)
                if "route" in stages:
                    enter(dve, "route", layer)
                    with dve.Fori(0, STEPS["route"]) as step:
                        for q in range(Q):
                            dve.wait_ge(route_product.sem, earlier(route_product, "route", layer, step, q, 4))
                            four = step * (2 * TOKENS) + 4 * q
                            iota4 = cst("iota").unsqueeze(1).broadcast_to([128, 4, 128])
                            tt(oh_i[:, q % 4], pickT[:, 0, ds(four, 4)].unsqueeze(2).broadcast_to([128, 4, 128]), iota4,
                               ALU.is_equal).then_inc(onehots_i.sem, 1)
                            dve.wait_ge(onehots_weighted.sem, onehots_weighted.at("route", layer, step, q - 3))
                            tt(oh_j[:, q % 4], pickT[:, 1, ds(four, 4)].unsqueeze(2).broadcast_to([128, 4, 128]), iota4,
                               ALU.is_equal).then_inc(onehots_j.sem, 1)
                    leave(dve)
                if "dense" in stages:
                    enter(dve, "dense", layer)

                    def weigh(step, j, ahead=0, stage="dense"):
                        n = ahead * GROUP + j + 1
                        if j == 0:
                            dve.wait_ge(route_loaded.sem, route_loaded.at(stage, layer, step, 16 * (ahead + 1)))
                        if stage == "dense":
                            dve.wait_ge(gelu_done.sem, gelu_done.at("dense", layer, step, n))
                        elif j == 0:
                            dve.wait_ge(early_loaded.sem, early_loaded.at("early", layer, step, 16))
                        a3 = act_out[:, j, :].rearrange("p (g t) -> p g t", t=TOKENS)
                        tt(a3, a3, g_cur[:, :, j * TOKENS:(j + 1) * TOKENS], ALU.mult).then_inc(weighted.sem, 1)

                    def split(step, j, stage="dense"):
                        dve.wait_ge(weighted.sem, weighted.at(stage, layer, step, j + 1))
                        dve.wait_ge(v_used.sem, v_used.at(stage, layer, step, j + 1 - GROUP))
                        nc.vector.tensor_copy(a_parts[0][:, j, :], act_out[:, j, :]).then_inc(a_hi_done.sem, 1)
                        dve.wait_ge(a_hi_done.sem, a_hi_done.at(stage, layer, step, j + 1))
                        tt(a_parts[1][:, j, :], act_out[:, j, :], a_parts[0][:, j, :].bitcast(F32),
                           ALU.subtract).then_inc(a_lo_done.sem, 1)
                        dve.wait_ge(v_hi_done.sem, v_hi_done.at(stage, layer, step, j + 1))
                        raw, _, _ = tile(stage, layer, step, j + (GROUP if stage == "dense" else 0))
                        tt(v_parts[1][:, j, :], raw, v_parts[0][:, j, :].bitcast(F32), ALU.subtract
                           ).then_inc(v_lo_done.sem, 1)

                    def add_up(step):
                        for m in range(KT):
                            if m < KT - 1:
                                dve.wait_ge(y_ready.sem, y_ready.at("dense", layer, step, m + 1))
                            else:
                                dve.wait_ge(v_used.sem, v_used.at("dense", layer, step, GROUP))
                            tt(y_sum[:, m, :], y_sum[:, m, :], PS[4 + m % 4][:], ALU.add).then_inc(y_added.sem, 1)

                    with dve.Fori(0, STEPS["early"]) as step:
                        for j in range(GROUP):
                            weigh(step, j, stage="early")
                            split(step, j, "early")
                    dve.wait_ge(v_used.sem, v_used.at("dense", layer, 0, 0))
                    for m in range(KT):
                        nc.vector.tensor_copy(y_sum[:, m, :], PS[m][:]).then_inc(early_added, 1)
                    for j in range(GROUP):
                        weigh(0, j)
                    with dve.Fori(0, STEPS["dense"] - 1) as step:
                        for j in range(GROUP):
                            split(step, j)
                            weigh(step, j, ahead=1)
                        add_up(step)
                    for j in range(GROUP):
                        split(STEPS["dense"] - 1, j)
                    add_up(STEPS["dense"] - 1)
                    leave(dve)
                if "final" in stages:
                    enter(dve, "final", layer)
                    for k in range(KT):
                        stt(xT[:, k, :], y_sum[:, k, :], modT[:, 5 * KT + k:5 * KT + k + 1], xT[:, k, :], ALU.mult, ALU.add)
                    leave(dve)
    assert not MISCOUNTED, MISCOUNTED


def lay_constants():
    c = np.zeros((128, CONST_COLS), np.float32)

    def put(name, a):
        a = np.asarray(a, np.float32)
        c[:a.shape[0], CONST[name][0]:CONST[name][0] + a.shape[1]] = a

    put("ident", np.eye(128))
    b = np.zeros((128, 128))
    b[:64, :64] = b[64:, 64:] = 1
    put("block64", b)
    put("ones", np.ones((128, 128)))

    def rotation(size, starts, half):
        r = np.zeros((size, size))
        for s in starts:
            for i in range(half):
                r[s + half + i, s + i] = -1
                r[s + i, s + half + i] = 1
        return r

    put("rot_a", rotation(128, (0, 64), 32))
    put("rot_b", rotation(128, (64,), 16))
    pos = np.arange(T, dtype=np.float32)
    for name, dim, starts in (("a", 64, (0, 64)), ("b", 32, (64,))):
        inv = np.float32(10000.0) ** (-np.arange(0, dim, 2, dtype=np.float32) / np.float32(dim))
        ang = (pos[:, None] * inv[None, :]).astype(np.float32).astype(np.float64)
        cos, sin = np.ones((128, T)), np.zeros((128, T))
        for s in starts:
            for h in range(2):
                cos[s + h * dim // 2:s + (h + 1) * dim // 2] = np.cos(ang).T
                sin[s + h * dim // 2:s + (h + 1) * dim // 2] = np.sin(ang).T
        put("cos_" + name, cos)
        put("sin_" + name, sin)
    q, k = np.arange(128)[:, None], np.arange(256)[None, :]
    put("mask_own_chunks", np.where(k[:, :128] // 64 <= q // 64, 0, NEG))
    qc = q // 64 + 2
    put("mask_window", np.where((k // 64 <= qc) & (k // 64 >= qc - 1), 0, NEG))
    put("mask_frames", np.where(k[:, :128] <= q, 0, NEG))
    put("iota", np.tile(np.arange(128), (128, 1)))
    e = np.zeros((104, 8))
    for r in (0, 32, 64, 96):
        e[r:r + 8] = np.eye(8)
    put("head_pick", e)
    put("eps", np.full((128, 1), EPS))
    put("one", np.ones((128, 1)))
    f = np.zeros((104, T))
    f[32:40] = f[96:104] = 1
    put("fq", f)
    put("fk", f[::-1])
    return c


def tiles_of(w):
    k, n = w.shape[0] // 128, w.shape[1] // 128
    return w.reshape(k, 128, n, 128).transpose(2, 1, 0, 3).reshape(n, 128, k * 128)


def lay_stream(w_ada, w_in, q_up, kv_up, w_branch, w_out, w_q):
    out = []

    def pad(a):
        t = np.zeros((128, 1024), np.float32)
        t[:, :a.shape[1]] = a
        return t

    mod = w_ada.T.reshape(6 * KT, 128, D)
    out += list(mod[:2 * KT])
    cuts = np.cumsum([0, 512, 128, 128, 256, 128, 32, 512, 512, 512, 8, 3 * D])
    aq, ak, av, cq, ckv, kr, fq, fk, fv, ff, gate = [w_in[:, a:b] for a, b in zip(cuts[:-1], cuts[1:])]
    pairs = [tiles_of(np.concatenate([aq[:, m * 64:m * 64 + 64], aq[:, (m + 4) * 64:(m + 5) * 64]], 1))[0]
             for m in range(PAIRS)]
    out += [tiles_of(ak)[0], tiles_of(av)[0], pairs[0]]
    for m in range(PAIRS):
        out.append(pairs[m + 1] if m + 1 < PAIRS else np.zeros((128, D), np.float32))
        out += list(mod[(2 + m) * KT:(3 + m) * KT])
    out += list(tiles_of(cq)) + list(tiles_of(ckv))
    misc = np.concatenate([kr, ff], 1)
    out.append(pad(misc.reshape(KT, 128, 40).transpose(1, 0, 2).reshape(128, KT * 40)))
    kv = kv_up.reshape(128, HEADS, 128)
    for m in range(PAIRS):
        q = q_up[:, m * 192:(m + 1) * 192].reshape(2, 128, 192).transpose(1, 0, 2).reshape(128, 384)
        out.append(pad(np.concatenate([q, kv[:, 2 * m, :64], kv[:, 2 * m + 1, :64],
                                       kv[:, 2 * m, 64:], kv[:, 2 * m + 1, 64:]], 1)))
    fq, fk, fv = tiles_of(fq), tiles_of(fk), tiles_of(fv)
    for m in range(PAIRS):
        out += [fq[m], fk[m], fv[m]]
    gates = tiles_of(gate)
    order = np.concatenate([np.r_[m * 64:m * 64 + 64, (m + 4) * 64:(m + 5) * 64] for m in range(PAIRS)])
    br = [tiles_of(w_branch[0][order]), tiles_of(w_branch[1]), tiles_of(w_branch[2])]
    for m in range(0, KT, 2):
        for a in range(3):
            pairs = [((2 * a + b) // 3 + m, (2 * a + b) % 3) for b in range(2)]
            out += [gates[i * KT + mm] for mm, i in pairs]
            out.append(np.concatenate([br[i][mm] for mm, i in pairs], 1))
    out += list(tiles_of(w_out)) + list(tiles_of(w_q))
    return out


def lay_vectors(b_ada, n1, n2, b_gate, b_forget, sink, aq, ak, cq, ckv, bq, bk, fq, fk, keys):
    v = np.zeros((128, VEC_COLS), np.float32)

    def put(name, a):
        v[:a.shape[0], VEC[name][0]:VEC[name][0] + a.shape[1]] = a

    put("b_ada", b_ada.reshape(48, 128).T)
    put("norm1", n1.reshape(KT, 128).T)
    put("norm2", n2.reshape(KT, 128).T)
    put("b_gate", b_gate.reshape(3, KT, 128).transpose(2, 1, 0).reshape(128, 24))
    put("sink", np.tile(sink.reshape(2, 4).T.reshape(1, 8), (128, 1)))
    put("swa_q", np.tile(aq, 2)[:, None])
    put("swa_k", np.tile(ak, 2)[:, None])
    put("cq", cq.reshape(2, 128).T)
    put("ckv", ckv[:, None])
    put("mla_q", bq[:, None])
    put("mla_k", bk[:, None])
    put("fox_q", np.tile(fq, 2)[:, None])
    put("fox_k", np.tile(fk, 2)[:, None])
    put("b_forget", b_forget[:, None])
    put("keys", keys.transpose(0, 2, 1).reshape(128, 128))
    return v


def kernel(**inputs):
    import concourse.bacc as bacc
    from concourse.bass_utils import run_bass_kernel_spmd as run

    arrays = lay_inputs(inputs)
    nc = bacc.Bacc("TRN2", target_bir_lowering=False, num_devices=1)
    build(nc, arrays)
    r = run(nc, [arrays], core_ids=[0])
    y = r.results[0]["out_t"]
    return np.ascontiguousarray(y.transpose(2, 1, 0)).reshape(1, T, D)


def lay_inputs(inputs):
    a = {k: np.asarray(v) for k, v in inputs.items()}
    L = LAYERS
    stream = np.stack([t for l in range(L) for t in lay_stream(
        a["w_ada"][l], a["w_in"][l], a["mla_w_q_up"][l], a["mla_w_kv_up"][l], a["w_branch"][l],
        a["w_out"][l], a["peer_w_q"][l])])
    vecs = np.stack([lay_vectors(a["b_ada"][l], a["norm1_g"][l], a["norm2_g"][l], a["b_gate"][l],
                                 a["b_forget"][l], a["swa_sink"][l], a["swa_qnorm"][l], a["swa_knorm"][l],
                                 a["mla_q_norm"][l], a["mla_kv_norm"][l], a["mla_qnorm"][l], a["mla_knorm"][l],
                                 a["fox_qnorm"][l], a["fox_knorm"][l], a["peer_sub_keys"][l]) for l in range(L)])
    u = a["peer_u"].reshape(L, KEYS, KEYS, KT, 128).transpose(0, 2, 4, 3, 1)
    v = a["peer_v"].reshape(L, KEYS, KEYS, D).transpose(0, 2, 1, 3)
    return {
        "x_t": np.ascontiguousarray(a["x"][0].reshape(T, KT, 128).transpose(2, 1, 0)),
        "stream": np.ascontiguousarray(stream),
        "vecs": vecs,
        "c_rows": np.ascontiguousarray(np.broadcast_to(a["c"][0], (128, D))),
        "consts": lay_constants(),
        "tab_u": np.ascontiguousarray(u).reshape(L * KEYS, 128, D),
        "tab_v": np.ascontiguousarray(v).reshape(L * KEYS, 128, D),
    }


def build(nc, arrays, **options):
    args = {n: nc.dram_tensor(n, a.shape, mybir.dt.from_np(a.dtype), kind="ExternalInput").ap()
            for n, a in arrays.items()}
    out_t = nc.dram_tensor("out_t", (128, KT, T), F32, kind="ExternalOutput").ap()
    route = nc.dram_tensor("route_scratch", (128, T // TOKENS, 128 * TOKENS), F32, kind="Internal").ap()
    early = nc.dram_tensor("early_scratch", (128, EARLY * T), F32, kind="Internal").ap()
    build_trunk(nc, args["x_t"], args["stream"], args["vecs"], args["consts"], args["c_rows"], args["tab_u"], args["tab_v"],
                out_t, route, early, **options)
```
